# Optimizing a Trainium2 kernel written in Bass

```python
import math
import jax, jax.numpy as jnp
from jax import lax
import numpy as np

D_MODEL = 1024
BATCH = 1
SEQ = 256
DEPTH = 1

CHUNK = 64
N_ATTN_HEADS = 8
HEAD_DIM = 64
ATTN_WIDTH = N_ATTN_HEADS * HEAD_DIM
CONV_GROUPS = 8
CONV_WIDTH_CH = 512
CONV_K = 3
Q_BLOCK = 128
FFN_HIDDEN = int(math.ceil(8 * D_MODEL / 3 / 256) * 256)
RMS_EPS = 1e-6

_COLS = [ATTN_WIDTH, ATTN_WIDTH, ATTN_WIDTH, N_ATTN_HEADS,
         CONV_WIDTH_CH, CONV_WIDTH_CH, CONV_WIDTH_CH,
         D_MODEL, D_MODEL]
IN_COLS = sum(_COLS)
_SPLITS = list(np.cumsum(_COLS)[:-1])


def rmsnorm(x, g):
    xf = x.astype(jnp.float32)
    y = xf * lax.rsqrt(jnp.mean(xf * xf, axis=-1, keepdims=True) + RMS_EPS)
    return (y * g.astype(jnp.float32)).astype(x.dtype)

def causal_depthwise_conv(z, w):
    c = z.shape[-1]
    return lax.conv_general_dilated(
        z, w[:, None, :].astype(z.dtype), window_strides=(1,),
        padding=[(CONV_K - 1, 0)], dimension_numbers=("NWC", "WIO", "NWC"),
        feature_group_count=c)

def forgetting_attention(q, k, v, logf):
    s_len = q.shape[1]
    scale = 1.0 / math.sqrt(q.shape[-1])
    c = jnp.cumsum(logf, axis=1).transpose(0, 2, 1)
    outs = []
    for s0 in range(0, s_len, Q_BLOCK):
        s1 = s0 + Q_BLOCK
        logits = jnp.einsum("bqhd,bkhd->bhqk", q[:, s0:s1], k[:, :s1],
                            preferred_element_type=jnp.float32) * scale
        logits = logits + c[:, :, s0:s1, None] - c[:, :, None, :s1]
        qpos = jnp.arange(s0, s1)[:, None]
        kpos = jnp.arange(s1)[None, :]
        logits = jnp.where(kpos <= qpos, logits, -jnp.inf)
        p = jax.nn.softmax(logits, axis=-1)
        outs.append(jnp.einsum("bhqk,bkhd->bqhd", p.astype(v.dtype), v[:, :s1]))
    return jnp.concatenate(outs, axis=1)

def mixer(h, w_in, b_f, conv_w, w_branch, w_out):
    bsz, s_len, _ = h.shape
    proj = jnp.einsum("bsd,dn->bsn", h, w_in)
    q, k, v, f_logit, g_b, g_c, hc, gate_conv, gate_attn = jnp.split(proj, _SPLITS, axis=-1)
    ya = g_b * causal_depthwise_conv(g_c * hc, conv_w)
    shp = (bsz, s_len, N_ATTN_HEADS, HEAD_DIM)
    logf = jax.nn.log_sigmoid(f_logit.astype(jnp.float32) + b_f.astype(jnp.float32))
    yb = forgetting_attention(q.reshape(shp), k.reshape(shp), v.reshape(shp), logf)
    yb = yb.reshape(bsz, s_len, ATTN_WIDTH)
    ya_d = jnp.einsum("bsc,cd->bsd", ya, w_branch[0])
    yb_d = jnp.einsum("bsc,cd->bsd", yb, w_branch[1])
    merged = jax.nn.sigmoid(gate_conv) * ya_d + jax.nn.sigmoid(gate_attn) * yb_d
    return jnp.einsum("bsd,de->bse", merged, w_out)

def swiglu(h, w_gate_up, w_down):
    gu = jnp.einsum("bsd,df->bsf", h, w_gate_up)
    g, u = jnp.split(gu, 2, axis=-1)
    return jnp.einsum("bsf,fd->bsd", jax.nn.silu(g) * u, w_down)

def first_inputs(seed: int = 0) -> dict:
    key = jax.random.key(seed)
    ks = jax.random.split(key, 12)
    f32 = jnp.float32

    def nrm(k, shape, fan_in):
        return jax.random.normal(k, shape, f32) * (fan_in ** -0.5)

    def gain(k):
        return 1.0 + 0.05 * jax.random.normal(k, (DEPTH, D_MODEL), f32)

    return {
        "x": jax.random.normal(ks[0], (BATCH, SEQ, D_MODEL), f32),
        "norm_mix_pre": gain(ks[1]),
        "norm_mix_post": gain(ks[2]),
        "w_in": nrm(ks[3], (DEPTH, D_MODEL, IN_COLS), D_MODEL),
        "b_f": 2.0 + 0.5 * jax.random.normal(ks[4], (DEPTH, N_ATTN_HEADS), f32),
        "conv_w": nrm(ks[5], (DEPTH, CONV_K, CONV_WIDTH_CH), CONV_K),
        "w_branch": nrm(ks[6], (DEPTH, 2, ATTN_WIDTH, D_MODEL), ATTN_WIDTH),
        "w_out": nrm(ks[7], (DEPTH, D_MODEL, D_MODEL), D_MODEL),
        "norm_ffn_pre": gain(ks[8]),
        "norm_ffn_post": gain(ks[9]),
        "w_gate_up": nrm(ks[10], (DEPTH, D_MODEL, 2 * FFN_HIDDEN), D_MODEL),
        "w_down": nrm(ks[11], (DEPTH, FFN_HIDDEN, D_MODEL), FFN_HIDDEN),
    }

def first_block(x, norm_mix_pre, norm_mix_post, w_in, b_f, conv_w, w_branch, w_out,
              norm_ffn_pre, norm_ffn_post, w_gate_up, w_down):
    for l in range(DEPTH):
        h = rmsnorm(x, norm_mix_pre[l])
        m = mixer(h, w_in[l], b_f[l], conv_w[l], w_branch[l], w_out[l])
        x = x + rmsnorm(m, norm_mix_post[l])
        h = rmsnorm(x, norm_ffn_pre[l])
        f = swiglu(h, w_gate_up[l], w_down[l])
        x = x + rmsnorm(f, norm_ffn_post[l])
    return x


MEM_LEN = 256
RET_HEADS = 4
RET_HEAD_DIM = 128
RET_WIDTH = RET_HEADS * RET_HEAD_DIM
DIFF_HEADS = 4
DIFF_HALF_DIM = 64
DIFF_V_DIM = 2 * DIFF_HALF_DIM
DIFF_WIDTH = DIFF_HEADS * DIFF_V_DIM
MIX_WIDTH = RET_WIDTH + DIFF_WIDTH
IN_COLS_2 = 4 * RET_WIDTH + 3 * DIFF_WIDTH
MEM_HEADS = 4
MEM_HEAD_DIM = D_MODEL // MEM_HEADS
D_FF = 2816
CHUNK_2 = 128
EPS = 1e-6
NEG_BIG = -1e30


def rms_norm(x, g):
    xf = x.astype(jnp.float32)
    y = xf * lax.rsqrt(jnp.mean(xf * xf, axis=-1, keepdims=True) + EPS)
    return (y * g.astype(jnp.float32)).astype(x.dtype)

def group_norm(x, g):
    xf = x.astype(jnp.float32)
    mu = jnp.mean(xf, axis=-1, keepdims=True)
    xc = xf - mu
    y = xc * lax.rsqrt(jnp.mean(xc * xc, axis=-1, keepdims=True) + EPS)
    return (y * g.astype(jnp.float32)).astype(x.dtype)

def swiglu_2(h, w1, w3, w2):
    return (jax.nn.silu(h @ w1) * (h @ w3)) @ w2

def retention(q, k, v):
    b, s, h, d = q.shape
    nc = s // CHUNK_2
    log_gamma = jnp.log1p(-jnp.exp2(-5.0 - jnp.arange(h, dtype=jnp.float32)))
    idx = jnp.arange(CHUNK_2, dtype=jnp.float32)
    rel = idx[:, None] - idx[None, :]
    intra_decay = jnp.where(rel[None] >= 0,
                            jnp.exp(log_gamma[:, None, None] * jnp.maximum(rel, 0.0)[None]), 0.0)
    q = q.astype(jnp.float32).reshape(b, nc, CHUNK_2, h, d)
    k = k.astype(jnp.float32).reshape(b, nc, CHUNK_2, h, d) * (d ** -0.5)
    v = v.astype(jnp.float32).reshape(b, nc, CHUNK_2, h, d)
    scores = jnp.einsum('bnihd,bnjhd->bnhij', q, k) * intra_decay
    o_intra = jnp.einsum('bnhij,bnjhe->bnihe', scores, v)
    k_decay = jnp.exp(log_gamma[None, :] * (CHUNK_2 - 1.0 - idx)[:, None])
    kv = jnp.einsum('bnjhd,jh,bnjhe->bnhde', k, k_decay, v)
    chunk_decay = jnp.exp(log_gamma * CHUNK_2)[None, :, None, None]

    def step(state, kv_c):
        return chunk_decay * state + kv_c, state

    init = jnp.zeros((b, h, d, d), jnp.float32)
    _, states = lax.scan(step, init, jnp.moveaxis(kv, 1, 0))
    states = jnp.moveaxis(states, 0, 1)
    q_decay = jnp.exp(log_gamma[None, :] * (idx + 1.0)[:, None])
    o_cross = jnp.einsum('bnihd,ih,bnhde->bnihe', q, q_decay, states)
    return (o_intra + o_cross).reshape(b, s, h, d)

def diff_attention(q, k, v, lam):
    b, s, h, _, dh = q.shape
    dv = v.shape[-1]
    nb = s // Q_BLOCK
    slopes = jnp.exp2(-8.0 * jnp.arange(1, h + 1, dtype=jnp.float32) / h)
    scale = dh ** -0.5
    kpos = jnp.arange(s)
    qb = jnp.moveaxis(q.reshape(b, nb, Q_BLOCK, h, 2, dh), 1, 0)

    def block(args):
        q_blk, blk = args
        qpos = blk * Q_BLOCK + jnp.arange(Q_BLOCK)
        dist = (qpos[:, None] - kpos[None, :]).astype(jnp.float32)
        sc = jnp.einsum('bqhmd,bkhmd->bhmqk', q_blk, k).astype(jnp.float32) * scale
        sc = sc - slopes[None, :, None, None, None] * dist
        sc = jnp.where(dist >= 0, sc, NEG_BIG)
        p = jax.nn.softmax(sc, axis=-1)
        a = p[:, :, 0] - lam * p[:, :, 1]
        return jnp.einsum('bhqk,bkhe->bqhe', a.astype(v.dtype), v)

    out = lax.map(block, (qb, jnp.arange(nb)))
    return jnp.moveaxis(out, 0, 1).reshape(b, s, h, dv)

def hybrid_mixer(h, w_in, ret_norm, diff_q_norm, diff_k_norm,
                 lambda_q1, lambda_k1, lambda_q2, lambda_k2, diff_norm, w_out, lam_init):
    b, s, _ = h.shape
    proj = h @ w_in
    cuts = [RET_WIDTH, 2 * RET_WIDTH, 3 * RET_WIDTH, 4 * RET_WIDTH,
            4 * RET_WIDTH + DIFF_WIDTH, 4 * RET_WIDTH + 2 * DIFF_WIDTH]
    rq, rk, rv, rg, dq, dk, dvv = jnp.split(proj, cuts, axis=-1)
    shp_r = (b, s, RET_HEADS, RET_HEAD_DIM)
    ro = retention(rq.reshape(shp_r), rk.reshape(shp_r), rv.reshape(shp_r))
    ro = group_norm(ro, ret_norm).reshape(b, s, RET_WIDTH).astype(h.dtype)
    ro = jax.nn.silu(rg) * ro
    shp_d = (b, s, DIFF_HEADS, 2, DIFF_HALF_DIM)
    dq = rms_norm(dq.reshape(shp_d), diff_q_norm)
    dk = rms_norm(dk.reshape(shp_d), diff_k_norm)
    dvv = dvv.reshape(b, s, DIFF_HEADS, DIFF_V_DIM)
    lam = (jnp.exp(jnp.sum(lambda_q1.astype(jnp.float32) * lambda_k1.astype(jnp.float32)))
           - jnp.exp(jnp.sum(lambda_q2.astype(jnp.float32) * lambda_k2.astype(jnp.float32)))
           + lam_init)
    do = diff_attention(dq, dk, dvv, lam)
    do = (rms_norm(do, diff_norm) * (1.0 - lam_init)).reshape(b, s, DIFF_WIDTH).astype(h.dtype)
    return jnp.concatenate([ro, do], axis=-1) @ w_out

def memory_attention(h, mem_n, w_q, w_kv, w_o, q_norm, k_norm):
    b, s, _ = h.shape
    m = mem_n.shape[1]
    q = rms_norm((h @ w_q).reshape(b, s, MEM_HEADS, MEM_HEAD_DIM), q_norm)
    kv = (mem_n @ w_kv).reshape(b, m, 2, MEM_HEADS, MEM_HEAD_DIM)
    k = rms_norm(kv[:, :, 0], k_norm)
    v = kv[:, :, 1]
    sc = jnp.einsum('bqhd,bkhd->bhqk', q, k).astype(jnp.float32) * (MEM_HEAD_DIM ** -0.5)
    p = jax.nn.softmax(sc, axis=-1).astype(v.dtype)
    o = jnp.einsum('bhqk,bkhd->bqhd', p, v).reshape(b, s, D_MODEL)
    return o @ w_o

def second_inputs(seed: int = 0) -> dict:
    key = jax.random.key(seed)
    ks = iter(jax.random.split(key, 40))

    def dense(fan_in, fan_out):
        return jax.random.normal(next(ks), (DEPTH, fan_in, fan_out), jnp.float32) * fan_in ** -0.5

    def gain(n):
        return 1.0 + 0.02 * jax.random.normal(next(ks), (DEPTH, n), jnp.float32)

    def small(n):
        return 0.1 * jax.random.normal(next(ks), (DEPTH, n), jnp.float32)

    return {
        "x": jax.random.normal(next(ks), (BATCH, SEQ, D_MODEL), jnp.float32),
        "mem": jax.random.normal(next(ks), (BATCH, MEM_LEN, D_MODEL), jnp.float32),
        "norm_ffn1": gain(D_MODEL),
        "ffn1_w1": dense(D_MODEL, D_FF),
        "ffn1_w3": dense(D_MODEL, D_FF),
        "ffn1_w2": dense(D_FF, D_MODEL),
        "norm_mix": gain(D_MODEL),
        "w_in": dense(D_MODEL, IN_COLS_2),
        "ret_norm": gain(RET_HEAD_DIM),
        "diff_q_norm": gain(DIFF_HALF_DIM),
        "diff_k_norm": gain(DIFF_HALF_DIM),
        "lambda_q1": small(DIFF_HALF_DIM),
        "lambda_k1": small(DIFF_HALF_DIM),
        "lambda_q2": small(DIFF_HALF_DIM),
        "lambda_k2": small(DIFF_HALF_DIM),
        "diff_norm": gain(DIFF_V_DIM),
        "w_out": dense(MIX_WIDTH, D_MODEL),
        "norm_mem_q": gain(D_MODEL),
        "norm_mem_kv": gain(D_MODEL),
        "mem_w_q": dense(D_MODEL, D_MODEL),
        "mem_w_kv": dense(D_MODEL, 2 * D_MODEL),
        "mem_q_norm": gain(MEM_HEAD_DIM),
        "mem_k_norm": gain(MEM_HEAD_DIM),
        "mem_w_o": dense(D_MODEL, D_MODEL),
        "norm_ffn2": gain(D_MODEL),
        "ffn2_w1": dense(D_MODEL, D_FF),
        "ffn2_w3": dense(D_MODEL, D_FF),
        "ffn2_w2": dense(D_FF, D_MODEL),
        "norm_out": gain(D_MODEL),
    }

def second_block(x, mem, norm_ffn1, ffn1_w1, ffn1_w3, ffn1_w2, norm_mix, w_in, ret_norm,
              diff_q_norm, diff_k_norm, lambda_q1, lambda_k1, lambda_q2, lambda_k2, diff_norm,
              w_out, norm_mem_q, norm_mem_kv, mem_w_q, mem_w_kv, mem_q_norm, mem_k_norm, mem_w_o,
              norm_ffn2, ffn2_w1, ffn2_w3, ffn2_w2, norm_out):
    for l in range(DEPTH):
        lam_init = 0.8 - 0.6 * math.exp(-0.3 * l)
        x = x + 0.5 * swiglu_2(rms_norm(x, norm_ffn1[l]), ffn1_w1[l], ffn1_w3[l], ffn1_w2[l])
        x = x + hybrid_mixer(rms_norm(x, norm_mix[l]), w_in[l], ret_norm[l], diff_q_norm[l],
                             diff_k_norm[l], lambda_q1[l], lambda_k1[l], lambda_q2[l],
                             lambda_k2[l], diff_norm[l], w_out[l], lam_init)
        x = x + memory_attention(rms_norm(x, norm_mem_q[l]), rms_norm(mem, norm_mem_kv[l]),
                                 mem_w_q[l], mem_w_kv[l], mem_w_o[l], mem_q_norm[l], mem_k_norm[l])
        x = x + 0.5 * swiglu_2(rms_norm(x, norm_ffn2[l]), ffn2_w1[l], ffn2_w3[l], ffn2_w2[l])
        x = rms_norm(x, norm_out[l])
    return x


def setup_inputs(seed=0):
    out = dict(first_inputs(seed))
    for name, value in second_inputs(seed + 1).items():
        if name != "x":
            out[name + "_2"] = value
    return out


def reference(
    x, norm_mix_pre, norm_mix_post, w_in, b_f, conv_w, w_branch, w_out, norm_ffn_pre,
    norm_ffn_post, w_gate_up, w_down, mem_2, norm_ffn1_2, ffn1_w1_2, ffn1_w3_2, ffn1_w2_2,
    norm_mix_2, w_in_2, ret_norm_2, diff_q_norm_2, diff_k_norm_2, lambda_q1_2, lambda_k1_2,
    lambda_q2_2, lambda_k2_2, diff_norm_2, w_out_2, norm_mem_q_2, norm_mem_kv_2, mem_w_q_2,
    mem_w_kv_2, mem_q_norm_2, mem_k_norm_2, mem_w_o_2, norm_ffn2_2, ffn2_w1_2, ffn2_w3_2,
    ffn2_w2_2, norm_out_2,
):
    x = first_block(
        x, norm_mix_pre, norm_mix_post, w_in, b_f, conv_w, w_branch, w_out, norm_ffn_pre,
        norm_ffn_post, w_gate_up, w_down,
    )
    return second_block(
        x, mem_2, norm_ffn1_2, ffn1_w1_2, ffn1_w3_2, ffn1_w2_2, norm_mix_2, w_in_2, ret_norm_2,
        diff_q_norm_2, diff_k_norm_2, lambda_q1_2, lambda_k1_2, lambda_q2_2, lambda_k2_2,
        diff_norm_2, w_out_2, norm_mem_q_2, norm_mem_kv_2, mem_w_q_2, mem_w_kv_2, mem_q_norm_2,
        mem_k_norm_2, mem_w_o_2, norm_ffn2_2, ffn2_w1_2, ffn2_w3_2, ffn2_w2_2, norm_out_2,
    )


_drawn_inputs = setup_inputs


def setup_inputs(seed=0):
    import zlib

    import numpy as np

    out = dict(_drawn_inputs(seed))
    spreads = {}
    factors = {'norm_ffn1_2': 8.0,
     'norm_mix_2': 4.164,
     'ret_norm_2': 8.0,
     'diff_q_norm_2': 8.0,
     'diff_k_norm_2': 8.0,
     'diff_norm_2': 64.0,
     'norm_mem_q_2': 8.0,
     'norm_mem_kv_2': 8.0,
     'mem_q_norm_2': 8.0,
     'mem_k_norm_2': 8.0,
     'norm_ffn2_2': 26.08,
     'norm_out_2': 8.384}
    for name, (base, spread) in spreads.items():
        noise = np.random.default_rng([zlib.crc32(name.encode()), seed]).standard_normal(out[name].shape)
        drawn = base * np.exp(spread * noise) if base else spread * noise
        out[name] = __import__('jax').numpy.asarray(drawn.astype(out[name].dtype))
    for name, factor in factors.items():
        out[name] = (out[name] * factor).astype(out[name].dtype)
    return out
```

```python
from contextlib import ExitStack

import concourse.bass as bass
from concourse import mybir

F32 = mybir.dt.float32
F32R = mybir.dt.float32r
ALU = mybir.AluOpType
ACT = mybir.ActivationFunctionType
AX = mybir.AxisListType.X

P = 128
T = 256
D = 1024
KD = D // P
HID = 2816
PAIRS = HID // (2 * P)
CH = 2048
RING = 3
EPS = 1e-6
LAM_INIT = 0.2

Q, K, V, GB, GC, HC, GATE_C, GATE_A = 0, 2, 4, 6, 8, 10, 12, 16
BR0, BR1, OUT1, MEMK = 20, 22, 24, 28
FFN = [32, 69, 128]
MEMV = 65
DQ, DK, RV, RQ, RK, DV, RG = 102, 104, 106, 108, 110, 112, 114
OUT2, MEMQ, OUTM = 116, 120, 124
CHUNKS = 161
FFN_CHUNKS = 3 * PAIRS


def upnum(c):
    n = c if c < BR0 else c - 4
    for b in FFN:
        if c >= b + FFN_CHUNKS:
            n -= PAIRS
    return n


UP_FFN = [28, 54, 102]
assert all(upnum(b) == u for b, u in zip(FFN, UP_FFN))

A_TOKX, A_F, A_LOGF, A_CUM = 0, 1, 2, 3
A_KMEM = [4, 5, 7, 8]
A_TOKM = 6
A_DIFF = [9, 11, 12, 13]
A_TOK2 = 10
A_MEAN = [14, 15]
A_VAR = [16, 17]
A_DOUT = [18, 19]
A_QMEM = [20, 21, 22, 23]
H_KMEM, H_DIFF, H_VAR, H_DOUT, H_QMEM = 0, 4, 8, 10, 12

G_MIX_PRE, G_MIX_POST, G_FFN_PRE, G_FFN_POST = 0, 8, 16, 24
G_FFN1, G_MIX2, G_MEMQ, G_MEMKV, G_FFN2, G_OUT = 32, 40, 48, 56, 64, 72
CONV, RETN, DIFN, MQN, MKN, DQN, DKN, LAMQ, LAMK, BF = 80, 92, 93, 94, 96, 98, 99, 100, 101, 102
C_ID, C_ONE, C_BD, C_TRI, C_CAUSAL, C_END = 0, 128, 256, 384, 640, 896


def build(nc, a, out):
    with ExitStack() as ctx:
        def sb(name, shape, dt=F32):
            return ctx.enter_context(nc.sbuf_tensor(name, shape, dt))

        def sem(name):
            return ctx.enter_context(nc.semaphore(name))

        stage = sb("stage", [P, RING, CH])
        w_hi = sb("w_hi", [P, RING, CH], F32R)
        w_lo = sb("w_lo", [P, RING, CH], F32R)
        x_T = sb("x_T", [P, KD, T])
        act_hi = sb("act_hi", [P, KD, T], F32R)
        act_lo = sb("act_lo", [P, KD, T], F32R)
        mix_hi = sb("mix_hi", [P, KD, T], F32R)
        mix_lo = sb("mix_lo", [P, KD, T], F32R)
        ffn_hi = sb("ffn_hi", [P, 2, T], F32R)
        ffn_lo = sb("ffn_lo", [P, 2, T], F32R)
        k_mem = sb("k_mem", [P, KD, T])
        v_mem = sb("v_mem", [P, 2, D])
        rs = sb("rs", [P, T])
        rs_post = sb("rs_post", [P, T])
        rs_mem = sb("rs_mem", [P, T])
        std = sb("std", [P, T])
        tok = sb("tok", [P, 2])
        tok_mem = sb("tok_mem", [P, 2])
        sq_acc = sb("sq_acc", [P, 2, T])
        sq_tmp = sb("sq_tmp", [P, 2, T])
        h_sq = sb("h_sq", [P, 2, T])
        h_std = sb("h_std", [P, 2, T])
        q_pad = sb("q_pad", [P, 2, 4, T])
        k_T = sb("k_T", [P, 4, T])
        v_tok = sb("v_tok", [P, 2, 512])
        L0 = sb("L0", [P, 8, P])
        L1 = sb("L1", [P, 8, T])
        gate = sb("gate", [P, 16, T])
        const = sb("const", [P, C_END])
        table = sb("table", [P, 8, T])
        par_rows = sb("par_rows", [P, P])
        par = sb("par", [P, P])
        first_rows = sb("first_rows", [KD, P])
        first_gain = sb("first_gain", [P, KD])
        wf = sb("wf", [P, KD, 8])
        forget = sb("forget", [P, 4, T])
        fz, fe, logf, negc = (forget[:, i, :] for i in range(4))
        logf_tok = sb("logf_tok", [P, 2, 8])
        c_tok = sb("c_tok", [P, 2, 8])
        small = sb("small", [P, 64])
        eps_t = sb("eps_t", [P, 1])

        natural = gate[:, 0:8, :].rearrange("p a b -> p (a b)").rearrange("p (t d) -> p t d", t=2)
        mem_nat = L1[:, :, :].rearrange("p a b -> p (a b)").rearrange("p (t d) -> p t d", t=2)
        mem_T = q_pad[:, :, :, :].rearrange("p a b t -> p (a b) t")
        p_T0 = mem_T
        p_T1 = k_T[:, :, :].rearrange("p a b -> p (a b)").rearrange("p (m q) -> p m q", m=8)
        wf_hi = mix_hi[:, 0:4, :].rearrange("p a b -> p (a b)").rearrange("p (k n) -> p k n", k=KD)
        wf_lo = mix_lo[:, 0:4, :].rearrange("p a b -> p (a b)").rearrange("p (k n) -> p k n", k=KD)
        v_flat = v_mem[:, :, :].rearrange("p a b -> p (a b)")
        gb_T = v_flat[:, 0:1024].rearrange("p (a t) -> p a t", a=4)
        hc_T = v_flat[:, 1024:2048].rearrange("p (j a t) -> p j a t", j=2, a=2)
        k_flat = k_mem[:, :, :].rearrange("p a b -> p (a b)")
        z_T = k_flat[:, 0:4 * (T + 2)].rearrange("p (a t) -> p a t", a=4)
        y_T = k_flat[:, 1040:1040 + 2 * T].rearrange("p (a t) -> p a t", a=2)
        gate_c, gate_a = gate[:, 0:8, :], gate[:, 8:16, :]
        m_T = gate[:, 8:16, :]
        g_s, silu, u_s, h_T = (gate[:, 2 * i:2 * i + 2, :] for i in range(4))
        sel = table[:, 0:4, :].rearrange("p a b -> p (a b)").rearrange("p (h m) -> p h m", h=8)
        alibi, decay = table[:, 0:4, :], table[:, 4:8, :]
        raw = gate[:, 0:8, :]
        rq_T, rk_T = gate[:, 8:12, :], gate[:, 12:16, :]
        rv_tok = [forget[:, 2 * t:2 * t + 2, :].rearrange("p a b -> p (a b)") for t in range(2)]
        a_T0 = gate[:, 0:4, :]
        a_T1 = gate[:, 4:6, :].rearrange("p a b -> p (a b)").rearrange("p (h q) -> p h q", h=4)
        rg_s, ret_o = L1[:, 0:4, :], L1[:, 4:8, :]
        diff_o = gate[:, 8:12, :]
        p_mem = L1
        p_memT = L0[:, :, :].rearrange("p a b -> p (a b)").rearrange("p (h k q) -> p h k q", h=2, k=2)
        ident = const[:, C_ID:C_ID + P]
        ones = const[:, C_ONE:C_ONE + P]
        halves = const[:, C_BD:C_BD + P]
        tri = const[:, C_TRI:C_TRI + T]
        causal = const[:, C_CAUSAL:C_CAUSAL + T]
        eps = eps_t[:, :]
        raw_k = L1
        tok_std = small[:, 56:58]
        nmax, psum_, prec = small[:, 8:24], small[:, 24:40], small[:, 40:56]
        lam, lam_e, lam_p = small[:, 1:2], small[:, 2:4], small[:, 4:6]

        bank = [ctx.enter_context(nc.psum_tensor(f"bank{i}", [P, 512], F32)) for i in range(8)]
        pair = [b[:, :].rearrange("p (a t) -> p a t", a=2) for b in bank]
        quad = [b[:, :].rearrange("p (a t) -> p a t", a=4) for b in bank]
        UP, SUM, AUX, ACC = 0, 2, 3, 4
        back = [bank[i] for i in (0, 1, 3, 4)]

        x_landed, const_landed, par_landed = sem("x_landed"), sem("const_landed"), sem("par_landed")
        ident_landed = sem("ident_landed")
        gain_landed, gain_turned, gain_done = sem("gain_landed"), sem("gain_turned"), sem("gain_done")
        wf_landed, mem_landed, table_landed = sem("wf_landed"), sem("mem_landed"), sem("table_landed")
        landed = [sem(f"landed{i}") for i in range(RING)]
        hi_done, lo_done, used, up_free = sem("hi_done"), sem("lo_done"), sem("used"), sem("up_free")
        zeroed, par_turned, par_ready = sem("zeroed"), sem("par_turned"), sem("par_ready")
        x_turned, x_done = sem("x_turned"), sem("x_done")
        act_hi_done, act_lo_done = sem("act_hi_done"), sem("act_lo_done")
        sq_done, sum_done, std_done, rs_done = sem("sq_done"), sem("sum_done"), sem("std_done"), sem("rs_done")
        aux_done, aux_free = sem("aux_done"), sem("aux_free")
        hsq_done, hn_done = sem("hsq_done"), sem("hn_done")
        wf_hi_done, wf_lo_done = sem("wf_hi_done"), sem("wf_lo_done")
        fz_done, fexp_done, fln_done = sem("fz_done"), sem("fexp_done"), sem("fln_done")
        logf_done = sem("logf_done")
        lg_done, lg_free, max_done, exp_done = sem("lg_done"), sem("lg_free"), sem("max_done"), sem("exp_done")
        p_done, tp_done, tp_free, pv_done = sem("p_done"), sem("tp_done"), sem("tp_free"), sem("pv_done")
        mixhi_done, mixlo_done = sem("mixhi_done"), sem("mixlo_done")
        hc_done, z_done, y_done = sem("hc_done"), sem("z_done"), sem("y_done")
        gates_done, br_free, merged = sem("gates_done"), sem("br_free"), sem("merged")
        memt_turned, memt_done = sem("memt_turned"), sem("memt_done")
        mem_hi_done, mem_lo_done = sem("mem_hi_done"), sem("mem_lo_done")
        m_done, down_done = sem("m_done"), sem("down_done")
        silu_done, h_done = sem("silu_done"), sem("h_done")
        ffn_hi_done, ffn_lo_done = sem("ffn_hi_done"), sem("ffn_lo_done")
        lam_done, lamx_done = sem("lam_done"), sem("lamx_done")
        sc_done, at_done, ro_done, rg_done = sem("sc_done"), sem("at_done"), sem("ro_done"), sem("rg_done")
        xc_done, ro_sum = sem("xc_done"), sem("ro_sum")
        diff_done = sem("diff_done")
        dve_step, pool_step, act_step = sem("dve_step"), sem("pool_step"), sem("act_step")
        res_done, res_turned, nat_done, stored = sem("res_done"), sem("res_turned"), [sem(f"nat_done{i}") for i in range(2)], sem("stored")

        block = ctx.enter_context(nc.Block())
        w_in, w_in2 = a["w_in"][0], a["w_in_2"][0]

        def parameters(engine):
            engine.wait_ge(zeroed, 1)

            def rows(r, n, src, cols=P, at=0):
                engine.dma_start(par_rows[r:r + n, at:at + cols], src).then_inc(par_landed, 16)

            for r, name in ((G_MIX_PRE, "norm_mix_pre"), (G_MIX_POST, "norm_mix_post"), (G_FFN_PRE, "norm_ffn_pre"),
                            (G_FFN_POST, "norm_ffn_post"), (G_FFN1, "norm_ffn1_2"), (G_MIX2, "norm_mix_2"),
                            (G_MEMQ, "norm_mem_q_2"), (G_MEMKV, "norm_mem_kv_2"), (G_FFN2, "norm_ffn2_2"),
                            (G_OUT, "norm_out_2")):
                rows(r, KD, a[name][0].rearrange("(k p) -> k p", p=P))
            rows(CONV, 12, a["conv_w"][0].rearrange("j (b p) -> (j b) p", p=P))
            rows(RETN, 1, a["ret_norm_2"])
            rows(DIFN, 1, a["diff_norm_2"])
            rows(MQN, 2, a["mem_q_norm_2"][0].rearrange("(k p) -> k p", p=P))
            rows(MKN, 2, a["mem_k_norm_2"][0].rearrange("(k p) -> k p", p=P))
            for r, name in ((DQN, "diff_q_norm_2"), (DKN, "diff_k_norm_2")):
                rows(r, 1, a[name], 64, 0)
                rows(r, 1, a[name], 64, 64)
            for r, at, name in ((LAMQ, 0, "lambda_q1_2"), (LAMQ, 64, "lambda_q2_2"),
                                (LAMK, 0, "lambda_k1_2"), (LAMK, 64, "lambda_k2_2")):
                rows(r, 1, a[name], 64, at)
            rows(BF, 1, a["b_f"], 8, 0)

        def store(engine, t, j):
            cols = slice(512 * j, 512 * j + 512)
            engine.dma_start(out[0, P * t:P * t + P, cols], natural[:, t, cols]).then_inc(stored, 16)

        @block.sync
        def _(sp):
            def slot(c):
                return c % RING

            def free(c):
                if isinstance(c, int) and c < RING:
                    return
                sp.wait_ge(lo_done, c - RING + 1)

            def whole(c, w, col, place):
                free(c)
                sp.dma_start(stage[:, place, :].rearrange("p (k n) -> p k n", k=KD),
                             w.rearrange("(k p) n -> p k n", p=P)[:, :, bass.ds(col, 2 * P)]
                             ).then_inc(landed[place], 16)

            def rows(c, w, r, n, col, width, place):
                free(c)
                sp.dma_start(stage[:, place, :].rearrange("p (k n) -> p k n", k=n),
                             w[bass.ds(r, n * P), col:col + width].rearrange("(k p) n -> p k n", p=P)
                             ).then_inc(landed[place], 16)

            def wholes(c, w, col, n):
                for i in range(n):
                    whole(c + i, w, col + 256 * i, slot(c + i))

            def feed_forward(base, w_g, g_col, w_u, u_col, w_d):
                whole(base, w_g, g_col, slot(base))
                whole(base + 1, w_u, u_col, slot(base + 1))
                with sp.Fori(0, PAIRS - 2) as t:
                    c = base + 2 + t * 3
                    whole(c, w_g, t * 256 + (g_col + 256), slot(base + 2))
                    rows(c + 1, w_d, t * 256, 2, 0, D, slot(base + 3))
                    whole(c + 2, w_u, t * 256 + (u_col + 256), slot(base + 4))
                last = base + FFN_CHUNKS - 1
                whole(last - 3, w_g, (PAIRS - 1) * 256 + g_col, slot(last - 3))
                whole(last - 2, w_u, (PAIRS - 1) * 256 + u_col, slot(last - 2))
                for i in range(2):
                    rows(last - 1 + i, w_d, (PAIRS - 2 + i) * 256, 2, 0, D, slot(last - 1 + i))

            for t in range(2):
                sp.dma_start(natural[:, t, :], a["x"][0, t * P:t * P + P, :]).then_inc(x_landed, 16)
            wholes(Q, w_in, 0, 3)
            parameters(sp)
            wholes(K + 1, w_in, 256 * 3, 3)
            wholes(GB, w_in, 1544, 14)
            for i in range(4):
                rows(BR0 + i, a["w_branch"][0, i // 2], 0, 4, 512 * (i % 2), 512, slot(BR0 + i))
            wholes(OUT1, a["w_out"][0], 0, 4)
            wholes(MEMK, a["mem_w_kv_2"][0], 0, 4)
            feed_forward(FFN[0], a["w_gate_up"][0], 0, a["w_gate_up"][0], HID, a["w_down"][0])
            wholes(MEMV, a["mem_w_kv_2"][0], D, 4)
            feed_forward(FFN[1], a["ffn1_w1_2"][0], 0, a["ffn1_w3_2"][0], 0, a["ffn1_w2_2"][0])
            for c, col in ((DQ, 2048), (DK, 2560), (RV, 1024), (RQ, 0), (RK, 512), (DV, 3072), (RG, 1536)):
                wholes(c, w_in2, col, 2)
            wholes(OUT2, a["w_out_2"][0], 0, 4)
            wholes(MEMQ, a["mem_w_q_2"][0], 0, 4)
            wholes(OUTM, a["mem_w_o_2"][0], 0, 4)
            feed_forward(FFN[2], a["ffn2_w1_2"][0], 0, a["ffn2_w3_2"][0], 0, a["ffn2_w2_2"][0])
            for j in range(2):
                sp.wait_ge(nat_done[0], j + 1)
                store(sp, 0, j)
            sp.wait_ge(stored, 64)

        @block.tensor
        def _(pe):
            def three(dst, w, lo_w, x, lo_x, first, last, group=True):
                pe.matmul(dst, w, x, start=first, stop=False, skip_group_check=not group)
                pe.matmul(dst, w, lo_x, start=False, stop=False, skip_group_check=not group)
                return pe.matmul(dst, lo_w, x, start=False, stop=last, skip_group_check=not group)

            def up_bank(c, u):
                pe.wait_ge(lo_done, c + 1)
                if not isinstance(u, int) or u >= 2:
                    pe.wait_ge(up_free, u - 1)

            def up(c, hi, lo, ready=None, base=0, u=None, place=None, bank_no=None):
                u = upnum(c) if u is None else u
                place = c % RING if place is None else place
                dst = pair[UP + (u % 2 if bank_no is None else bank_no)]
                up_bank(c, u)
                wh = w_hi[:, place, :].rearrange("p (k n) -> p k n", k=KD)
                wl = w_lo[:, place, :].rearrange("p (k n) -> p k n", k=KD)
                if ready is None:
                    for m in range(2):
                        for k in range(KD):
                            mm = three(dst[:, m, :], wh[:, k, m * P:m * P + P], wl[:, k, m * P:m * P + P],
                                       hi[:, k, :], lo[:, k, :], k == 0, k == KD - 1)
                else:
                    for k in range(KD):
                        pe.wait_ge(ready, base + k + 1)
                        for m in range(2):
                            mm = three(dst[:, m, :], wh[:, k, m * P:m * P + P], wl[:, k, m * P:m * P + P],
                                       hi[:, k, :], lo[:, k, :], k == 0 and m == 0, k == KD - 1, group=False)
                mm.then_inc(used, 1)

            def up_tok(c, hi, lo):
                u, place = upnum(c), c % RING
                up_bank(c, u)
                wh = w_hi[:, place, :].rearrange("p (k n) -> p k n", k=KD)
                wl = w_lo[:, place, :].rearrange("p (k n) -> p k n", k=KD)
                for t in range(2):
                    for k in range(KD):
                        xs = slice(t * P, t * P + P)
                        mm = three(pair[UP + u % 2][:, t, :], hi[:, k, xs], lo[:, k, xs],
                                   wh[:, k, :], wl[:, k, :], k == 0, k == KD - 1)
                mm.then_inc(used, 1)

            def sums(n):
                pe.wait_ge(sq_done, n + 1)
                if n:
                    pe.wait_ge(std_done, n)
                pe.matmul(bank[SUM][:, 0:T], ones, sq_acc[:, 0, :], start=True, stop=False)
                pe.matmul(bank[SUM][:, 0:T], ones, sq_acc[:, 1, :], start=False, stop=True).then_inc(sum_done, 1)

            def aux(n):
                if n:
                    pe.wait_ge(aux_free, n)

            def turn_rs(n, which, norm):
                pe.wait_ge(rs_done, norm + 1)
                aux(n)
                pe.transpose(bank[AUX][:, 0:P], which[:, 0:P], ident)
                pe.transpose(bank[AUX][:, P:2 * P], which[:, P:T], ident).then_inc(aux_done, 1)

            def head_norm(n, j, mat, both):
                pe.wait_ge(hsq_done, j + 1)
                aux(n)
                if both:
                    pe.matmul(bank[AUX][:, 0:T], mat, h_sq[:, 0, :], start=True, stop=False)
                    mm = pe.matmul(bank[AUX][:, 0:T], mat, h_sq[:, 1, :], start=False, stop=True)
                else:
                    mm = pe.matmul(bank[AUX][:, :], mat, h_sq[:, :, :], start=True, stop=True)
                mm.then_inc(aux_done, 1)

            def logits(g, first, bias):
                qt, b = g // 4, g % 4
                nk = P * (qt + 1)
                if qt:
                    pe.wait_ge(lg_free, first + g - 3)
                for par_ in range(2):
                    dst = pair[ACC + b][:, par_, 0:nk]
                    mm = pe.matmul(dst, q_pad[:, par_, b, qt * P:qt * P + P], k_T[:, b, 0:nk],
                                   start=True, stop=not bias)
                    if bias:
                        mm = pe.matmul(dst, sel[:, 2 * b + par_, :], negc[:, 0:nk], start=False, stop=True)
                mm.then_inc(lg_done, 1)

            def ffn_chunk(c, base, f, i, first, place):
                pe.wait_ge(lo_done, c + 1)
                pe.wait_ge(ffn_lo_done, i + (f * PAIRS + 1))
                wh = w_hi[:, place, :].rearrange("p (k n) -> p k n", k=2)
                wl = w_lo[:, place, :].rearrange("p (k n) -> p k n", k=2)
                last = first == "last"
                hid_hi, hid_lo = (act_hi, act_lo) if last else (ffn_hi, ffn_lo)
                for m in range(KD):
                    for k in range(2):
                        ms = slice(m * P, m * P + P)
                        mm = three(pair[ACC + m // 2][:, m % 2, :], wh[:, k, ms], wl[:, k, ms], hid_hi[:, k, :],
                                   hid_lo[:, k, :], first == "first" and k == 0 and m % 2 == 0, last and k == 1,
                                   group=False)
                    if last and m % 2 and m < KD - 1:
                        mm.then_inc(down_done, 1)
                mm.then_inc(used, 1)

            def feed_forward(f, prep, norm, extra=None):
                base, u0 = FFN[f], UP_FFN[f]
                up(base, act_hi, act_lo, act_lo_done, 8 * prep)
                if extra is not None:
                    extra()
                sums(norm)
                up(base + 1, act_hi, act_lo)
                s = [(base + 2 + j) % RING for j in range(3)]

                def body(t, first):
                    c = base + 2 + t * 3
                    up(c, act_hi, act_lo, u=u0 + 2 + t * 2, place=s[0], bank_no=0)
                    ffn_chunk(c + 1, base, f, t, first, s[1])
                    up(c + 2, act_hi, act_lo, u=u0 + 3 + t * 2, place=s[2], bank_no=1)

                body(0, "first")
                with pe.Fori(1, PAIRS - 2) as t:
                    body(t, "")
                t = PAIRS - 2
                c = base + 2 + t * 3
                up(c, act_hi, act_lo, u=u0 + 2 + t * 2, bank_no=0)
                up(c + 1, act_hi, act_lo, u=u0 + 3 + t * 2, bank_no=1)
                ffn_chunk(c + 2, base, f, t, "", (c + 2) % RING)
                ffn_chunk(base + FFN_CHUNKS - 1, base, f, PAIRS - 1, "last", (base + FFN_CHUNKS - 1) % RING)

            pe.wait_ge(ident_landed, 16)
            pe.wait_ge(gain_landed, 16)
            pe.transpose(bank[SUM][:, 0:KD], first_rows[:, :], ident[0:KD, 0:KD]).then_inc(gain_turned, 1)
            pe.wait_ge(x_landed, 32)
            for b in range(4):
                for m in range(2):
                    for t in range(2):
                        d0 = (2 * b + m) * P
                        mm = pe.transpose(pair[ACC + b][:, m, t * P:t * P + P], natural[:, t, d0:d0 + P], ident)
                mm.then_inc(x_turned, 1)

            for _ in range(9):
                pe.matmul(bank[AUX][:, 0:P], ident, ident, start=True, stop=True)
            up(Q, act_hi, act_lo, act_lo_done, 0)
            pe.wait_ge(const_landed, 16)
            pe.wait_ge(gain_done, 1)
            sums(0)
            up(Q + 1, act_hi, act_lo)
            pe.wait_ge(par_landed, 16 * 24)
            pe.wait_ge(std_done, 1)
            pe.transpose(bank[SUM][:, 0:P], par_rows[:, :], ident).then_inc(par_turned, 1)
            up(K, act_hi, act_lo)
            turn_rs(A_TOKX, rs, 0)
            pe.wait_ge(par_ready, 2)
            pe.matmul(bank[SUM][:, 0:2], ones, lam_p, start=True, stop=True).then_inc(lam_done, 1)
            up(K + 1, act_hi, act_lo)
            pe.wait_ge(wf_lo_done, 1)
            aux(A_F)
            for k in range(KD):
                mm = three(bank[AUX][:, 0:T], wf_hi[:, k, :], wf_lo[:, k, :], act_hi[:, k, :], act_lo[:, k, :],
                           k == 0, k == KD - 1)
            mm.then_inc(aux_done, 1)
            up_tok(V, act_hi, act_lo)
            up_tok(V + 1, act_hi, act_lo)
            up(GB, act_hi, act_lo)
            up(GB + 1, act_hi, act_lo)
            pe.wait_ge(logf_done, 1)
            aux(A_LOGF)
            for t in range(2):
                mm = pe.transpose(bank[AUX][:, t * P:t * P + P], logf[:, t * P:t * P + P], ident)
            mm.then_inc(aux_done, 1)
            up(GC, act_hi, act_lo)
            aux(A_CUM)
            pe.matmul(bank[AUX][:, 0:8], tri[:, 0:P], logf_tok[:, 0, :], start=True, stop=True)
            pe.matmul(bank[AUX][:, 8:16], tri[:, P:T], logf_tok[:, 0, :], start=True, stop=False)
            pe.matmul(bank[AUX][:, 8:16], tri[:, 0:P], logf_tok[:, 1, :], start=False, stop=True)
            pe.matmul(bank[AUX][0:8, T:2 * T], logf_tok[:, 0, :], tri, start=True, stop=False)
            pe.matmul(bank[AUX][0:8, T + P:2 * T], logf_tok[:, 1, :], tri[:, 0:P],
                      start=False, stop=True).then_inc(aux_done, 1)
            up(GC + 1, act_hi, act_lo)
            up(HC, act_hi, act_lo)
            pe.wait_ge(aux_free, A_CUM + 1)
            pe.wait_ge(x_done, 4)
            pe.wait_ge(table_landed, 16)
            for g in range(4):
                logits(g, 0, True)
            up(HC + 1, act_hi, act_lo)
            for g in range(4, 8):
                logits(g, 0, True)
            up(GATE_C, act_hi, act_lo)
            up(GATE_C + 1, act_hi, act_lo)
            up(GATE_C + 2, act_hi, act_lo)

            def turn_probs(e, tile, src, maps, e0):
                pe.wait_ge(p_done, tile + 1)
                if e >= 4 + e0:
                    pe.wait_ge(tp_free, e - 3)
                for i in range(4):
                    mm = pe.transpose(quad[ACC + (e - e0) % 4][:, i, :], src(maps + i), ident)
                mm.then_inc(tp_done, 1)

            pe.wait_ge(lg_free, 8)
            for e in range(2):
                turn_probs(e, 0, lambda m: L0[:, m, :], 4 * e, 0)
            up(GATE_C + 3, act_hi, act_lo)
            for e in range(2, 6):
                k0 = P * ((e - 2) // 2)
                turn_probs(e, 1, lambda m: L1[:, m, k0:k0 + P], 4 * (e % 2), 0)
            up(GATE_A, act_hi, act_lo)
            up(GATE_A + 1, act_hi, act_lo)
            pe.wait_ge(tp_free, 6)
            for b in range(4):
                for par_ in range(2):
                    m = 2 * b + par_
                    pe.matmul(pair[ACC + b][:, par_, :], v_tok[:, 0, b * P:b * P + P], p_T0[:, m, :],
                              start=True, stop=False)
                    mm = pe.matmul(pair[ACC + b][:, par_, P:T], v_tok[:, 1, b * P:b * P + P], p_T1[:, m, :],
                                   start=False, stop=True)
                mm.then_inc(pv_done, 1)
            up(GATE_A + 2, act_hi, act_lo)
            up(GATE_A + 3, act_hi, act_lo)
            for j in range(4):
                c = BR0 + j
                pe.wait_ge(lo_done, c + 1)
                pe.wait_ge(mixlo_done, 6 if j == 0 else 8)
                if j >= 2:
                    pe.wait_ge(br_free, j - 1)
                wh = w_hi[:, c % RING, :].rearrange("p (k n) -> p k n", k=4)
                wl = w_lo[:, c % RING, :].rearrange("p (k n) -> p k n", k=4)
                for m in range(4):
                    for k in range(4):
                        ms, kk = slice(m * P, m * P + P), 4 * (j // 2) + k
                        mm = three(pair[ACC + 2 * (j % 2) + m // 2][:, m % 2, :], wh[:, k, ms], wl[:, k, ms],
                                   mix_hi[:, kk, :], mix_lo[:, kk, :], k == 0, k == 3)
                mm.then_inc(used, 1)
            up(OUT1, act_hi, act_lo, act_lo_done, 8)
            pe.wait_ge(mem_landed, 16)
            pe.wait_ge(br_free, 4)
            for b in range(4):
                for m in range(2):
                    for t in range(2):
                        d0 = (2 * b + m) * P
                        mm = pe.transpose(pair[ACC + b][:, m, t * P:t * P + P], mem_nat[:, t, d0:d0 + P], ident)
                mm.then_inc(memt_turned, 1)
            up(OUT1 + 1, act_hi, act_lo)
            up(OUT1 + 2, act_hi, act_lo)
            sums(1)
            up(OUT1 + 3, act_hi, act_lo)
            up(MEMK, mix_hi, mix_lo, mem_lo_done, 0)
            sums(2)
            up(MEMK + 1, mix_hi, mix_lo)
            head_norm(A_KMEM[0], H_KMEM, ones, True)
            up(MEMK + 2, mix_hi, mix_lo)
            head_norm(A_KMEM[1], H_KMEM + 1, ones, True)
            turn_rs(A_TOKM, rs_mem, 1)
            up(MEMK + 3, mix_hi, mix_lo)
            head_norm(A_KMEM[2], H_KMEM + 2, ones, True)
            pe.wait_ge(memt_done, 4)
            feed_forward(0, 2, 3, lambda: head_norm(A_KMEM[3], H_KMEM + 3, ones, True))
            up_tok(MEMV, mix_hi, mix_lo)
            sums(4)
            for j in range(1, 4):
                up_tok(MEMV + j, mix_hi, mix_lo)
            feed_forward(1, 3, 5)
            up(DQ, act_hi, act_lo, act_lo_done, 32)
            up(DQ + 1, act_hi, act_lo)
            sums(6)
            up(DK, act_hi, act_lo)
            head_norm(A_DIFF[0], H_DIFF, halves, False)
            turn_rs(A_TOK2, rs, 6)
            up(DK + 1, act_hi, act_lo)
            head_norm(A_DIFF[1], H_DIFF + 1, halves, False)
            up_tok(RV, act_hi, act_lo)
            head_norm(A_DIFF[2], H_DIFF + 2, halves, False)
            up_tok(RV + 1, act_hi, act_lo)
            head_norm(A_DIFF[3], H_DIFF + 3, halves, False)
            up(RQ, act_hi, act_lo)
            pe.wait_ge(hn_done, H_DIFF + 4)
            for g in range(4):
                logits(g, 8, False)
            up(RQ + 1, act_hi, act_lo)
            for g in range(4, 8):
                logits(g, 8, False)
            up(RK, act_hi, act_lo)
            up(RK + 1, act_hi, act_lo)
            up_tok(DV, act_hi, act_lo)
            pe.wait_ge(lg_free, 16)
            turn_probs(6, 2, lambda m: L0[:, 2 * m, :], 0, 6)
            for e in (7, 8):
                k0 = P * (e - 7)
                turn_probs(e, 3, lambda m: L1[:, 2 * m, k0:k0 + P], 0, 6)
            up_tok(DV + 1, act_hi, act_lo)
            pe.wait_ge(up_free, upnum(RK + 1) + 1)
            pe.wait_ge(tp_free, 9)
            for h in range(4):
                pe.matmul(pair[ACC + h // 2][:, h % 2, :], rk_T[:, h, 0:P], rq_T[:, h, :], start=True, stop=True)
            for h in range(4):
                mm = pe.matmul(quad[ACC + 2][:, h, :], rk_T[:, h, P:T], rq_T[:, h, P:T], start=True, stop=True)
            mm.then_inc(sc_done, 1)
            up(RG, act_hi, act_lo)
            pe.wait_ge(at_done, 1)
            for b in range(2):
                for i in range(2):
                    h = 2 * b + i
                    pe.matmul(pair[ACC + b][:, i, :], rv_tok[0][:, h * P:h * P + P], a_T0[:, h, :],
                              start=True, stop=False)
                    mm = pe.matmul(pair[ACC + b][:, i, P:T], rv_tok[1][:, h * P:h * P + P], a_T1[:, h, :],
                                   start=False, stop=True)
            mm.then_inc(ro_done, 1)
            pe.wait_ge(up_free, upnum(DV + 1) + 1)
            for b in range(2):
                for i in range(2):
                    h = 2 * b + i
                    pe.matmul(pair[ACC + 2 + b][:, i, :], v_tok[:, 0, h * P:h * P + P], p_T0[:, h, :],
                              start=True, stop=False)
                    mm = pe.matmul(pair[ACC + 2 + b][:, i, P:T], v_tok[:, 1, h * P:h * P + P], p_T1[:, h, :],
                                   start=False, stop=True)
            mm.then_inc(pv_done, 1)
            up(RG + 1, act_hi, act_lo)
            for b in range(2):
                pe.wait_ge(ro_sum, b + 1)
                aux(A_MEAN[b])
                pe.matmul(bank[AUX][:, :], ones, ret_o[:, 2 * b:2 * b + 2, :], start=True, stop=True).then_inc(aux_done, 1)
            for b in range(2):
                head_norm(A_VAR[b], H_VAR + b, ones, False)
            for b in range(2):
                head_norm(A_DOUT[b], H_DOUT + b, ones, False)
            up(OUT2, mix_hi, mix_lo, mixlo_done, 8)
            for j in range(1, 4):
                up(OUT2 + j, mix_hi, mix_lo)
            up(MEMQ, act_hi, act_lo, act_lo_done, 40)
            up(MEMQ + 1, act_hi, act_lo)
            sums(7)

            def mem_scores(h):
                pe.wait_ge(hn_done, H_QMEM + h + 1)
                if h >= 2:
                    pe.wait_ge(exp_done, 4 + h - 1)
                for t in range(2):
                    for i in range(2):
                        mm = pe.matmul(pair[ACC][:, t, :] if h % 2 == 0 else pair[ACC + 1][:, t, :],
                                       mem_T[:, 2 * h + i, t * P:t * P + P], k_mem[:, 2 * h + i, :],
                                       start=i == 0, stop=i == 1)
                mm.then_inc(lg_done, 1)

            def mem_turn(h):
                pe.wait_ge(p_done, 4 + h + 1)
                for k in range(2):
                    for t in range(2):
                        mm = pe.transpose(pair[ACC + 2][:, k, t * P:t * P + P],
                                          p_mem[:, 2 * h + t, k * P:k * P + P], ident)
                mm.then_inc(tp_done, 1)

            def mem_values(h):
                pe.wait_ge(tp_free, 9 + h + 1)
                if h:
                    pe.wait_ge(mixlo_done, 16 + 2 * h)
                for e in range(2):
                    for k in range(2):
                        d0 = (2 * h + e) * P
                        mm = pe.matmul(pair[ACC + 3][:, e, :], v_mem[:, k, d0:d0 + P], p_memT[:, h % 2, k, :],
                                       start=k == 0, stop=k == 1)
                mm.then_inc(pv_done, 1)

            up(MEMQ + 2, act_hi, act_lo)
            head_norm(A_QMEM[0], H_QMEM, ones, True)
            up(MEMQ + 3, act_hi, act_lo)
            head_norm(A_QMEM[1], H_QMEM + 1, ones, True)
            mem_scores(0)
            head_norm(A_QMEM[2], H_QMEM + 2, ones, True)
            mem_scores(1)
            head_norm(A_QMEM[3], H_QMEM + 3, ones, True)
            mem_turn(0)
            mem_values(0)
            mem_scores(2)
            mem_turn(1)
            mem_values(1)
            mem_scores(3)
            mem_turn(2)
            mem_values(2)
            mem_turn(3)
            mem_values(3)
            up(OUTM, mix_hi, mix_lo, mixlo_done, 16)
            for j in range(1, 4):
                up(OUTM + j, mix_hi, mix_lo)
            feed_forward(2, 6, 8)
            pe.wait_ge(up_free, UP_FFN[2] + 2 * PAIRS)
            for j in range(2):
                for m in range(4):
                    pe.wait_ge(res_done, 4 * j + m + 1)
                    for t in range(2):
                        mm = pe.transpose(back[2 * j + t][:, m * P:m * P + P], m_T[:, 4 * j + m, t * P:t * P + P], ident)
                if j == 0:
                    mm.then_inc(res_turned, 1)
            mm.then_inc(res_turned, 1)
            pe.wait_ge(sq_done, 12)
            pe.wait_ge(std_done, 9)
            for t in range(2):
                for i in range(2):
                    mm = pe.matmul(bank[SUM][:, t:t + 1], sq_acc[:, i, t * P:t * P + P], ones[:, 0:1],
                                   start=i == 0, stop=i == 1)
            mm.then_inc(sum_done, 1)

        @block.scalar
        def _(act):
            copy, table_exp = ACT.Copy, ACT.Exp

            def hi(c, place=None):
                place = c % RING if place is None else place
                if isinstance(c, int):
                    act.wait_ge(landed[place], 16 * (c // RING + 1))
                    if c >= RING:
                        act.wait_ge(used, c - RING + 1)
                    act.activation(w_hi[:, place, :], stage[:, place, :], copy).then_inc(hi_done, 1)

            def hi_in_loop(t, first):
                place = first % RING
                act.wait_ge(landed[place], t * 16 + 16 * (first // RING + 1))
                act.wait_ge(used, t * 3 + (first - RING + 1))
                act.activation(w_hi[:, place, :], stage[:, place, :], copy).then_inc(hi_done, 1)

            def gained(gains, col, pairs_done, after):
                for b in range(KD):
                    act.wait_ge(x_done, pairs_done + b // 2 + 1)
                    if b == 0 and after:
                        act.wait_ge(used, after)
                    act.activation(act_hi[:, b, :], x_T[:, b, :], copy,
                                   scale=gains[:, col + b:col + b + 1]).then_inc(act_hi_done, 1)

            def warm(function):
                act.activation(small[:, 6:7], eps, function)

            def deviation(n):
                act.wait_ge(sum_done, n + 1)
                if n:
                    act.wait_ge(rs_done, n)
                act.activation(std[:, :], bank[SUM][:, 0:T], ACT.Sqrt, bias=eps, scale=1.0 / D).then_inc(std_done, 1)

            def head_deviation(n, j, width, both):
                act.wait_ge(aux_done, n + 1)
                if j:
                    act.wait_ge(hn_done, j)
                to, of = (h_std[:, 0, :], bank[AUX][:, 0:T]) if both else (h_std[:, :, :], pair[AUX])
                act.activation(to, of, ACT.Sqrt, bias=eps, scale=1.0 / width).then_inc(aux_free, 1)

            def exps(tile, L, nk):
                act.wait_ge(max_done, tile + 1)
                o = 8 * (tile % 2)
                for m in range(8):
                    e = act.activation(L[:, m, 0:nk], L[:, m, 0:nk], table_exp, bias=nmax[:, o + m:o + m + 1],
                                       accum_out=psum_[:, o + m:o + m + 1])
                e.then_inc(exp_done, 1)

            def feed_forward(f):
                base, u0 = FFN[f], UP_FFN[f]

                def hidden(t, i):
                    act.wait_ge(up_free, t * 2 + (u0 + 2 * i + 1))
                    act.activation(silu, g_s, ACT.Silu).then_inc(silu_done, 1)

                def hidden_hi(t, i, after, to):
                    act.wait_ge(h_done, t + (f * PAIRS + i + 1))
                    if after is not None:
                        act.wait_ge(used, after)
                    act.activation(to, h_T, copy).then_inc(ffn_hi_done, 1)

                hidden(0, 0)
                hidden_hi(0, 0, None if f == 0 else FFN[f - 1] + FFN_CHUNKS, ffn_hi[:, :, :])
                with act.Fori(0, PAIRS - 2) as t:
                    hi_in_loop(t, base + 4)
                    hidden(t, 1)
                    hi_in_loop(t, base + 5)
                    hi_in_loop(t, base + 6)
                    hidden_hi(t, 1, t * 3 + (base + 4), ffn_hi[:, :, :])
                last = base + FFN_CHUNKS - 1
                hi(last - 1)
                hidden(PAIRS - 2, 1)
                hi(last)
                hidden_hi(PAIRS - 2, 1, last - 1, act_hi[:, 0:2, :])
                if last + 1 < CHUNKS:
                    hi(last + 1)

            act.dma_start(ident, a["consts"][:, C_ID:C_ID + P]).then_inc(ident_landed, 16)
            act.dma_start(first_rows[:, :], a["norm_mix_pre"][0].rearrange("(k p) -> k p", p=P)).then_inc(gain_landed, 16)
            act.dma_start(const[:, P:C_END], a["consts"][:, P:C_END]).then_inc(const_landed, 16)
            act.dma_start(wf[:, :, :], a["w_in"][0].rearrange("(k p) n -> p k n", p=P)[:, :, 1536:1544]
                          ).then_inc(wf_landed, 16)
            act.dma_start(sel, a["consts"][:, C_END:C_END + 1024].rearrange("p (h m) -> p h m", h=8)
                          ).then_inc(table_landed, 16)
            hi(0)
            act.wait_ge(gain_done, 1)
            gained(first_gain, 0, 0, 0)
            hi(1)
            act.wait_ge(wf_landed, 16)
            act.wait_ge(zeroed, 10)
            act.activation(wf_hi[:, :, 0:8], wf[:, :, :], copy).then_inc(wf_hi_done, 1)
            warm(ACT.Sqrt)
            hi(2)
            deviation(0)
            hi(3)
            hi(4)
            act.wait_ge(lam_done, 1)
            act.activation(lam_e, bank[SUM][:, 0:2], table_exp).then_inc(lamx_done, 1)
            hi(5)
            hi(6)
            hi(7)
            act.wait_ge(fz_done, 1)
            act.activation(fe[0:8, :], fe[0:8, :], table_exp).then_inc(fexp_done, 1)
            act.wait_ge(fexp_done, 1)
            act.activation(fe[0:8, :], fe[0:8, :], ACT.Ln, bias=1.0).then_inc(fln_done, 1)
            for c in range(8, 15):
                hi(c)
            exps(0, L0, P)
            hi(15)
            exps(1, L1, T)

            def conv_hi(b):
                act.wait_ge(y_done, b + 1)
                if b == 0:
                    act.wait_ge(aux_done, A_F + 1)
                act.activation(mix_hi[:, b, :], y_T[:, b % 2, :], copy).then_inc(mixhi_done, 1)

            def keep_probs(e, to):
                act.wait_ge(tp_done, e + 1)
                act.activation(to, quad[ACC + (e if e < 6 else e - 6) % 4], copy).then_inc(tp_free, 1)

            conv_hi(0)
            hi(16)
            for e in range(2):
                keep_probs(e, p_T0[:, 4 * e:4 * e + 4, 0:P])
            conv_hi(1)
            hi(17)
            conv_hi(2)
            hi(18)
            for e in range(2, 4):
                keep_probs(e, p_T0[:, 4 * e - 8:4 * e - 4, P:T])
            for e in range(4, 6):
                keep_probs(e, p_T1[:, 4 * e - 16:4 * e - 12, :])
            conv_hi(3)
            act.wait_ge(tp_done, 6)
            act.dma_start(mem_nat, a["mem_2"][0].rearrange("(t p) d -> p t d", p=P)).then_inc(mem_landed, 16)
            act.wait_ge(lg_done, 8)
            act.dma_start(table[:, :, :], a["consts"][:, C_END + 1024:C_END + 3072].rearrange("p (h m) -> p h m", h=8)
                          ).then_inc(table_landed, 16)
            hi(19)
            hi(20)
            for b in range(4):
                act.wait_ge(pv_done, b + 1)
                act.activation(mix_hi[0:64, 4 + b, :], pair[ACC + b][0:64, 0, :], copy)
                act.activation(mix_hi[64:P, 4 + b, :], pair[ACC + b][64:P, 1, :], copy).then_inc(mixhi_done, 1)
            hi(21)
            for i in range(8):
                if i == 4:
                    hi(22)
                act.wait_ge(up_free, upnum(GATE_C + i) + 1)
                act.activation(gate[:, 2 * i:2 * i + 2, :], gate[:, 2 * i:2 * i + 2, :], ACT.Sigmoid).then_inc(gates_done, 1)
            hi(23)
            hi(24)
            act.wait_ge(used, GATE_A + 4)
            for i in range(4):
                if i == 2:
                    hi(25)
                act.wait_ge(merged, i + 1)
                act.activation(act_hi[:, 2 * i:2 * i + 2, :], gate_c[:, 2 * i:2 * i + 2, :], copy).then_inc(act_hi_done, 2)
            hi(26)
            hi(27)
            hi(28)
            for b in range(KD):
                act.wait_ge(memt_done, b // 2 + 1)
                if b == 0:
                    act.wait_ge(used, BR1 + 2)
                act.activation(mix_hi[:, b, :], mem_T[:, b, :], copy,
                               scale=par[:, G_MEMKV + b:G_MEMKV + b + 1]).then_inc(mem_hi_done, 1)
            deviation(1)
            hi(29)
            hi(30)
            hi(31)
            deviation(2)
            hi(32)
            head_deviation(A_KMEM[0], H_KMEM, T, True)
            gained(par, G_FFN_PRE, 4, OUT1 + 4)
            hi(33)
            head_deviation(A_KMEM[1], H_KMEM + 1, T, True)
            hi(34)
            head_deviation(A_KMEM[2], H_KMEM + 2, T, True)
            head_deviation(A_KMEM[3], H_KMEM + 3, T, True)
            deviation(3)
            warm(ACT.Silu)
            hi(35)
            feed_forward(0)
            warm(ACT.Sqrt)
            hi(66)
            hi(67)
            deviation(4)
            hi(68)
            gained(par, G_FFN1, 8, FFN[0] + FFN_CHUNKS)
            hi(69)
            hi(70)
            hi(71)
            deviation(5)
            warm(ACT.Silu)
            hi(72)
            feed_forward(1)
            hi(103)
            warm(ACT.Sqrt)
            gained(par, G_MIX2, 12, FFN[1] + FFN_CHUNKS)
            hi(104)
            hi(105)
            deviation(6)
            hi(106)
            for j in range(4):
                hi(107 + j)
                head_deviation(A_DIFF[j], H_DIFF + j, 64, False)
            hi(111)
            hi(112)
            exps(2, L0, P)
            hi(113)
            exps(3, L1, T)
            hi(114)
            hi(115)
            keep_probs(6, p_T0[:, 0:4, 0:P])
            keep_probs(7, p_T0[:, 0:4, P:T])
            keep_probs(8, p_T1[:, 0:4, :])
            hi(116)
            hi(117)
            for i in range(2):
                act.wait_ge(up_free, upnum(RG + i) + 1)
                act.activation(rg_s[:, 2 * i:2 * i + 2, :], rg_s[:, 2 * i:2 * i + 2, :], ACT.Silu).then_inc(rg_done, 1)
            for b in range(2):
                head_deviation(A_VAR[b], H_VAR + b, P, False)
            for b in range(2):
                head_deviation(A_DOUT[b], H_DOUT + b, P, False)
            for b in range(4):
                src = ret_o if b < 2 else diff_o
                act.wait_ge(y_done, 4 + b + 1)
                if b == 0:
                    act.wait_ge(used, MEMV + 4)
                i = 2 * (b % 2)
                act.activation(mix_hi[:, 2 * b:2 * b + 2, :], src[:, i:i + 2, :], copy).then_inc(mixhi_done, 2)
            for c in range(118, 122):
                hi(c)
            gained(par, G_MEMQ, 16, RG + 2)
            hi(122)
            hi(123)
            deviation(7)
            hi(124)
            hi(125)

            def mem_exps(h):
                act.wait_ge(max_done, 4 + h + 1)
                for t in range(2):
                    i = 2 * h + t
                    e = act.activation(p_mem[:, i, :], pair[ACC + h % 2][:, t, :], table_exp, bias=nmax[:, i:i + 1],
                                       scale=1.0 / 16, accum_out=psum_[:, i:i + 1])
                e.then_inc(exp_done, 1)

            def mem_out(h):
                act.wait_ge(tp_done, 9 + h + 1)
                act.activation(p_memT[:, h % 2, :, :], pair[ACC + 2], copy).then_inc(tp_free, 1)

            def mem_hi(h):
                act.wait_ge(pv_done, 5 + h + 1)
                if h == 0:
                    act.wait_ge(used, OUT2 + 4)
                act.activation(mix_hi[:, 2 * h:2 * h + 2, :], pair[ACC + 3], copy).then_inc(mixhi_done, 2)

            head_deviation(A_QMEM[0], H_QMEM, T, True)
            hi(126)
            head_deviation(A_QMEM[1], H_QMEM + 1, T, True)
            mem_exps(0)
            head_deviation(A_QMEM[2], H_QMEM + 2, T, True)
            mem_exps(1)
            head_deviation(A_QMEM[3], H_QMEM + 3, T, True)
            mem_out(0)
            mem_hi(0)
            mem_exps(2)
            mem_out(1)
            mem_hi(1)
            mem_exps(3)
            mem_out(2)
            mem_hi(2)
            mem_out(3)
            mem_hi(3)
            for c in range(127, 130):
                hi(c)
            gained(par, G_FFN2, 20, MEMQ + 4)
            hi(130)
            deviation(8)
            warm(ACT.Silu)
            hi(131)
            feed_forward(2)
            warm(ACT.Sqrt)
            for b in range(KD):
                act.wait_ge(x_done, 24 + b // 2 + 1)
                if b in (4, 6):
                    act.activation((h_std if b == 4 else h_sq)[:, :, :], x_T[:, b:b + 2, :], ACT.Square
                                   ).then_inc(hsq_done, 1)
                act.activation(m_T[:, b, :], x_T[:, b, :], copy, scale=par[:, G_OUT + b:G_OUT + b + 1]).then_inc(res_done, 1)
            act.wait_ge(sum_done, 10)
            act.activation(tok_std, bank[SUM][:, 0:2], ACT.Sqrt, bias=eps, scale=1.0 / D).then_inc(std_done, 1)
            act.wait_ge(rs_done, 10)
            for j in range(2):
                act.wait_ge(res_turned, j + 1)
                act.activation(natural[:, 0, 512 * j:512 * j + 512], back[2 * j][:, :], copy, scale=tok[:, 0:1]
                               ).then_inc(nat_done[0], 1)
            for j in range(2):
                act.wait_ge(nat_done[1], j + 1)
                store(act, 1, j)

        @block.vector
        def _(dve):
            steps = [0]

            def then(ins):
                steps[0] += 1
                ins.then_inc(dve_step, 1)
                dve.wait_ge(dve_step, steps[0])

            def over(r, n=2, p=slice(0, P)):
                return r[p, None, :].to_broadcast([p.stop - p.start, n, T])

            def lo(c):
                place = c % RING
                dve.wait_ge(hi_done, c + 1)
                dve.tensor_tensor(w_lo[:, place, :], stage[:, place, :], w_hi[:, place, :].bitcast(F32),
                                  ALU.subtract).then_inc(lo_done, 1)

            def lo_in_loop(t, first):
                place = first % RING
                dve.wait_ge(hi_done, t * 3 + (first + 1))
                dve.tensor_tensor(w_lo[:, place, :], stage[:, place, :], w_hi[:, place, :].bitcast(F32),
                                  ALU.subtract).then_inc(lo_done, 1)

            def gained(gains, col, prep, blocks=range(KD)):
                for b in blocks:
                    dve.wait_ge(act_hi_done, 8 * prep + b + 1)
                    dve.scalar_tensor_tensor(act_lo[:, b, :], x_T[:, b, :], gains[:, col + b:col + b + 1],
                                             act_hi[:, b, :].bitcast(F32), ALU.mult, ALU.subtract
                                             ).then_inc(act_lo_done, 1)

            def factor(n, to):
                dve.wait_ge(std_done, n + 1)
                dve.reciprocal(to[:, :], std[:, :]).then_inc(rs_done, 1)
                dve.wait_ge(rs_done, n + 1)

            def result(c):
                dve.wait_ge(used, c + 1)
                return pair[UP + upnum(c) % 2]

            def scaled(c, to, r):
                dve.tensor_tensor(to, result(c), over(r), ALU.mult).then_inc(up_free, 1)

            def scaled_tok(c, to, r):
                src = result(c)
                dve.tensor_scalar(to[0], src[:, 0, :], r[:, 0:1], None, ALU.mult)
                dve.tensor_scalar(to[1], src[:, 1, :], r[:, 1:2], None, ALU.mult).then_inc(up_free, 1)

            def keep_tok(n, to):
                dve.wait_ge(aux_done, n + 1)
                dve.tensor_copy(to[:, :], bank[AUX][:, 0:2 * P:P]).then_inc(aux_free, 1)
                dve.wait_ge(aux_free, n + 1)

            def head_norm(n, j, both, apply):
                dve.wait_ge(aux_free, n + 1)
                r = h_std[:, 0, :] if both else h_std[:, :, :]
                then(dve.reciprocal(r, r))
                apply(r).then_inc(hn_done, 1)

            def softmax_max(tile, L, nk):
                o = 8 * (tile % 2)
                dve.wait_ge(dve_step, steps[0])
                dve.tensor_reduce(nmax[:, o:o + 8], L[:, :, 0:nk], AX, ALU.max, negate=True).then_inc(max_done, 1)

            def inverse_sums(tile):
                o = 8 * (tile % 2)
                dve.wait_ge(exp_done, tile + 1)
                then(dve.reciprocal(prec[:, o:o + 8], psum_[:, o:o + 8]))
                return o

            def read_scores(g, first):
                qt, b = g // 4, g % 4
                nk = P * (qt + 1)
                L = L1 if qt else L0
                dve.wait_ge(lg_done, first + g + 1)
                for i in range(2):
                    m = 2 * b + i
                    src = pair[ACC + b][:, i, 0:nk]
                    if first == 0:
                        ins = dve.scalar_tensor_tensor(L[:, m, :], src, c_tok[:, qt, m:m + 1],
                                                       causal[:, T - nk:T], ALU.add, ALU.add)
                    else:
                        ins = dve.scalar_tensor_tensor(L[:, m, :], src, 0.125, alibi[:, b, T - nk:T],
                                                       ALU.mult, ALU.add)
                ins.then_inc(lg_free, 1)
                dve.wait_ge(lg_free, first + g + 1)

            def feed_forward(f):
                base, u0 = FFN[f], UP_FFN[f]

                def gate_part(t, i):
                    dve.wait_ge(used, t * 3 + (base + (2 + 3 * (i - 1) if i else 0) + 1))
                    dve.tensor_tensor(g_s, pair[UP], over(rs), ALU.mult).then_inc(up_free, 1)

                def up_part(t, i, chunk, to=ffn_lo[:, :, :], of=ffn_hi[:, :, :]):
                    n = f * PAIRS + i + 1
                    dve.wait_ge(used, t * 3 + (chunk + 1))
                    dve.tensor_tensor(u_s, pair[UP + 1], over(rs), ALU.mult).then_inc(up_free, 1)
                    dve.wait_ge(up_free, t * 2 + (u0 + 2 * i + 2))
                    dve.wait_ge(silu_done, t + n)
                    dve.tensor_tensor(h_T, u_s, silu, ALU.mult).then_inc(h_done, 1)
                    dve.wait_ge(ffn_hi_done, t + n)
                    dve.tensor_tensor(to, h_T, of.bitcast(F32), ALU.subtract).then_inc(ffn_lo_done, 1)

                gate_part(0, 0)
                up_part(0, 0, base + 1)
                with dve.Fori(0, PAIRS - 2) as t:
                    lo_in_loop(t, base + 4)
                    gate_part(t, 1)
                    lo_in_loop(t, base + 5)
                    lo_in_loop(t, base + 6)
                    up_part(t, 1, base + 4)
                last = base + FFN_CHUNKS - 1
                lo(last - 1)
                gate_part(PAIRS - 2, 1)
                lo(last)
                up_part(PAIRS - 2, 1, base + 3, act_lo[:, 0:2, :], act_hi[:, 0:2, :])
                if last + 1 < CHUNKS:
                    lo(last + 1)

            def down_ready(f, p):
                if p < 3:
                    dve.wait_ge(down_done, 3 * f + p + 1)
                else:
                    dve.wait_ge(used, FFN[f] + FFN_CHUNKS)
                return pair[ACC + p]

            def post_pair(p, col, count):
                for b in (2 * p, 2 * p + 1):
                    ins = dve.scalar_tensor_tensor(m_T[:, b, :], m_T[:, b, :], par[:, col + b:col + b + 1],
                                                   rs_post[:, :], ALU.mult, ALU.mult)
                then(ins)
                dve.tensor_tensor(x_T[:, 2 * p:2 * p + 2, :], x_T[:, 2 * p:2 * p + 2, :], m_T[:, 2 * p:2 * p + 2, :],
                                  ALU.add).then_inc(x_done, 1)
                dve.wait_ge(x_done, count + p + 1)

            dve.wait_ge(gain_turned, 1)
            dve.tensor_copy(first_gain[:, :], bank[SUM][:, 0:KD]).then_inc(gain_done, 1)
            for b in range(4):
                dve.wait_ge(x_turned, b + 1)
                dve.tensor_copy(x_T[:, 2 * b:2 * b + 2, :], pair[ACC + b]).then_inc(x_done, 1)
            dve.wait_ge(x_done, 4)
            lo(0)
            gained(first_gain, 0, 0)
            lo(1)
            dve.wait_ge(wf_hi_done, 1)
            dve.wait_ge(zeroed, 10)
            dve.tensor_tensor(wf_lo[:, :, 0:8], wf[:, :, :], wf_hi[:, :, 0:8].bitcast(F32), ALU.subtract
                              ).then_inc(wf_lo_done, 1)
            lo(2)
            factor(0, rs)

            def query(c):
                src, b = result(c), 2 * (c - Q)
                dve.scalar_tensor_tensor(q_pad[0:64, 0, b:b + 2, :], src[0:64, :, :], 0.125, over(rs, p=slice(0, 64)),
                                         ALU.mult, ALU.mult)
                dve.scalar_tensor_tensor(q_pad[64:P, 1, b:b + 2, :], src[64:P, :, :], 0.125, over(rs, p=slice(64, P)),
                                         ALU.mult, ALU.mult).then_inc(up_free, 1)

            query(Q)
            lo(3)
            query(Q + 1)
            dve.wait_ge(par_turned, 1)
            dve.tensor_copy(par[:, :], bank[SUM][:, 0:P]).then_inc(par_ready, 1)
            dve.wait_ge(par_ready, 1)
            dve.tensor_tensor(lam_p[0:64, 0:1], par[0:64, LAMQ:LAMQ + 1], par[0:64, LAMK:LAMK + 1], ALU.mult)
            dve.tensor_tensor(lam_p[64:P, 1:2], par[64:P, LAMQ:LAMQ + 1], par[64:P, LAMK:LAMK + 1], ALU.mult
                              ).then_inc(par_ready, 1)
            lo(4)
            scaled(K, k_T[:, 0:2, :], rs)
            lo(5)
            dve.wait_ge(lamx_done, 1)
            then(dve.tensor_tensor(lam, lam_e[:, 1:2], lam_e[:, 0:1], ALU.subtract))
            then(dve.tensor_scalar(lam, lam, -LAM_INIT, None, ALU.add))
            then(dve.tensor_scalar(par[:, DIFN:DIFN + 1], par[:, DIFN:DIFN + 1], 1.0 - LAM_INIT, None, ALU.mult))
            keep_tok(A_TOKX, tok)
            scaled(K + 1, k_T[:, 2:4, :], rs)
            lo(6)
            dve.wait_ge(aux_done, A_F + 1)
            dve.tensor_tensor(fz[0:8, :], bank[AUX][0:8, 0:T], rs[0:8, :], ALU.mult).then_inc(aux_free, 1)
            dve.wait_ge(aux_free, A_F + 1)
            then(dve.tensor_scalar(fz[0:8, :], fz[0:8, :], par[0:8, BF:BF + 1], None, ALU.add))
            dve.scalar_tensor_tensor(fe[0:8, :], fz[0:8, :], -1.0, fz[0:8, :], ALU.mult, ALU.min).then_inc(fz_done, 1)
            scaled_tok(V, [v_tok[:, t, 0:256] for t in range(2)], tok)
            lo(7)
            scaled_tok(V + 1, [v_tok[:, t, 256:512] for t in range(2)], tok)
            lo(8)
            dve.wait_ge(fln_done, 1)
            dve.scalar_tensor_tensor(logf[0:8, :], fz[0:8, :], 0.0, fe[0:8, :], ALU.min, ALU.subtract).then_inc(logf_done, 1)
            scaled(GB, gb_T[:, 0:2, :], rs)
            lo(9)
            scaled(GB + 1, gb_T[:, 2:4, :], rs)
            lo(10)
            dve.wait_ge(aux_done, A_LOGF + 1)
            dve.tensor_copy(logf_tok[:, :, :], pair[AUX].rearrange("p a t -> p (a t)")[:, 0:2 * P].rearrange(
                "p (t q) -> p t q", t=2)[:, :, 0:8]).then_inc(aux_free, 1)
            scaled(GC, z_T[:, 0:2, 2:T + 2], rs)
            lo(11)
            dve.wait_ge(aux_done, A_CUM + 1)
            dve.tensor_copy(c_tok[:, :, :].rearrange("p a b -> p (a b)"), bank[AUX][:, 0:16])
            dve.tensor_scalar(negc[0:8, :], bank[AUX][0:8, T:2 * T], -1.0, None, ALU.mult).then_inc(aux_free, 1)
            dve.wait_ge(aux_free, A_CUM + 1)
            scaled(GC + 1, z_T[:, 2:4, 2:T + 2], rs)
            lo(12)
            scaled(HC, hc_T[:, 0, :, :], rs)
            lo(13)
            for g in range(4):
                read_scores(g, 0)
            softmax_max(0, L0, P)
            scaled(HC + 1, hc_T[:, 1, :, :], rs)
            lo(14)
            for g in range(4, 8):
                read_scores(g, 0)
            softmax_max(1, L1, T)
            scaled(GATE_C, gate[:, 0:2, :], rs)
            lo(15)

            def normal(tile, L, nk):
                o = inverse_sums(tile)
                dve.tensor_tensor(L[:, :, 0:nk], L[:, :, 0:nk], prec[:, o:o + 8, None].to_broadcast([P, 8, nk]), ALU.mult
                                  ).then_inc(p_done, 1)

            def conv(b):
                dve.wait_ge(z_done, b // 2 + 1)
                if b >= 2:
                    dve.wait_ge(mixhi_done, b - 1)
                y = y_T[:, b % 2, :]
                for j in range(3):
                    w = par[:, CONV + 4 * j + b:CONV + 4 * j + b + 1]
                    if j == 0:
                        then(dve.tensor_scalar(y, z_T[:, b, 0:T], w, None, ALU.mult))
                    else:
                        then(dve.scalar_tensor_tensor(y, z_T[:, b, j:j + T], w, y, ALU.mult, ALU.add))
                dve.tensor_tensor(y, y, gb_T[:, b, :], ALU.mult).then_inc(y_done, 1)

            def conv_lo(b):
                dve.wait_ge(mixhi_done, b + 1)
                dve.tensor_tensor(mix_lo[:, b, :], y_T[:, b % 2, :], mix_hi[:, b, :].bitcast(F32), ALU.subtract
                                  ).then_inc(mixlo_done, 1)

            scaled(GATE_C + 1, gate[:, 2:4, :], rs)
            normal(0, L0, P)
            conv(0)
            lo(16)
            scaled(GATE_C + 2, gate[:, 4:6, :], rs)
            normal(1, L1, T)
            conv_lo(0)
            conv(1)
            lo(17)
            scaled(GATE_C + 3, gate[:, 6:8, :], rs)
            conv_lo(1)
            conv(2)
            lo(18)
            scaled(GATE_A, gate[:, 8:10, :], rs)
            conv_lo(2)
            conv(3)
            lo(19)
            scaled(GATE_A + 1, gate[:, 10:12, :], rs)
            conv_lo(3)
            lo(20)
            scaled(GATE_A + 2, gate[:, 12:14, :], rs)
            for b in range(4):
                dve.wait_ge(mixhi_done, 4 + b + 1)
                for p, i in ((slice(0, 64), 0), (slice(64, P), 1)):
                    ins = dve.tensor_tensor(mix_lo[p, 4 + b, :], pair[ACC + b][p, i, :], mix_hi[p, 4 + b, :].bitcast(F32),
                                            ALU.subtract)
                ins.then_inc(mixlo_done, 1)
            lo(21)
            scaled(GATE_A + 3, gate[:, 14:16, :], rs)
            lo(22)
            for j in range(2):
                dve.wait_ge(used, BR0 + j + 1)
                dve.wait_ge(gates_done, 2 * j + 2)
                for i in range(2):
                    g = gate_c[:, 4 * j + 2 * i:4 * j + 2 * i + 2, :]
                    ins = dve.tensor_tensor(g, pair[ACC + 2 * j + i], g, ALU.mult)
                ins.then_inc(br_free, 1)
                lo(23 + j)
            for j in range(2):
                dve.wait_ge(used, BR1 + j + 1)
                dve.wait_ge(gates_done, 4 + 2 * j + 2)
                for i in range(2):
                    g = gate_a[:, 4 * j + 2 * i:4 * j + 2 * i + 2, :]
                    ins = dve.tensor_tensor(g, pair[ACC + 2 * j + i], g, ALU.mult)
                ins.then_inc(br_free, 1)
                dve.wait_ge(br_free, 3 + j)
                for i in range(2):
                    s = slice(4 * j + 2 * i, 4 * j + 2 * i + 2)
                    dve.tensor_tensor(gate_c[:, s, :], gate_c[:, s, :], gate_a[:, s, :], ALU.add).then_inc(merged, 1)
                for i in range(2):
                    s = slice(4 * j + 2 * i, 4 * j + 2 * i + 2)
                    dve.wait_ge(act_hi_done, 8 + 4 * j + 2 * i + 2)
                    dve.tensor_tensor(act_lo[:, s, :], gate_c[:, s, :], act_hi[:, s, :].bitcast(F32), ALU.subtract
                                      ).then_inc(act_lo_done, 2)
            lo(25)
            lo(26)

            def out1(p):
                dve.tensor_copy(m_T[:, 2 * p:2 * p + 2, :], result(OUT1 + p)).then_inc(up_free, 1)

            out1(0)
            for b in range(4):
                dve.wait_ge(memt_turned, b + 1)
                dve.tensor_copy(mem_T[:, 2 * b:2 * b + 2, :], pair[ACC + b]).then_inc(memt_done, 1)
            lo(27)
            out1(1)
            lo(28)
            dve.wait_ge(memt_done, 4)
            for b in range(KD):
                dve.wait_ge(mem_hi_done, b + 1)
                dve.scalar_tensor_tensor(mix_lo[:, b, :], mem_T[:, b, :], par[:, G_MEMKV + b:G_MEMKV + b + 1],
                                         mix_hi[:, b, :].bitcast(F32), ALU.mult, ALU.subtract).then_inc(mem_lo_done, 1)
            out1(2)
            factor(1, rs_mem)
            lo(29)
            out1(3)
            lo(30)

            def key_raw(j):
                scaled(MEMK + j, raw_k[:, 2 * j:2 * j + 2, :], rs_mem)

            def key(j):
                def apply(r):
                    for i in range(2):
                        ins = dve.scalar_tensor_tensor(k_mem[:, 2 * j + i, :], raw_k[:, 2 * j + i, :],
                                                       par[:, MKN + i:MKN + i + 1], r, ALU.mult, ALU.mult)
                    return ins
                head_norm(A_KMEM[j], H_KMEM + j, True, apply)

            key_raw(0)
            lo(31)
            factor(2, rs_post)
            for p in range(2):
                post_pair(p, G_MIX_POST, 4)
            key_raw(1)
            lo(32)
            for p in range(2, 4):
                post_pair(p, G_MIX_POST, 4)
            key(0)
            gained(par, G_FFN_PRE, 2, range(0, 4))
            key_raw(2)
            gained(par, G_FFN_PRE, 2, range(4, 8))
            lo(33)
            key(1)
            keep_tok(A_TOKM, tok_mem)
            key_raw(3)
            lo(34)
            key(2)
            key(3)
            factor(3, rs)
            lo(35)
            feed_forward(0)

            def memory_values(j):
                scaled_tok(MEMV + j, [v_mem[:, t, 256 * j:256 * j + 256] for t in range(2)], tok_mem)

            for p in range(4):
                src = down_ready(0, p)
                dve.tensor_copy(m_T[:, 2 * p:2 * p + 2, :], src).then_inc(m_done, 1)
            lo(66)
            memory_values(0)
            lo(67)
            factor(4, rs_post)
            for p in range(2):
                post_pair(p, G_FFN_POST, 8)
            memory_values(1)
            lo(68)
            for p in range(2, 4):
                post_pair(p, G_FFN_POST, 8)
            gained(par, G_FFN1, 3, range(0, 4))
            memory_values(2)
            gained(par, G_FFN1, 3, range(4, 8))
            lo(69)
            lo(70)
            memory_values(3)
            lo(71)
            factor(5, rs)
            lo(72)
            feed_forward(1)

            def half_residual(f, count):
                for p in range(4):
                    src = down_ready(f, p)
                    xs = x_T[:, 2 * p:2 * p + 2, :]
                    dve.scalar_tensor_tensor(xs, src, 0.5, xs, ALU.mult, ALU.add).then_inc(x_done, 1)
                    dve.wait_ge(x_done, count + p + 1)

            lo(103)
            half_residual(1, 12)
            gained(par, G_MIX2, 4)
            lo(104)
            lo(105)
            factor(6, rs)

            def diff_raw(j):
                scaled(DQ + j, raw[:, 2 * j:2 * j + 2, :], rs)

            def diff_qk(j):
                def apply(r):
                    s = slice(2 * (j % 2), 2 * (j % 2) + 2)
                    src = raw[:, 2 * j:2 * j + 2, :]
                    if j >= 2:
                        return dve.scalar_tensor_tensor(k_T[:, s, :], src, par[:, DKN:DKN + 1], r, ALU.mult, ALU.mult)
                    for p, i in ((slice(0, 64), 0), (slice(64, P), 1)):
                        ins = dve.scalar_tensor_tensor(q_pad[p, i, s, :], src[p], par[p, DQN:DQN + 1], r[p],
                                                       ALU.mult, ALU.mult)
                    return ins
                head_norm(A_DIFF[j], H_DIFF + j, False, apply)

            diff_raw(0)
            diff_raw(1)
            lo(106)
            dve.wait_ge(zeroed, 11)
            lo(107)
            diff_qk(0)
            keep_tok(A_TOK2, tok)
            diff_raw(2)
            diff_raw(3)
            lo(108)
            diff_qk(1)
            scaled_tok(RV, [r[:, 0:256] for r in rv_tok], tok)
            lo(109)
            diff_qk(2)
            scaled_tok(RV + 1, [r[:, 256:512] for r in rv_tok], tok)
            lo(110)
            diff_qk(3)
            scaled(RQ, rq_T[:, 0:2, :], rs)
            lo(111)
            dve.wait_ge(table_landed, 32)
            for g in range(4):
                read_scores(g, 8)
            softmax_max(2, L0, P)
            scaled(RQ + 1, rq_T[:, 2:4, :], rs)
            lo(112)
            for g in range(4, 8):
                read_scores(g, 8)
            softmax_max(3, L1, T)
            scaled(RK, rk_T[:, 0:2, :], rs)
            lo(113)

            def difference(tile, L, nk):
                o = inverse_sums(tile)
                odd = prec[:, o + 1:o + 8:2]
                then(dve.tensor_scalar(odd, odd, lam, None, ALU.mult))
                then(dve.tensor_tensor(L[:, :, 0:nk], L[:, :, 0:nk], prec[:, o:o + 8, None].to_broadcast([P, 8, nk]), ALU.mult))
                dve.tensor_tensor(L[:, 0:8:2, 0:nk], L[:, 0:8:2, 0:nk], L[:, 1:8:2, 0:nk], ALU.add).then_inc(p_done, 1)

            difference(2, L0, P)
            scaled(RK + 1, rk_T[:, 2:4, :], rs)
            lo(114)
            difference(3, L1, T)
            scaled_tok(DV, [v_tok[:, t, 0:256] for t in range(2)], tok)
            lo(115)
            scaled_tok(DV + 1, [v_tok[:, t, 256:512] for t in range(2)], tok)
            lo(116)
            dve.wait_ge(sc_done, 1)
            for b in range(2):
                dve.tensor_tensor(a_T0[:, 2 * b:2 * b + 2, :], pair[ACC + b], decay[:, 2 * b:2 * b + 2, :], ALU.mult)
            dve.tensor_tensor(a_T1, quad[ACC + 2], decay[:, :, 0:P], ALU.mult).then_inc(at_done, 1)
            scaled(RG, rg_s[:, 0:2, :], rs)
            lo(117)
            dve.wait_ge(ro_done, 1)
            for b in range(2):
                dve.tensor_copy(ret_o[:, 2 * b:2 * b + 2, :], pair[ACC + b]).then_inc(ro_sum, 1)
            dve.wait_ge(pv_done, 5)
            for b in range(2):
                dve.tensor_copy(diff_o[:, 2 * b:2 * b + 2, :], pair[ACC + 2 + b]).then_inc(diff_done, 1)
            scaled(RG + 1, rg_s[:, 2:4, :], rs)
            dve.wait_ge(ro_sum, 2)
            for b in range(2):
                o = ret_o[:, 2 * b:2 * b + 2, :]
                dve.wait_ge(aux_done, A_MEAN[b] + 1)
                dve.scalar_tensor_tensor(o, pair[AUX], -1.0 / P, o, ALU.mult, ALU.add).then_inc(aux_free, 1)
                dve.wait_ge(aux_free, A_MEAN[b] + 1)
            for b in range(2):
                o = ret_o[:, 2 * b:2 * b + 2, :]
                head_norm(A_VAR[b], H_VAR + b, False, lambda r: dve.scalar_tensor_tensor(
                    o, o, par[:, RETN:RETN + 1], r, ALU.mult, ALU.mult))
                dve.wait_ge(hn_done, H_VAR + b + 1)
                dve.wait_ge(rg_done, b + 1)
                dve.tensor_tensor(o, o, rg_s[:, 2 * b:2 * b + 2, :], ALU.mult).then_inc(y_done, 1)
            dve.wait_ge(diff_done, 2)
            for b in range(2):
                o = diff_o[:, 2 * b:2 * b + 2, :]
                head_norm(A_DOUT[b], H_DOUT + b, False, lambda r: dve.scalar_tensor_tensor(
                    o, o, par[:, DIFN:DIFN + 1], r, ALU.mult, ALU.mult))
                dve.wait_ge(hn_done, H_DOUT + b + 1)
                dve.engine_nop().then_inc(y_done, 1)
            dve.wait_ge(y_done, 8)
            for b in range(4):
                i = 2 * (b % 2)
                src = (ret_o if b < 2 else diff_o)[:, i:i + 2, :]
                dve.wait_ge(mixhi_done, 8 + 2 * b + 2)
                dve.tensor_tensor(mix_lo[:, 2 * b:2 * b + 2, :], src, mix_hi[:, 2 * b:2 * b + 2, :].bitcast(F32), ALU.subtract
                                  ).then_inc(mixlo_done, 2)

            def residual(c, p, count):
                xs = x_T[:, 2 * p:2 * p + 2, :]
                dve.tensor_tensor(xs, result(c), xs, ALU.add).then_inc(x_done, 1)
                dve.wait_ge(x_done, count + p + 1)
                dve.sem_inc(up_free, 1)

            for j in range(4):
                lo(118 + j)
                residual(OUT2 + j, j, 16)
            gained(par, G_MEMQ, 5)
            lo(122)
            lo(123)
            factor(7, rs)

            def mem_raw(j):
                scaled(MEMQ + j, raw[:, 2 * j:2 * j + 2, :], rs)

            def mem_query(j):
                def apply(r):
                    for i in range(2):
                        ins = dve.scalar_tensor_tensor(mem_T[:, 2 * j + i, :], raw[:, 2 * j + i, :],
                                                       par[:, MQN + i:MQN + i + 1], r, ALU.mult, ALU.mult)
                    return ins
                head_norm(A_QMEM[j], H_QMEM + j, True, apply)

            def mem_max(h):
                dve.wait_ge(lg_done, 16 + h + 1)
                then(dve.tensor_reduce(nmax[:, 2 * h:2 * h + 2], pair[ACC + h % 2], AX, ALU.max, negate=True))
                dve.tensor_scalar(nmax[:, 2 * h:2 * h + 2], nmax[:, 2 * h:2 * h + 2], 1.0 / 16, None, ALU.mult
                                  ).then_inc(max_done, 1)

            def mem_normal(h):
                dve.wait_ge(exp_done, 4 + h + 1)
                s = slice(2 * h, 2 * h + 2)
                then(dve.reciprocal(prec[:, s], psum_[:, s]))
                dve.tensor_tensor(p_mem[:, s, :], p_mem[:, s, :], prec[:, s, None].to_broadcast([P, 2, T]), ALU.mult
                                  ).then_inc(p_done, 1)

            def mem_lo(h):
                s = slice(2 * h, 2 * h + 2)
                dve.wait_ge(mixhi_done, 16 + 2 * h + 2)
                dve.tensor_tensor(mix_lo[:, s, :], pair[ACC + 3], mix_hi[:, s, :].bitcast(F32), ALU.subtract
                                  ).then_inc(mixlo_done, 2)

            mem_raw(0)
            mem_raw(1)
            lo(124)
            mem_raw(2)
            lo(125)
            mem_query(0)
            mem_raw(3)
            lo(126)
            mem_query(1)
            mem_max(0)
            mem_query(2)
            mem_max(1)
            mem_normal(0)
            mem_query(3)
            mem_normal(1)
            mem_lo(0)
            mem_max(2)
            mem_lo(1)
            mem_normal(2)
            mem_max(3)
            mem_lo(2)
            mem_normal(3)
            mem_lo(3)
            for j in range(4):
                if j < 3:
                    lo(127 + j)
                residual(OUTM + j, j, 20)
            gained(par, G_FFN2, 6)
            lo(130)
            factor(8, rs)
            lo(131)
            feed_forward(2)
            half_residual(2, 24)
            for i, squares in enumerate((h_std, h_sq)):
                dve.wait_ge(sq_done, 10 + i)
                dve.wait_ge(hsq_done, 17 + i)
                dve.tensor_tensor(sq_acc[:, :, :], sq_acc[:, :, :], squares[:, :, :], ALU.add).then_inc(sq_done, 1)
            dve.wait_ge(std_done, 10)
            dve.reciprocal(tok[:, :], tok_std).then_inc(rs_done, 1)
            dve.wait_ge(rs_done, 10)
            for j in range(2):
                dve.wait_ge(res_turned, j + 1)
                dve.tensor_scalar(natural[:, 1, 512 * j:512 * j + 512], back[2 * j + 1][:, :], tok[:, 1:2], None, ALU.mult
                                  ).then_inc(nat_done[1], 1)

        @block.gpsimd
        def _(pool):
            steps = [0]

            def then(ins):
                steps[0] += 1
                ins.then_inc(pool_step, 1)
                pool.wait_ge(pool_step, steps[0])

            def squares(n, src, ready, base, pairs=4):
                for p in range(pairs):
                    pool.wait_ge(ready, base + p + 1)
                    if p == 0 and n:
                        pool.wait_ge(sum_done, n)
                    s = src[:, 2 * p:2 * p + 2, :]
                    if p == 0:
                        then(pool.tensor_tensor(sq_acc[:, :, :], s, s, ALU.mult))
                        continue
                    then(pool.tensor_tensor(sq_tmp[:, :, :], s, s, ALU.mult))
                    ins = pool.tensor_tensor(sq_acc[:, :, :], sq_acc[:, :, :], sq_tmp[:, :, :], ALU.add)
                    if p < pairs - 1:
                        then(ins)
                    else:
                        ins.then_inc(sq_done, 1)

            def head_squares(src, before):
                if before is not None:
                    pool.wait_ge(aux_done, before + 1)
                pool.tensor_tensor(h_sq[:, :, :], src, src, ALU.mult).then_inc(hsq_done, 1)

            pool.memset(par_rows[:, :], 0.0).then_inc(zeroed, 1)
            pool.memset(small[:, :], 0.0).then_inc(zeroed, 1)
            pool.memset(wf_hi.bitcast(F32), 0.0).then_inc(zeroed, 1)
            pool.memset(wf_lo.bitcast(F32), 0.0).then_inc(zeroed, 1)
            pool.memset(q_pad[:, :, :, :], 0.0).then_inc(zeroed, 1)
            pool.memset(logf[:, :], 0.0).then_inc(zeroed, 1)
            pool.memset(negc[:, :], 0.0).then_inc(zeroed, 1)
            pool.memset(z_T[:, :, 0:2], 0.0).then_inc(zeroed, 1)
            pool.memset(eps_t[:, :], EPS).then_inc(zeroed, 1)
            pool.memset(fe[:, :], 0.0).then_inc(zeroed, 1)
            squares(0, x_T, x_done, 0)
            for j in range(2):
                pool.wait_ge(up_free, upnum(HC + j) + 1)
                zs = z_T[:, 2 * j:2 * j + 2, 2:T + 2]
                pool.tensor_tensor(zs, zs, hc_T[:, j, :, :], ALU.mult).then_inc(z_done, 1)
            squares(1, mem_T, memt_done, 0)
            squares(2, m_T, up_free, upnum(OUT1))
            for j in range(3):
                pool.wait_ge(up_free, upnum(MEMK + j) + 1)
                head_squares(raw_k[:, 2 * j:2 * j + 2, :], A_KMEM[j - 1] if j else None)
            squares(3, x_T, x_done, 4)
            pool.wait_ge(up_free, upnum(MEMK + 3) + 1)
            head_squares(raw_k[:, 6:8, :], A_KMEM[2])
            squares(4, m_T, m_done, 0)
            squares(5, x_T, x_done, 8)
            pool.wait_ge(mem_lo_done, 8)
            pool.memset(q_pad[:, :, :, :], 0.0).then_inc(zeroed, 1)
            squares(6, x_T, x_done, 12)
            for j in range(4):
                pool.wait_ge(up_free, upnum(DQ + j) + 1)
                head_squares(raw[:, 2 * j:2 * j + 2, :], A_DIFF[j - 1] if j else A_KMEM[3])
            for b in range(2):
                pool.wait_ge(aux_free, A_MEAN[b] + 1)
                head_squares(ret_o[:, 2 * b:2 * b + 2, :], A_VAR[0] if b else A_DIFF[3])
            for b in range(2):
                pool.wait_ge(diff_done, b + 1)
                head_squares(diff_o[:, 2 * b:2 * b + 2, :], A_DOUT[0] if b else A_VAR[1])
            squares(7, x_T, x_done, 16)
            for j in range(4):
                pool.wait_ge(up_free, upnum(MEMQ + j) + 1)
                head_squares(raw[:, 2 * j:2 * j + 2, :], A_QMEM[j - 1] if j else A_DOUT[1])
            squares(8, x_T, x_done, 20)
            squares(9, x_T, x_done, 24, 2)


def constants():
    import numpy as np

    i = np.arange(P)
    q, k = np.arange(P)[:, None], np.arange(T)[None, :]
    tri = np.concatenate([i[:, None] <= i[None, :], np.ones((P, P))], 1)
    causal = np.where(P + q >= k, 0.0, -1e30)
    sel = (i[:, None, None] == np.arange(8)[None, :, None]) * np.ones((1, 1, P))
    dist = P + q - k
    slopes = 2.0 ** (-8.0 * np.arange(1, 5) / 4)
    alibi = np.where(dist[:, None, :] >= 0, -slopes[None, :, None] * dist[:, None, :], -1e30)
    rel = np.arange(T)[None, :] - i[:, None]
    gamma = 1.0 - 2.0 ** (-5.0 - np.arange(4))
    decay = np.where(rel[:, None, :] >= 0, gamma[None, :, None] ** np.maximum(rel, 0)[:, None, :], 0.0) * P ** -0.5
    parts = [np.eye(P), np.ones((P, P)), i[:, None] // 64 == i[None, :] // 64, tri, causal, sel, alibi, decay]
    return np.concatenate([np.asarray(x, np.float32).reshape(P, -1) for x in parts], 1)


def kernel(**inputs):
    import numpy as np
    import concourse.bacc as bacc
    from concourse.bass_utils import run_bass_kernel_spmd

    nc = bacc.Bacc("TRN2", target_bir_lowering=False, num_devices=1)
    arrays, args = {}, {}
    for name, value in {**inputs, "consts": constants()}.items():
        v = np.ascontiguousarray(value)
        arrays[f"in_{name}"] = v
        args[name] = nc.dram_tensor(f"in_{name}", v.shape, mybir.dt.from_np(v.dtype), kind="ExternalInput").ap()
    out = nc.dram_tensor("out_dram", (1, T, D), F32, kind="ExternalOutput").ap()
    build(nc, args, out)
    r = run_bass_kernel_spmd(nc, [arrays], core_ids=[0])
    return r.results[0]["out_dram"]
```

```python
from contextlib import ExitStack

import concourse.bass as bass
from concourse import mybir

F32 = mybir.dt.float32
F32R = mybir.dt.float32r
ALU = mybir.AluOpType
ACT = mybir.ActivationFunctionType
AX = mybir.AxisListType.X

P = 128
T = 256
D = 1024
KD = D // P
HID = 2816
PAIRS = HID // (2 * P)
CH = 2048
RING = 3
EPS = 1e-6
LAM_INIT = 0.2

Q, K, V, GB, GC, HC, GATE_C, GATE_A = 0, 2, 4, 6, 8, 10, 12, 16
BR0, BR1, OUT1, MEMK = 20, 22, 24, 28
FFN = [32, 68, 128]
MEMV = [65, 66, 67, 101]
DQ, DK, RV, RQ, RK, DV, RG = 102, 104, 106, 108, 110, 112, 114
OUT2, MEMQ, OUTM = 116, 120, 124
CHUNKS = 161
FFN_CHUNKS = 3 * PAIRS


def ffn_ups(base):
    inner = [base + 2 + 3 * t + i for t in range(PAIRS - 2) for i in (0, 2)]
    return [base, base + 1, *inner, base + FFN_CHUNKS - 4, base + FFN_CHUNKS - 3]


BANK, BEFORE, FREED = {}, {}, {}
BY_ACT = {V, V + 1, *range(OUT1, OUT1 + 4), *range(MEMK, MEMK + 4), *MEMV, RV, RV + 1, DV, DV + 1,
          *range(MEMQ, MEMQ + 4)}


def through_banks(chunks, first=0):
    for i, c in enumerate(chunks):
        b = (first + i) % 2
        BEFORE[c] = next((x for x in reversed(BANK) if BANK[x] == b), None)
        BANK[c] = b
        FREED[c] = sum((x in BY_ACT) == (c in BY_ACT) for x in BANK)


through_banks(range(Q, BR0))
through_banks(range(OUT1, OUT1 + 8))
through_banks(ffn_ups(FFN[0]))
through_banks(MEMV[:3], 1)
through_banks(ffn_ups(FFN[1]))
through_banks(MEMV[3:], 1)
through_banks(range(DQ, OUT2 + 4))
through_banks(range(MEMQ, MEMQ + 4))
through_banks(ffn_ups(FFN[2]))
UP_FFN = [FREED[b] - 1 for b in FFN]


def made(n):
    return n + 1 if n < 7 else n


A_TOKX, A_F, A_LOGF, A_CUM = 0, 1, 2, 3
A_DIFF = [4, 6, 7, 8]
A_TOK2 = 5
A_MEAN = [9, 10]
A_VAR = [11, 12]
A_DOUT = [13, 14]
A_QMEM = [15, 16]
A_BEFORE_FFN = [4, 4, 17]
H_DIFF, H_VAR, H_DOUT = 0, 4, 6

G_MIX_PRE, G_MIX_POST, G_FFN_PRE, G_FFN_POST = 0, 8, 16, 24
G_FFN1, G_MIX2, G_MEMQ, G_MEMKV, G_FFN2, G_OUT = 32, 40, 48, 56, 64, 72
CONV, RETN, DIFN, MQN, MKN, DQN, DKN, LAMQ, LAMK, BF = 80, 92, 93, 94, 96, 98, 99, 100, 101, 102
C_ID, C_ONE, C_BD, C_TRI, C_CAUSAL, C_END = 0, 128, 256, 384, 640, 896


def build(nc, a, out):
    with ExitStack() as ctx:
        def sb(name, shape, dt=F32):
            return ctx.enter_context(nc.sbuf_tensor(name, shape, dt))

        def sem(name):
            return ctx.enter_context(nc.semaphore(name))

        stage = sb("stage", [P, RING, CH])
        w_hi = sb("w_hi", [P, RING, CH], F32R)
        w_lo = sb("w_lo", [P, RING, CH], F32R)
        x_T = sb("x_T", [P, KD, T])
        act_hi = sb("act_hi", [P, KD, T], F32R)
        act_lo = sb("act_lo", [P, KD, T], F32R)
        mix_hi = sb("mix_hi", [P, KD, T], F32R)
        mix_lo = sb("mix_lo", [P, KD, T], F32R)
        ffn_hi = sb("ffn_hi", [P, 2, T], F32R)
        ffn_lo = sb("ffn_lo", [P, 2, T], F32R)
        k_mem = sb("k_mem", [P, KD, T])
        v_mem = sb("v_mem", [P, 2, D])
        rs = sb("rs", [P, T])
        rs_post = sb("rs_post", [P, T])
        rs_mem = sb("rs_mem", [P, T])
        std = sb("std", [P, T])
        tok = sb("tok", [P, 2])
        tok_mem = sb("tok_mem", [P, 2])
        sq_acc = sb("sq_acc", [P, 2, T])
        sq_tmp = sb("sq_tmp", [P, 2, T])
        h_sq = sb("h_sq", [P, 2, T])
        h_std = sb("h_std", [P, 2, T])
        q_pad = sb("q_pad", [P, 2, 4, T])
        k_T = sb("k_T", [P, 4, T])
        v_tok = sb("v_tok", [P, 2, 512])
        L0 = sb("L0", [P, 8, P])
        L1 = sb("L1", [P, 8, T])
        gate = sb("gate", [P, 16, T])
        const = sb("const", [P, C_END])
        table = sb("table", [P, 8, T])
        par_rows = sb("par_rows", [P, P])
        par = sb("par", [P, P])
        first_rows = sb("first_rows", [KD, P])
        first_gain = sb("first_gain", [P, KD])
        wf = sb("wf", [P, KD, 8])
        forget = sb("forget", [P, 4, T])
        fz, fe, logf, negc = (forget[:, i, :] for i in range(4))
        logf_tok = sb("logf_tok", [P, 2, 8])
        c_tok = sb("c_tok", [P, 2, 8])
        small = sb("small", [P, 80])
        eps_t = sb("eps_t", [P, 1])

        natural = gate[:, 0:8, :].rearrange("p a b -> p (a b)").rearrange("p (t d) -> p t d", t=2)
        mem_nat = L1[:, :, :].rearrange("p a b -> p (a b)").rearrange("p (t d) -> p t d", t=2)
        mem_T = q_pad[:, :, :, :].rearrange("p a b t -> p (a b) t")
        p_T0 = mem_T
        p_T1 = k_T[:, :, :].rearrange("p a b -> p (a b)").rearrange("p (m q) -> p m q", m=8)
        wf_hi = mix_hi[:, 0:4, :].rearrange("p a b -> p (a b)").rearrange("p (k n) -> p k n", k=KD)
        wf_lo = mix_lo[:, 0:4, :].rearrange("p a b -> p (a b)").rearrange("p (k n) -> p k n", k=KD)
        v_flat = v_mem[:, :, :].rearrange("p a b -> p (a b)")
        gb_T = v_flat[:, 0:1024].rearrange("p (a t) -> p a t", a=4)
        hc_T = v_flat[:, 1024:2048].rearrange("p (j a t) -> p j a t", j=2, a=2)
        k_flat = k_mem[:, :, :].rearrange("p a b -> p (a b)")
        z_T = k_flat[:, 0:4 * (T + 2)].rearrange("p (a t) -> p a t", a=4)
        y_T = k_flat[:, 1040:1040 + 2 * T].rearrange("p (a t) -> p a t", a=2)
        gate_c, gate_a = gate[:, 0:8, :], gate[:, 8:16, :]
        m_T = gate[:, 8:16, :]
        g_s, silu, u_s, h_T = (gate[:, 2 * i:2 * i + 2, :] for i in range(4))
        sel = table[:, 0:4, :].rearrange("p a b -> p (a b)").rearrange("p (h m) -> p h m", h=8)
        alibi, decay = table[:, 0:4, :], table[:, 4:8, :]
        raw = gate[:, 0:8, :]
        rq_T, rk_T = gate[:, 8:12, :], gate[:, 12:16, :]
        rv_tok = [forget[:, 2 * t:2 * t + 2, :].rearrange("p a b -> p (a b)") for t in range(2)]
        a_T0 = gate[:, 0:4, :]
        a_T1 = gate[:, 4:6, :].rearrange("p a b -> p (a b)").rearrange("p (h q) -> p h q", h=4)
        rg_s, ret_o = L1[:, 0:4, :], L1[:, 4:8, :]
        diff_o = gate[:, 8:12, :]
        p_mem = L1
        p_memT = L0[:, :, :].rearrange("p a b -> p (a b)").rearrange("p (h k q) -> p h k q", h=2, k=2)
        ident = const[:, C_ID:C_ID + P]
        ones = const[:, C_ONE:C_ONE + P]
        halves = const[:, C_BD:C_BD + P]
        tri = const[:, C_TRI:C_TRI + T]
        causal = const[:, C_CAUSAL:C_CAUSAL + T]
        eps = eps_t[:, :]
        raw_k = L1[:, :, :].rearrange("p a b -> p (a b)").rearrange("p (t n) -> p t n", t=2)
        tok_std = small[:, 56:58]
        q_eps, q_f = small[:, 58:60], small[:, 60:68]
        k_eps, k_f = small[:, 68:70], small[:, 72:80]
        q_sq = [h_sq, h_std]
        nmax, psum_, prec = small[:, 8:24], small[:, 24:40], small[:, 40:56]
        lam, lam_e, lam_p = small[:, 1:2], small[:, 2:4], small[:, 4:6]

        bank = [ctx.enter_context(nc.psum_tensor(f"bank{i}", [P, 512], F32)) for i in range(8)]
        pair = [b[:, :].rearrange("p (a t) -> p a t", a=2) for b in bank]
        quad = [b[:, :].rearrange("p (a t) -> p a t", a=4) for b in bank]
        UP, SUM, AUX, ACC = 0, 2, 3, 4
        SCORES, TURN, VALUES = (ACC, ACC + 1, UP, UP + 1), (ACC + 2, SUM, SUM, UP), (ACC + 3, AUX, AUX, UP + 1)
        back = [bank[i] for i in (0, 1, 3, 4)]

        x_landed, const_landed, par_landed = sem("x_landed"), sem("const_landed"), sem("par_landed")
        ident_landed = sem("ident_landed")
        gain_landed, gain_turned, gain_done = sem("gain_landed"), sem("gain_turned"), sem("gain_done")
        wf_landed, mem_landed, table_landed = sem("wf_landed"), sem("mem_landed"), sem("table_landed")
        landed = [sem(f"landed{i}") for i in range(RING)]
        hi_done, lo_done, used = sem("hi_done"), sem("lo_done"), sem("used")
        up_free, up_free_act = sem("up_free"), sem("up_free_act")
        msq_done, post_done = sem("msq_done"), sem("post_done")
        keps_done, kdev_done, kf_done = sem("keps_done"), sem("kdev_done"), sem("kf_done")
        kscaled_done, k_turned, k_done = sem("kscaled_done"), sem("k_turned"), sem("k_done")
        zeroed, par_turned, par_ready = sem("zeroed"), sem("par_turned"), sem("par_ready")
        x_turned, x_done = sem("x_turned"), sem("x_done")
        act_hi_done, act_lo_done = sem("act_hi_done"), sem("act_lo_done")
        sq_done, sum_done, std_done, rs_done = sem("sq_done"), sem("sum_done"), sem("std_done"), sem("rs_done")
        aux_done, aux_free = sem("aux_done"), sem("aux_free")
        hsq_done, hn_done = sem("hsq_done"), sem("hn_done")
        wf_hi_done, wf_lo_done = sem("wf_hi_done"), sem("wf_lo_done")
        fz_done, fexp_done, fln_done = sem("fz_done"), sem("fexp_done"), sem("fln_done")
        logf_done = sem("logf_done")
        lg_done, lg_free, max_done, exp_done = sem("lg_done"), sem("lg_free"), sem("max_done"), sem("exp_done")
        p_done, tp_done, tp_free, pv_done = sem("p_done"), sem("tp_done"), sem("tp_free"), sem("pv_done")
        mixhi_done, mixlo_done = sem("mixhi_done"), sem("mixlo_done")
        hc_done, z_done, y_done = sem("hc_done"), sem("z_done"), sem("y_done")
        gates_done, br_free, merged = sem("gates_done"), sem("br_free"), sem("merged")
        memt_turned, memt_done = sem("memt_turned"), sem("memt_done")
        mem_hi_done, mem_lo_done = sem("mem_hi_done"), sem("mem_lo_done")
        m_done, down_done = sem("m_done"), sem("down_done")
        silu_done, h_done = sem("silu_done"), sem("h_done")
        ffn_hi_done, ffn_lo_done = sem("ffn_hi_done"), sem("ffn_lo_done")
        lam_done, lamx_done = sem("lam_done"), sem("lamx_done")
        sc_done, at_done, ro_done, rg_done = sem("sc_done"), sem("at_done"), sem("ro_done"), sem("rg_done")
        xc_done, ro_sum = sem("xc_done"), sem("ro_sum")
        diff_done = sem("diff_done")
        qsq_done, qf_done, outm_done = sem("qsq_done"), sem("qf_done"), sem("outm_done")
        dve_step, pool_step, act_step = sem("dve_step"), sem("pool_step"), sem("act_step")
        res_done, res_turned, nat_done, stored = sem("res_done"), sem("res_turned"), [sem(f"nat_done{i}") for i in range(2)], sem("stored")

        block = ctx.enter_context(nc.Block())
        w_in, w_in2 = a["w_in"][0], a["w_in_2"][0]

        def wait_read(engine, c):
            engine.wait_ge(up_free_act if c in BY_ACT else up_free, FREED[c])

        def parameters(engine):
            engine.wait_ge(zeroed, 1)

            def rows(r, n, src, cols=P, at=0):
                engine.dma_start(par_rows[r:r + n, at:at + cols], src).then_inc(par_landed, 16)

            for r, name in ((G_MIX_PRE, "norm_mix_pre"), (G_MIX_POST, "norm_mix_post"), (G_FFN_PRE, "norm_ffn_pre"),
                            (G_FFN_POST, "norm_ffn_post"), (G_FFN1, "norm_ffn1_2"), (G_MIX2, "norm_mix_2"),
                            (G_MEMQ, "norm_mem_q_2"), (G_MEMKV, "norm_mem_kv_2"), (G_FFN2, "norm_ffn2_2"),
                            (G_OUT, "norm_out_2")):
                rows(r, KD, a[name][0].rearrange("(k p) -> k p", p=P))
            rows(CONV, 12, a["conv_w"][0].rearrange("j (b p) -> (j b) p", p=P))
            rows(RETN, 1, a["ret_norm_2"])
            rows(DIFN, 1, a["diff_norm_2"])
            rows(MQN, 2, a["mem_q_norm_2"][0].rearrange("(k p) -> k p", p=P))
            rows(MKN, 2, a["mem_k_norm_2"][0].rearrange("(k p) -> k p", p=P))
            for r, name in ((DQN, "diff_q_norm_2"), (DKN, "diff_k_norm_2")):
                rows(r, 1, a[name], 64, 0)
                rows(r, 1, a[name], 64, 64)
            for r, at, name in ((LAMQ, 0, "lambda_q1_2"), (LAMQ, 64, "lambda_q2_2"),
                                (LAMK, 0, "lambda_k1_2"), (LAMK, 64, "lambda_k2_2")):
                rows(r, 1, a[name], 64, at)
            rows(BF, 1, a["b_f"], 8, 0)

        def store(engine, t, j):
            cols = slice(512 * j, 512 * j + 512)
            engine.dma_start(out[0, P * t:P * t + P, cols], natural[:, t, cols]).then_inc(stored, 16)

        @block.sync
        def _(sp):
            def slot(c):
                return c % RING

            def free(c):
                if isinstance(c, int) and c < RING:
                    return
                sp.wait_ge(lo_done, c - RING + 1)

            def whole(c, w, col, place):
                free(c)
                sp.dma_start(stage[:, place, :].rearrange("p (k n) -> p k n", k=KD),
                             w.rearrange("(k p) n -> p k n", p=P)[:, :, bass.ds(col, 2 * P)]
                             ).then_inc(landed[place], 16)

            def rows(c, w, r, n, col, width, place):
                free(c)
                sp.dma_start(stage[:, place, :].rearrange("p (k n) -> p k n", k=n),
                             w[bass.ds(r, n * P), col:col + width].rearrange("(k p) n -> p k n", p=P)
                             ).then_inc(landed[place], 16)

            def wholes(c, w, col, n):
                for i in range(n):
                    whole(c + i, w, col + 256 * i, slot(c + i))

            def feed_forward(base, w_g, g_col, w_u, u_col, w_d):
                whole(base, w_g, g_col, slot(base))
                whole(base + 1, w_u, u_col, slot(base + 1))
                with sp.Fori(0, PAIRS - 2) as t:
                    c = base + 2 + t * 3
                    whole(c, w_g, t * 256 + (g_col + 256), slot(base + 2))
                    rows(c + 1, w_d, t * 256, 2, 0, D, slot(base + 3))
                    whole(c + 2, w_u, t * 256 + (u_col + 256), slot(base + 4))
                last = base + FFN_CHUNKS - 1
                whole(last - 3, w_g, (PAIRS - 1) * 256 + g_col, slot(last - 3))
                whole(last - 2, w_u, (PAIRS - 1) * 256 + u_col, slot(last - 2))
                for i in range(2):
                    rows(last - 1 + i, w_d, (PAIRS - 2 + i) * 256, 2, 0, D, slot(last - 1 + i))

            for t in range(2):
                sp.dma_start(natural[:, t, :], a["x"][0, t * P:t * P + P, :]).then_inc(x_landed, 16)
            wholes(Q, w_in, 0, 3)
            parameters(sp)
            wholes(K + 1, w_in, 256 * 3, 3)
            wholes(GB, w_in, 1544, 14)
            for i in range(4):
                rows(BR0 + i, a["w_branch"][0, i // 2], 0, 4, 512 * (i % 2), 512, slot(BR0 + i))
            wholes(OUT1, a["w_out"][0], 0, 4)
            wholes(MEMK, a["mem_w_kv_2"][0], 0, 4)
            feed_forward(FFN[0], a["w_gate_up"][0], 0, a["w_gate_up"][0], HID, a["w_down"][0])
            wholes(MEMV[0], a["mem_w_kv_2"][0], D, 3)
            feed_forward(FFN[1], a["ffn1_w1_2"][0], 0, a["ffn1_w3_2"][0], 0, a["ffn1_w2_2"][0])
            wholes(MEMV[3], a["mem_w_kv_2"][0], D + 3 * 256, 1)
            for c, col in ((DQ, 2048), (DK, 2560), (RV, 1024), (RQ, 0), (RK, 512), (DV, 3072), (RG, 1536)):
                wholes(c, w_in2, col, 2)
            wholes(OUT2, a["w_out_2"][0], 0, 4)
            wholes(MEMQ, a["mem_w_q_2"][0], 0, 4)
            for j in range(4):
                rows(OUTM + j, a["mem_w_o_2"][0], 256 * j, 2, 0, D, slot(OUTM + j))
            feed_forward(FFN[2], a["ffn2_w1_2"][0], 0, a["ffn2_w3_2"][0], 0, a["ffn2_w2_2"][0])
            for j in range(2):
                sp.wait_ge(nat_done[0], j + 1)
                store(sp, 0, j)
            sp.wait_ge(stored, 64)

        @block.tensor
        def _(pe):
            def three(dst, w, lo_w, x, lo_x, first, last, group=True):
                pe.matmul(dst, w, x, start=first, stop=False, skip_group_check=not group)
                pe.matmul(dst, w, lo_x, start=False, stop=False, skip_group_check=not group)
                return pe.matmul(dst, lo_w, x, start=False, stop=last, skip_group_check=not group)

            def up_bank(c):
                pe.wait_ge(lo_done, c + 1)
                if BEFORE[c] is not None:
                    wait_read(pe, BEFORE[c])

            def up_product(dst, place, hi, lo, ready=None, base=0):
                wh = w_hi[:, place, :].rearrange("p (k n) -> p k n", k=KD)
                wl = w_lo[:, place, :].rearrange("p (k n) -> p k n", k=KD)
                if ready is None:
                    for m in range(2):
                        for k in range(KD):
                            mm = three(dst[:, m, :], wh[:, k, m * P:m * P + P], wl[:, k, m * P:m * P + P],
                                       hi[:, k, :], lo[:, k, :], k == 0, k == KD - 1)
                else:
                    for k in range(KD):
                        pe.wait_ge(ready, base + k + 1)
                        for m in range(2):
                            mm = three(dst[:, m, :], wh[:, k, m * P:m * P + P], wl[:, k, m * P:m * P + P],
                                       hi[:, k, :], lo[:, k, :], k == 0 and m == 0, k == KD - 1, group=False)
                mm.then_inc(used, 1)

            def up(c, hi, lo, ready=None, base=0):
                up_bank(c)
                up_product(pair[UP + BANK[c]], c % RING, hi, lo, ready, base)

            def up_tok(c, hi, lo, ready=None):
                up_bank(c)
                wh = w_hi[:, c % RING, :].rearrange("p (k n) -> p k n", k=KD)
                wl = w_lo[:, c % RING, :].rearrange("p (k n) -> p k n", k=KD)
                for t in range(2):
                    for k in range(KD):
                        if ready is not None and t == 0:
                            pe.wait_ge(ready, k + 1)
                        xs = slice(t * P, t * P + P)
                        mm = three(pair[UP + BANK[c]][:, t, :], hi[:, k, xs], lo[:, k, xs],
                                   wh[:, k, :], wl[:, k, :], k == 0, k == KD - 1)
                mm.then_inc(used, 1)

            def sums(n):
                pe.wait_ge(sq_done, n + 1)
                if n:
                    pe.wait_ge(std_done, n)
                pe.matmul(bank[SUM][:, 0:T], ones, sq_acc[:, 0, :], start=True, stop=False)
                pe.matmul(bank[SUM][:, 0:T], ones, sq_acc[:, 1, :], start=False, stop=True).then_inc(sum_done, 1)

            def sums_by_token(n):
                pe.wait_ge(sq_done, n + 1 if n < 9 else 12)
                pe.wait_ge(std_done, n)
                for t in range(2):
                    for i in range(2):
                        mm = pe.matmul(bank[SUM][:, t:t + 1], sq_acc[:, i, t * P:t * P + P], ones[:, 0:1],
                                       start=i == 0, stop=i == 1)
                mm.then_inc(sum_done, 1)

            def aux(n):
                if n:
                    pe.wait_ge(aux_free, n)

            def turn_rs(n, which, norm):
                pe.wait_ge(rs_done, made(norm))
                aux(n)
                pe.transpose(bank[AUX][:, 0:P], which[:, 0:P], ident)
                pe.transpose(bank[AUX][:, P:2 * P], which[:, P:T], ident).then_inc(aux_done, 1)

            def head_norm(n, j, mat, both):
                pe.wait_ge(hsq_done, j + 1)
                aux(n)
                if both:
                    pe.matmul(bank[AUX][:, 0:T], mat, h_sq[:, 0, :], start=True, stop=False)
                    mm = pe.matmul(bank[AUX][:, 0:T], mat, h_sq[:, 1, :], start=False, stop=True)
                else:
                    mm = pe.matmul(bank[AUX][:, :], mat, h_sq[:, :, :], start=True, stop=True)
                mm.then_inc(aux_done, 1)

            def logits(g, first, bias):
                qt, b = g // 4, g % 4
                nk = P * (qt + 1)
                if qt:
                    pe.wait_ge(lg_free, first + g - 3)
                for par_ in range(2):
                    dst = pair[ACC + b][:, par_, 0:nk]
                    mm = pe.matmul(dst, q_pad[:, par_, b, qt * P:qt * P + P], k_T[:, b, 0:nk],
                                   start=True, stop=not bias)
                    if bias:
                        mm = pe.matmul(dst, sel[:, 2 * b + par_, :], negc[:, 0:nk], start=False, stop=True)
                mm.then_inc(lg_done, 1)

            def down(c, place, hid_hi, hid_lo, first, done=None):
                pe.wait_ge(lo_done, c + 1)
                wh = w_hi[:, place, :].rearrange("p (k n) -> p k n", k=2)
                wl = w_lo[:, place, :].rearrange("p (k n) -> p k n", k=2)
                for m in range(KD):
                    for k in range(2):
                        ms = slice(m * P, m * P + P)
                        mm = three(pair[ACC + m // 2][:, m % 2, :], wh[:, k, ms], wl[:, k, ms], hid_hi[:, k, :],
                                   hid_lo[:, k, :], first and k == 0 and m % 2 == 0, done is not None and k == 1,
                                   group=False)
                    if done is not None and m % 2 and m < KD - 1:
                        mm.then_inc(done, 1)
                mm.then_inc(used, 1)

            def ffn_chunk(c, f, i, first, place):
                pe.wait_ge(ffn_lo_done, i + (f * PAIRS + 1))
                if f == 0 and first == "first":
                    pe.wait_ge(k_done, 4)
                hid_hi, hid_lo = (act_hi, act_lo) if first == "last" else (ffn_hi, ffn_lo)
                down(c, place, hid_hi, hid_lo, first == "first", down_done if first == "last" else None)

            def feed_forward(f, prep, norm, extra=None):
                base, free = FFN[f], UP_FFN[f]
                up(base, act_hi, act_lo, act_lo_done, 8 * prep)
                sums(norm)
                up(base + 1, act_hi, act_lo)
                if extra is not None:
                    extra()
                s = [(base + 2 + j) % RING for j in range(3)]

                def body(t, first):
                    c = base + 2 + t * 3
                    pe.wait_ge(lo_done, c + 1)
                    if first:
                        aux(A_BEFORE_FFN[f])
                    else:
                        pe.wait_ge(up_free, t * 2 + (free + 1))
                    up_product(pair[AUX if first else UP], s[0], act_hi, act_lo)
                    ffn_chunk(c + 1, f, t, first, s[1])
                    pe.wait_ge(lo_done, c + 3)
                    pe.wait_ge(up_free, t * 2 + (free + 2))
                    up_product(pair[UP + 1], s[2], act_hi, act_lo)

                body(0, "first")
                with pe.Fori(1, PAIRS - 2) as t:
                    body(t, "")
                last = base + FFN_CHUNKS - 1
                up(last - 3, act_hi, act_lo)
                up(last - 2, act_hi, act_lo)
                ffn_chunk(last - 1, f, PAIRS - 2, "", (last - 1) % RING)
                ffn_chunk(last, f, PAIRS - 1, "last", last % RING)

            pe.wait_ge(ident_landed, 16)
            pe.wait_ge(gain_landed, 16)
            pe.transpose(bank[SUM][:, 0:KD], first_rows[:, :], ident[0:KD, 0:KD]).then_inc(gain_turned, 1)
            pe.wait_ge(x_landed, 32)
            for b in range(4):
                for m in range(2):
                    for t in range(2):
                        d0 = (2 * b + m) * P
                        mm = pe.transpose(pair[ACC + b][:, m, t * P:t * P + P], natural[:, t, d0:d0 + P], ident)
                mm.then_inc(x_turned, 1)

            for _ in range(9):
                pe.matmul(bank[AUX][:, 0:P], ident, ident, start=True, stop=True)
            up(Q, act_hi, act_lo, act_lo_done, 0)
            pe.wait_ge(const_landed, 16)
            pe.wait_ge(gain_done, 1)
            sums(0)
            up(Q + 1, act_hi, act_lo)
            pe.wait_ge(par_landed, 16 * 24)
            pe.wait_ge(std_done, 1)
            pe.transpose(bank[SUM][:, 0:P], par_rows[:, :], ident).then_inc(par_turned, 1)
            up(K, act_hi, act_lo)
            turn_rs(A_TOKX, rs, 0)
            pe.wait_ge(par_ready, 2)
            pe.matmul(bank[SUM][:, 0:2], ones, lam_p, start=True, stop=True).then_inc(lam_done, 1)
            up(K + 1, act_hi, act_lo)
            pe.wait_ge(wf_lo_done, 1)
            aux(A_F)
            for k in range(KD):
                mm = three(bank[AUX][:, 0:T], wf_hi[:, k, :], wf_lo[:, k, :], act_hi[:, k, :], act_lo[:, k, :],
                           k == 0, k == KD - 1)
            mm.then_inc(aux_done, 1)
            up_tok(V, act_hi, act_lo)
            up_tok(V + 1, act_hi, act_lo)
            up(GB, act_hi, act_lo)
            up(GB + 1, act_hi, act_lo)
            pe.wait_ge(logf_done, 1)
            aux(A_LOGF)
            for t in range(2):
                mm = pe.transpose(bank[AUX][:, t * P:t * P + P], logf[:, t * P:t * P + P], ident)
            mm.then_inc(aux_done, 1)
            up(GC, act_hi, act_lo)
            aux(A_CUM)
            pe.matmul(bank[AUX][:, 0:8], tri[:, 0:P], logf_tok[:, 0, :], start=True, stop=True)
            pe.matmul(bank[AUX][:, 8:16], tri[:, P:T], logf_tok[:, 0, :], start=True, stop=False)
            pe.matmul(bank[AUX][:, 8:16], tri[:, 0:P], logf_tok[:, 1, :], start=False, stop=True)
            pe.matmul(bank[AUX][0:8, T:2 * T], logf_tok[:, 0, :], tri, start=True, stop=False)
            pe.matmul(bank[AUX][0:8, T + P:2 * T], logf_tok[:, 1, :], tri[:, 0:P],
                      start=False, stop=True).then_inc(aux_done, 1)
            up(GC + 1, act_hi, act_lo)
            up(HC, act_hi, act_lo)
            pe.wait_ge(aux_free, A_CUM + 1)
            pe.wait_ge(x_done, 4)
            pe.wait_ge(table_landed, 16)
            for g in range(4):
                logits(g, 0, True)
            up(HC + 1, act_hi, act_lo)
            for g in range(4, 8):
                logits(g, 0, True)
            up(GATE_C, act_hi, act_lo)
            up(GATE_C + 1, act_hi, act_lo)
            up(GATE_C + 2, act_hi, act_lo)

            def turn_probs(e, tile, src, maps, e0):
                pe.wait_ge(p_done, tile + 1)
                if e >= 4 + e0:
                    pe.wait_ge(tp_free, e - 3)
                for i in range(4):
                    mm = pe.transpose(quad[ACC + (e - e0) % 4][:, i, :], src(maps + i), ident)
                mm.then_inc(tp_done, 1)

            pe.wait_ge(lg_free, 8)
            for e in range(2):
                turn_probs(e, 0, lambda m: L0[:, m, :], 4 * e, 0)
            up(GATE_C + 3, act_hi, act_lo)
            for e in range(2, 6):
                k0 = P * ((e - 2) // 2)
                turn_probs(e, 1, lambda m: L1[:, m, k0:k0 + P], 4 * (e % 2), 0)
            up(GATE_A, act_hi, act_lo)
            up(GATE_A + 1, act_hi, act_lo)
            pe.wait_ge(tp_free, 6)
            for b in range(4):
                for par_ in range(2):
                    m = 2 * b + par_
                    pe.matmul(pair[ACC + b][:, par_, :], v_tok[:, 0, b * P:b * P + P], p_T0[:, m, :],
                              start=True, stop=False)
                    mm = pe.matmul(pair[ACC + b][:, par_, P:T], v_tok[:, 1, b * P:b * P + P], p_T1[:, m, :],
                                   start=False, stop=True)
                mm.then_inc(pv_done, 1)
            up(GATE_A + 2, act_hi, act_lo)
            up(GATE_A + 3, act_hi, act_lo)
            for j in range(4):
                c = BR0 + j
                pe.wait_ge(lo_done, c + 1)
                pe.wait_ge(mixlo_done, 6 if j == 0 else 8)
                if j >= 2:
                    pe.wait_ge(br_free, j - 1)
                wh = w_hi[:, c % RING, :].rearrange("p (k n) -> p k n", k=4)
                wl = w_lo[:, c % RING, :].rearrange("p (k n) -> p k n", k=4)
                for m in range(4):
                    for k in range(4):
                        ms, kk = slice(m * P, m * P + P), 4 * (j // 2) + k
                        mm = three(pair[ACC + 2 * (j % 2) + m // 2][:, m % 2, :], wh[:, k, ms], wl[:, k, ms],
                                   mix_hi[:, kk, :], mix_lo[:, kk, :], k == 0, k == 3)
                mm.then_inc(used, 1)
            up(OUT1, act_hi, act_lo, act_lo_done, 8)
            pe.wait_ge(mem_landed, 16)
            pe.wait_ge(br_free, 4)
            for b in range(4):
                for m in range(2):
                    for t in range(2):
                        d0 = (2 * b + m) * P
                        mm = pe.transpose(pair[ACC + b][:, m, t * P:t * P + P], mem_nat[:, t, d0:d0 + P], ident)
                mm.then_inc(memt_turned, 1)
            up(OUT1 + 1, act_hi, act_lo)
            up(OUT1 + 2, act_hi, act_lo)
            sums_by_token(1)
            up(OUT1 + 3, act_hi, act_lo)
            up_tok(MEMK, mix_hi, mix_lo, mem_lo_done)
            sums(2)
            for j in range(1, 4):
                up_tok(MEMK + j, mix_hi, mix_lo)

            def turn_keys():
                pe.wait_ge(memt_done, 4)
                for h in range(4):
                    pe.wait_ge(kscaled_done, h + 1)
                    for i in range(2):
                        for t in range(2):
                            n0 = (2 * h + i) * P
                            mm = pe.transpose(pair[ACC + h][:, i, t * P:t * P + P], raw_k[:, t, n0:n0 + P], ident)
                    mm.then_inc(k_turned, 1)

            feed_forward(0, 2, 3, turn_keys)
            up_tok(MEMV[0], mix_hi, mix_lo)
            sums(4)
            for j in range(1, 3):
                up_tok(MEMV[j], mix_hi, mix_lo)
            feed_forward(1, 3, 5)
            up_tok(MEMV[3], mix_hi, mix_lo)
            up(DQ, act_hi, act_lo, act_lo_done, 32)
            up(DQ + 1, act_hi, act_lo)
            sums(6)
            up(DK, act_hi, act_lo)
            head_norm(A_DIFF[0], H_DIFF, halves, False)
            turn_rs(A_TOK2, rs, 6)
            up(DK + 1, act_hi, act_lo)
            head_norm(A_DIFF[1], H_DIFF + 1, halves, False)
            up_tok(RV, act_hi, act_lo)
            head_norm(A_DIFF[2], H_DIFF + 2, halves, False)
            up_tok(RV + 1, act_hi, act_lo)
            head_norm(A_DIFF[3], H_DIFF + 3, halves, False)
            up(RQ, act_hi, act_lo)
            pe.wait_ge(hn_done, H_DIFF + 4)
            for g in range(4):
                logits(g, 8, False)
            up(RQ + 1, act_hi, act_lo)
            for g in range(4, 8):
                logits(g, 8, False)
            up(RK, act_hi, act_lo)
            up(RK + 1, act_hi, act_lo)
            up_tok(DV, act_hi, act_lo)
            pe.wait_ge(lg_free, 16)
            turn_probs(6, 2, lambda m: L0[:, 2 * m, :], 0, 6)
            for e in (7, 8):
                k0 = P * (e - 7)
                turn_probs(e, 3, lambda m: L1[:, 2 * m, k0:k0 + P], 0, 6)
            up_tok(DV + 1, act_hi, act_lo)
            wait_read(pe, RK + 1)
            pe.wait_ge(tp_free, 9)
            for h in range(4):
                pe.matmul(pair[ACC + h // 2][:, h % 2, :], rk_T[:, h, 0:P], rq_T[:, h, :], start=True, stop=True)
            for h in range(4):
                mm = pe.matmul(quad[ACC + 2][:, h, :], rk_T[:, h, P:T], rq_T[:, h, P:T], start=True, stop=True)
            mm.then_inc(sc_done, 1)
            up(RG, act_hi, act_lo)
            pe.wait_ge(at_done, 1)
            wait_read(pe, RV + 1)
            for b in range(2):
                for i in range(2):
                    h = 2 * b + i
                    pe.matmul(pair[ACC + b][:, i, :], rv_tok[0][:, h * P:h * P + P], a_T0[:, h, :],
                              start=True, stop=False)
                    mm = pe.matmul(pair[ACC + b][:, i, P:T], rv_tok[1][:, h * P:h * P + P], a_T1[:, h, :],
                                   start=False, stop=True)
            mm.then_inc(ro_done, 1)
            wait_read(pe, DV + 1)
            for b in range(2):
                for i in range(2):
                    h = 2 * b + i
                    pe.matmul(pair[ACC + 2 + b][:, i, :], v_tok[:, 0, h * P:h * P + P], p_T0[:, h, :],
                              start=True, stop=False)
                    mm = pe.matmul(pair[ACC + 2 + b][:, i, P:T], v_tok[:, 1, h * P:h * P + P], p_T1[:, h, :],
                                   start=False, stop=True)
            mm.then_inc(pv_done, 1)
            up(RG + 1, act_hi, act_lo)
            for b in range(2):
                pe.wait_ge(ro_sum, b + 1)
                aux(A_MEAN[b])
                pe.matmul(bank[AUX][:, :], ones, ret_o[:, 2 * b:2 * b + 2, :], start=True, stop=True).then_inc(aux_done, 1)
            for b in range(2):
                head_norm(A_VAR[b], H_VAR + b, ones, False)
            for b in range(2):
                head_norm(A_DOUT[b], H_DOUT + b, ones, False)
            up(OUT2, mix_hi, mix_lo, mixlo_done, 8)
            for j in range(1, 4):
                up(OUT2 + j, mix_hi, mix_lo)
            def query(j):
                up(MEMQ + j, act_hi, act_lo, None if j else act_lo_done, 40)

            def query_squares(h):
                pe.wait_ge(qsq_done, h + 1)
                if h % 2 == 0:
                    aux(A_QMEM[h // 2])
                for t in range(2):
                    for i in range(2):
                        mm = pe.matmul(bank[AUX][:, 2 * h + t:2 * h + t + 1], q_sq[h % 2][:, i, t * P:t * P + P],
                                       ones[:, 0:1], start=i == 0, stop=i == 1)
                if h % 2:
                    mm.then_inc(aux_done, 1)

            def mem_scores(h):
                wait_read(pe, MEMQ + h)
                for t in range(2):
                    for i in range(2):
                        mm = pe.matmul(pair[SCORES[h]][:, t, :], mem_T[:, 2 * h + i, t * P:t * P + P], k_mem[:, 2 * h + i, :],
                                       start=i == 0, stop=i == 1)
                mm.then_inc(lg_done, 1)

            def mem_turn(h):
                pe.wait_ge(p_done, 4 + h + 1)
                for k in range(2):
                    for t in range(2):
                        mm = pe.transpose(pair[TURN[h]][:, k, t * P:t * P + P],
                                          p_mem[:, 2 * h + t, k * P:k * P + P], ident)
                mm.then_inc(tp_done, 1)

            def mem_values(h):
                pe.wait_ge(tp_free, 9 + h + 1)
                if h:
                    aux(A_QMEM[1] + 1)
                if h == 2:
                    pe.wait_ge(mixlo_done, 20)
                for e in range(2):
                    for k in range(2):
                        d0 = (2 * h + e) * P
                        mm = pe.matmul(pair[VALUES[h]][:, e, :], v_mem[:, k, d0:d0 + P], p_memT[:, h % 2, k, :],
                                       start=k == 0, stop=k == 1)
                mm.then_inc(pv_done, 1)

            def mem_output(h):
                pe.wait_ge(mixlo_done, 16 + 2 * h + 2)
                s = slice(2 * h, 2 * h + 2)
                down(OUTM + h, (OUTM + h) % RING, mix_hi[:, s, :], mix_lo[:, s, :], h == 0, outm_done if h == 3 else None)

            query(0)
            query(1)
            sums_by_token(7)
            query_squares(0)
            mem_scores(0)
            query(2)
            query_squares(1)
            mem_scores(1)
            query(3)
            mem_turn(0)
            query_squares(2)
            mem_scores(2)
            mem_turn(1)
            mem_values(0)
            query_squares(3)
            mem_scores(3)
            mem_values(1)
            mem_output(0)
            mem_turn(2)
            mem_turn(3)
            mem_output(1)
            mem_values(2)
            mem_values(3)
            mem_output(2)
            mem_output(3)
            feed_forward(2, 6, 8)
            wait_read(pe, CHUNKS - 3)
            for j in range(2):
                for m in range(4):
                    pe.wait_ge(res_done, 4 * j + m + 1)
                    for t in range(2):
                        mm = pe.transpose(back[2 * j + t][:, m * P:m * P + P], m_T[:, 4 * j + m, t * P:t * P + P], ident)
                if j == 0:
                    mm.then_inc(res_turned, 1)
            mm.then_inc(res_turned, 1)
            sums_by_token(9)

        @block.scalar
        def _(act):
            copy, table_exp = ACT.Copy, ACT.Exp

            def hi(c, place=None):
                place = c % RING if place is None else place
                if isinstance(c, int):
                    act.wait_ge(landed[place], 16 * (c // RING + 1))
                    if c >= RING:
                        act.wait_ge(used, c - RING + 1)
                    act.activation(w_hi[:, place, :], stage[:, place, :], copy).then_inc(hi_done, 1)

            def hi_in_loop(t, first):
                place = first % RING
                act.wait_ge(landed[place], t * 16 + 16 * (first // RING + 1))
                act.wait_ge(used, t * 3 + (first - RING + 1))
                act.activation(w_hi[:, place, :], stage[:, place, :], copy).then_inc(hi_done, 1)

            def gained(gains, col, pairs_done, after, blocks=range(KD)):
                for b in blocks:
                    act.wait_ge(x_done, pairs_done + b // 2 + 1)
                    if b == 0 and after:
                        act.wait_ge(used, after)
                    act.activation(act_hi[:, b, :], x_T[:, b, :], copy,
                                   scale=gains[:, col + b:col + b + 1]).then_inc(act_hi_done, 1)

            def warm(function):
                act.activation(small[:, 6:7], eps, function)

            def deviation(n):
                act.wait_ge(sum_done, n + 1)
                if n:
                    act.wait_ge(rs_done, made(n - 1))
                act.activation(std[:, :], bank[SUM][:, 0:T], ACT.Sqrt, bias=eps, scale=1.0 / D).then_inc(std_done, 1)

            def head_deviation(n, j, width, both):
                act.wait_ge(aux_done, n + 1)
                if j:
                    act.wait_ge(hn_done, j)
                to, of = (h_std[:, 0, :], bank[AUX][:, 0:T]) if both else (h_std[:, :, :], pair[AUX])
                act.activation(to, of, ACT.Sqrt, bias=eps, scale=1.0 / width).then_inc(aux_free, 1)

            def result(c):
                act.wait_ge(used, c + 1)
                return pair[UP + BANK[c]]

            def scaled_tok(c, to, r):
                src = result(c)
                for t in range(2):
                    e = act.activation(to[t], src[:, t, :], copy, scale=r[:, t:t + 1])
                e.then_inc(up_free_act, 1)

            def keep_m(p, src):
                if p % 2:
                    act.activation((h_sq if p == 1 else h_std)[:, :, :], src, ACT.Square).then_inc(msq_done, 1)
                return act.activation(m_T[:, 2 * p:2 * p + 2, :], src, copy)

            def down_ready(f, p):
                if p < 3:
                    act.wait_ge(down_done, 3 * f + p + 1)
                else:
                    act.wait_ge(used, FFN[f] + FFN_CHUNKS)
                return pair[ACC + p]

            def exps(tile, L, nk):
                act.wait_ge(max_done, tile + 1)
                o = 8 * (tile % 2)
                for m in range(8):
                    e = act.activation(L[:, m, 0:nk], L[:, m, 0:nk], table_exp, bias=nmax[:, o + m:o + m + 1],
                                       accum_out=psum_[:, o + m:o + m + 1])
                e.then_inc(exp_done, 1)

            def feed_forward(f):
                base, u0 = FFN[f], UP_FFN[f]

                def hidden(t, i):
                    act.wait_ge(up_free, t * 2 + (u0 + 2 * i + 1))
                    act.activation(silu, g_s, ACT.Silu).then_inc(silu_done, 1)

                def hidden_hi(t, i, after, to):
                    act.wait_ge(h_done, t + (f * PAIRS + i + 1))
                    if after is not None:
                        act.wait_ge(used, after)
                    act.activation(to, h_T, copy).then_inc(ffn_hi_done, 1)

                hidden(0, 0)
                hidden_hi(0, 0, None if f == 0 else FFN[f - 1] + FFN_CHUNKS, ffn_hi[:, :, :])
                with act.Fori(0, PAIRS - 2) as t:
                    hi_in_loop(t, base + 4)
                    hidden(t, 1)
                    hi_in_loop(t, base + 5)
                    hi_in_loop(t, base + 6)
                    hidden_hi(t, 1, t * 3 + (base + 4), ffn_hi[:, :, :])
                last = base + FFN_CHUNKS - 1
                hi(last - 1)
                hidden(PAIRS - 2, 1)
                hi(last)
                hidden_hi(PAIRS - 2, 1, last - 1, act_hi[:, 0:2, :])
                if last + 1 < CHUNKS:
                    hi(last + 1)

            act.dma_start(ident, a["consts"][:, C_ID:C_ID + P]).then_inc(ident_landed, 16)
            act.dma_start(first_rows[:, :], a["norm_mix_pre"][0].rearrange("(k p) -> k p", p=P)).then_inc(gain_landed, 16)
            act.dma_start(const[:, P:C_END], a["consts"][:, P:C_END]).then_inc(const_landed, 16)
            act.dma_start(wf[:, :, :], a["w_in"][0].rearrange("(k p) n -> p k n", p=P)[:, :, 1536:1544]
                          ).then_inc(wf_landed, 16)
            act.dma_start(sel, a["consts"][:, C_END:C_END + 1024].rearrange("p (h m) -> p h m", h=8)
                          ).then_inc(table_landed, 16)
            hi(0)
            act.wait_ge(gain_done, 1)
            gained(first_gain, 0, 0, 0)
            hi(1)
            act.wait_ge(wf_landed, 16)
            act.wait_ge(zeroed, 10)
            act.activation(wf_hi[:, :, 0:8], wf[:, :, :], copy).then_inc(wf_hi_done, 1)
            warm(ACT.Sqrt)
            hi(2)
            deviation(0)
            hi(3)
            hi(4)
            act.wait_ge(lam_done, 1)
            act.activation(lam_e, bank[SUM][:, 0:2], table_exp).then_inc(lamx_done, 1)
            hi(5)
            hi(6)
            hi(7)
            act.wait_ge(aux_free, A_TOKX + 1)
            scaled_tok(V, [v_tok[:, t, 0:256] for t in range(2)], tok)
            act.wait_ge(fz_done, 1)
            act.activation(fe[0:8, :], fe[0:8, :], table_exp).then_inc(fexp_done, 1)
            act.wait_ge(fexp_done, 1)
            act.activation(fe[0:8, :], fe[0:8, :], ACT.Ln, bias=1.0).then_inc(fln_done, 1)
            hi(8)
            scaled_tok(V + 1, [v_tok[:, t, 256:512] for t in range(2)], tok)
            for c in range(9, 15):
                hi(c)
            exps(0, L0, P)
            hi(15)
            exps(1, L1, T)

            def conv_hi(b):
                act.wait_ge(y_done, b + 1)
                if b == 0:
                    act.wait_ge(aux_done, A_F + 1)
                act.activation(mix_hi[:, b, :], y_T[:, b % 2, :], copy).then_inc(mixhi_done, 1)

            def keep_probs(e, to):
                act.wait_ge(tp_done, e + 1)
                act.activation(to, quad[ACC + (e if e < 6 else e - 6) % 4], copy).then_inc(tp_free, 1)

            conv_hi(0)
            hi(16)
            for e in range(2):
                keep_probs(e, p_T0[:, 4 * e:4 * e + 4, 0:P])
            conv_hi(1)
            hi(17)
            conv_hi(2)
            hi(18)
            for e in range(2, 4):
                keep_probs(e, p_T0[:, 4 * e - 8:4 * e - 4, P:T])
            for e in range(4, 6):
                keep_probs(e, p_T1[:, 4 * e - 16:4 * e - 12, :])
            conv_hi(3)
            act.wait_ge(tp_done, 6)
            act.dma_start(mem_nat, a["mem_2"][0].rearrange("(t p) d -> p t d", p=P)).then_inc(mem_landed, 16)
            act.wait_ge(lg_done, 8)
            act.dma_start(table[:, :, :], a["consts"][:, C_END + 1024:C_END + 3072].rearrange("p (h m) -> p h m", h=8)
                          ).then_inc(table_landed, 16)
            hi(19)
            hi(20)
            for b in range(4):
                act.wait_ge(pv_done, b + 1)
                act.activation(mix_hi[0:64, 4 + b, :], pair[ACC + b][0:64, 0, :], copy)
                act.activation(mix_hi[64:P, 4 + b, :], pair[ACC + b][64:P, 1, :], copy).then_inc(mixhi_done, 1)
            hi(21)
            for i in range(8):
                if i == 4:
                    hi(22)
                wait_read(act, GATE_C + i)
                act.activation(gate[:, 2 * i:2 * i + 2, :], gate[:, 2 * i:2 * i + 2, :], ACT.Sigmoid).then_inc(gates_done, 1)
            hi(23)
            hi(24)
            act.wait_ge(used, GATE_A + 4)
            for i in range(4):
                if i == 2:
                    hi(25)
                act.wait_ge(merged, i + 1)
                act.activation(act_hi[:, 2 * i:2 * i + 2, :], gate_c[:, 2 * i:2 * i + 2, :], copy).then_inc(act_hi_done, 2)
            hi(26)

            def out1(p):
                keep_m(p, result(OUT1 + p)).then_inc(up_free_act, 1)

            def key_read(h):
                src, s = result(MEMK + h), slice(256 * h, 256 * h + 256)
                if h >= 2:
                    wait_read(act, MEMK + h - 2)
                for t in range(2):
                    act.activation(forget[:, 2 * (h % 2) + t, :], src[:, t, :], ACT.Square, accum_out=k_f[:, 2 * h + t:2 * h + t + 1])
                act.activation(raw_k[:, :, s], src, copy).then_inc(up_free_act, 1)

            out1(0)
            hi(27)
            for b in range(KD):
                act.wait_ge(memt_done, b // 2 + 1)
                if b == 0:
                    act.wait_ge(used, BR1 + 2)
                act.activation(mix_hi[:, b, :], mem_T[:, b, :], copy,
                               scale=par[:, G_MEMKV + b:G_MEMKV + b + 1]).then_inc(mem_hi_done, 1)
            out1(1)
            hi(28)
            act.wait_ge(sum_done, 2)
            act.wait_ge(rs_done, 1)
            act.activation(tok_std, bank[SUM][:, 0:2], ACT.Sqrt, bias=eps, scale=1.0 / D).then_inc(std_done, 1)
            out1(2)
            hi(29)
            out1(3)
            hi(30)
            key_read(0)
            deviation(2)
            hi(31)
            key_read(1)
            hi(32)
            gained(par, G_FFN_PRE, 4, OUT1 + 4, range(0, 4))
            key_read(2)
            gained(par, G_FFN_PRE, 4, OUT1 + 4, range(4, 8))
            hi(33)
            key_read(3)
            act.wait_ge(keps_done, 1)
            wait_read(act, MEMK + 3)
            for t in range(2):
                e = act.activation(k_f[:, t::2], k_f[:, t::2], ACT.Sqrt, bias=k_eps[:, t:t + 1], scale=1.0 / T)
            e.then_inc(kdev_done, 1)
            hi(34)
            deviation(3)
            warm(ACT.Silu)
            hi(35)
            for h in range(4):
                act.wait_ge(k_turned, h + 1)
                for i in range(2):
                    e = act.activation(k_mem[:, 2 * h + i, :], pair[ACC + h][:, i, :], copy,
                                       scale=par[:, MKN + i:MKN + i + 1])
                e.then_inc(k_done, 1)
            feed_forward(0)
            warm(ACT.Sqrt)
            for p in range(4):
                keep_m(p, down_ready(0, p)).then_inc(m_done, 1)
            hi(66)

            def memory_values(j):
                scaled_tok(MEMV[j], [v_mem[:, t, 256 * j:256 * j + 256] for t in range(2)], tok_mem)

            memory_values(0)
            hi(67)
            deviation(4)
            memory_values(1)
            hi(68)
            gained(par, G_FFN1, 8, FFN[0] + FFN_CHUNKS)
            memory_values(2)
            hi(69)
            hi(70)
            deviation(5)
            warm(ACT.Silu)
            hi(71)
            feed_forward(1)
            hi(102)
            warm(ACT.Sqrt)
            gained(par, G_MIX2, 12, FFN[1] + FFN_CHUNKS)
            memory_values(3)
            hi(103)
            hi(104)
            hi(105)
            deviation(6)
            hi(106)
            for j in range(4):
                hi(107 + j)
                head_deviation(A_DIFF[j], H_DIFF + j, 64, False)
                if j in (1, 2):
                    act.wait_ge(aux_free, A_TOK2 + 1)
                    scaled_tok(RV + j - 1, [r[:, 256 * j - 256:256 * j] for r in rv_tok], tok)
            hi(111)
            hi(112)
            exps(2, L0, P)
            hi(113)
            exps(3, L1, T)
            hi(114)
            hi(115)
            scaled_tok(DV, [v_tok[:, t, 0:256] for t in range(2)], tok)
            keep_probs(6, p_T0[:, 0:4, 0:P])
            keep_probs(7, p_T0[:, 0:4, P:T])
            keep_probs(8, p_T1[:, 0:4, :])
            hi(116)
            scaled_tok(DV + 1, [v_tok[:, t, 256:512] for t in range(2)], tok)
            hi(117)
            for i in range(2):
                wait_read(act, RG + i)
                act.activation(rg_s[:, 2 * i:2 * i + 2, :], rg_s[:, 2 * i:2 * i + 2, :], ACT.Silu).then_inc(rg_done, 1)
            for b in range(2):
                head_deviation(A_VAR[b], H_VAR + b, P, False)
            for b in range(2):
                head_deviation(A_DOUT[b], H_DOUT + b, P, False)
            for b in range(4):
                src = ret_o if b < 2 else diff_o
                act.wait_ge(y_done, 4 + b + 1)
                if b == 0:
                    act.wait_ge(used, MEMV[3] + 1)
                i = 2 * (b % 2)
                act.activation(mix_hi[:, 2 * b:2 * b + 2, :], src[:, i:i + 2, :], copy).then_inc(mixhi_done, 2)
            for c in range(118, 122):
                hi(c)
            gained(par, G_MEMQ, 16, RG + 2)

            def query(h):
                src = result(MEMQ + h)
                if h == 2:
                    act.wait_ge(aux_done, A_QMEM[0] + 1)
                act.activation(q_sq[h % 2][:, :, :], src, ACT.Square).then_inc(qsq_done, 1)
                for i in range(2):
                    e = act.activation(mem_T[:, 2 * h + i, :], src[:, i, :], copy, scale=par[:, MQN + i:MQN + i + 1])
                e.then_inc(up_free_act, 1)

            def query_deviation(b):
                act.wait_ge(std_done, 8)
                act.wait_ge(aux_done, A_QMEM[b] + 1)
                for t in range(2):
                    s = slice(4 * b + t, 4 * b + 4, 2)
                    e = act.activation(q_f[:, s], bank[AUX][:, s], ACT.Sqrt, bias=q_eps[:, t:t + 1])
                e.then_inc(aux_free, 1)

            def mem_exps(h):
                act.wait_ge(max_done, 4 + h + 1)
                for t in range(2):
                    i = 2 * h + t
                    e = act.activation(p_mem[:, i, :], pair[SCORES[h]][:, t, :], table_exp, bias=nmax[:, i:i + 1],
                                       scale=q_f[:, i:i + 1], accum_out=psum_[:, i:i + 1])
                e.then_inc(exp_done, 1)

            def mem_out(h):
                act.wait_ge(tp_done, 9 + h + 1)
                act.activation(p_memT[:, h % 2, :, :], pair[TURN[h]], copy).then_inc(tp_free, 1)

            def mem_hi(h):
                act.wait_ge(pv_done, 5 + h + 1)
                if h == 0:
                    act.wait_ge(used, OUT2 + 4)
                act.activation(mix_hi[:, 2 * h:2 * h + 2, :], pair[VALUES[h]], copy).then_inc(mixhi_done, 2)

            warm(ACT.Sqrt)
            hi(122)
            query(0)
            hi(123)
            query(1)
            hi(124)
            query_deviation(0)
            mem_exps(0)
            query(2)
            mem_exps(1)
            hi(125)
            mem_out(0)
            query(3)
            mem_out(1)
            query_deviation(1)
            mem_hi(0)
            mem_hi(1)
            mem_exps(2)
            mem_exps(3)
            hi(126)
            mem_out(2)
            mem_out(3)
            hi(127)
            mem_hi(2)
            mem_hi(3)
            hi(128)
            gained(par, G_FFN2, 20, MEMQ + 4)
            hi(129)
            hi(130)
            deviation(8)
            warm(ACT.Silu)
            hi(131)
            feed_forward(2)
            warm(ACT.Sqrt)
            for b in range(KD):
                act.wait_ge(x_done, 24 + b // 2 + 1)
                if b in (4, 6):
                    act.activation((h_std if b == 4 else h_sq)[:, :, :], x_T[:, b:b + 2, :], ACT.Square
                                   ).then_inc(qsq_done, 1)
                act.activation(m_T[:, b, :], x_T[:, b, :], copy, scale=par[:, G_OUT + b:G_OUT + b + 1]).then_inc(res_done, 1)
            act.wait_ge(sum_done, 10)
            act.activation(tok_std, bank[SUM][:, 0:2], ACT.Sqrt, bias=eps, scale=1.0 / D).then_inc(std_done, 1)
            act.wait_ge(rs_done, made(9))
            for j in range(2):
                act.wait_ge(res_turned, j + 1)
                act.activation(natural[:, 0, 512 * j:512 * j + 512], back[2 * j][:, :], copy, scale=tok[:, 0:1]
                               ).then_inc(nat_done[0], 1)
            for j in range(2):
                act.wait_ge(nat_done[1], j + 1)
                store(act, 1, j)

        @block.vector
        def _(dve):
            steps = [0]

            def then(ins):
                steps[0] += 1
                ins.then_inc(dve_step, 1)
                dve.wait_ge(dve_step, steps[0])

            def over(r, n=2, p=slice(0, P)):
                return r[p, None, :].to_broadcast([p.stop - p.start, n, T])

            def lo(c):
                place = c % RING
                dve.wait_ge(hi_done, c + 1)
                dve.tensor_tensor(w_lo[:, place, :], stage[:, place, :], w_hi[:, place, :].bitcast(F32),
                                  ALU.subtract).then_inc(lo_done, 1)

            def lo_in_loop(t, first):
                place = first % RING
                dve.wait_ge(hi_done, t * 3 + (first + 1))
                dve.tensor_tensor(w_lo[:, place, :], stage[:, place, :], w_hi[:, place, :].bitcast(F32),
                                  ALU.subtract).then_inc(lo_done, 1)

            def gained(gains, col, prep, blocks=range(KD)):
                for b in blocks:
                    dve.wait_ge(act_hi_done, 8 * prep + b + 1)
                    dve.scalar_tensor_tensor(act_lo[:, b, :], x_T[:, b, :], gains[:, col + b:col + b + 1],
                                             act_hi[:, b, :].bitcast(F32), ALU.mult, ALU.subtract
                                             ).then_inc(act_lo_done, 1)

            def factor(n, to):
                dve.wait_ge(std_done, n + 1)
                dve.reciprocal(to[:, :], std[:, :]).then_inc(rs_done, 1)
                dve.wait_ge(rs_done, made(n))

            def result(c):
                dve.wait_ge(used, c + 1)
                return pair[UP + BANK[c]]

            def scaled(c, to, r):
                dve.tensor_tensor(to, result(c), over(r), ALU.mult).then_inc(up_free, 1)

            def keep_tok(n, to):
                dve.wait_ge(aux_done, n + 1)
                dve.tensor_copy(to[:, :], bank[AUX][:, 0:2 * P:P]).then_inc(aux_free, 1)
                dve.wait_ge(aux_free, n + 1)

            def head_norm(n, j, both, apply):
                dve.wait_ge(aux_free, n + 1)
                r = h_std[:, 0, :] if both else h_std[:, :, :]
                then(dve.reciprocal(r, r))
                apply(r).then_inc(hn_done, 1)

            def softmax_max(tile, L, nk):
                o = 8 * (tile % 2)
                dve.wait_ge(dve_step, steps[0])
                dve.tensor_reduce(nmax[:, o:o + 8], L[:, :, 0:nk], AX, ALU.max, negate=True).then_inc(max_done, 1)

            def inverse_sums(tile):
                o = 8 * (tile % 2)
                dve.wait_ge(exp_done, tile + 1)
                then(dve.reciprocal(prec[:, o:o + 8], psum_[:, o:o + 8]))
                return o

            def read_scores(g, first):
                qt, b = g // 4, g % 4
                nk = P * (qt + 1)
                L = L1 if qt else L0
                dve.wait_ge(lg_done, first + g + 1)
                for i in range(2):
                    m = 2 * b + i
                    src = pair[ACC + b][:, i, 0:nk]
                    if first == 0:
                        ins = dve.scalar_tensor_tensor(L[:, m, :], src, c_tok[:, qt, m:m + 1],
                                                       causal[:, T - nk:T], ALU.add, ALU.add)
                    else:
                        ins = dve.scalar_tensor_tensor(L[:, m, :], src, 0.125, alibi[:, b, T - nk:T],
                                                       ALU.mult, ALU.add)
                ins.then_inc(lg_free, 1)
                dve.wait_ge(lg_free, first + g + 1)

            def feed_forward(f):
                base, u0 = FFN[f], UP_FFN[f]

                def gate_part(t, i, src=pair[UP]):
                    dve.wait_ge(used, t * 3 + (base + (2 + 3 * (i - 1) if i else 0) + 1))
                    dve.tensor_tensor(g_s, src, over(rs), ALU.mult).then_inc(up_free, 1)

                def up_part(t, i, chunk, to=ffn_lo[:, :, :], of=ffn_hi[:, :, :]):
                    n = f * PAIRS + i + 1
                    dve.wait_ge(used, t * 3 + (chunk + 1))
                    dve.tensor_tensor(u_s, pair[UP + 1], over(rs), ALU.mult).then_inc(up_free, 1)
                    dve.wait_ge(up_free, t * 2 + (u0 + 2 * i + 2))
                    dve.wait_ge(silu_done, t + n)
                    dve.tensor_tensor(h_T, u_s, silu, ALU.mult).then_inc(h_done, 1)
                    dve.wait_ge(ffn_hi_done, t + n)
                    dve.tensor_tensor(to, h_T, of.bitcast(F32), ALU.subtract).then_inc(ffn_lo_done, 1)

                gate_part(0, 0)
                up_part(0, 0, base + 1)

                def body(t, src):
                    lo_in_loop(t, base + 4)
                    gate_part(t, 1, src)
                    lo_in_loop(t, base + 5)
                    lo_in_loop(t, base + 6)
                    up_part(t, 1, base + 4)

                body(0, pair[AUX])
                with dve.Fori(1, PAIRS - 2) as t:
                    body(t, pair[UP])
                last = base + FFN_CHUNKS - 1
                lo(last - 1)
                gate_part(PAIRS - 2, 1)
                lo(last)
                up_part(PAIRS - 2, 1, base + 3, act_lo[:, 0:2, :], act_hi[:, 0:2, :])
                if last + 1 < CHUNKS:
                    lo(last + 1)

            def down_ready(f, p):
                if p < 3:
                    dve.wait_ge(down_done, 3 * f + p + 1)
                else:
                    dve.wait_ge(used, FFN[f] + FFN_CHUNKS)
                return pair[ACC + p]

            def post_pair(p, col, n, count):
                dve.wait_ge(post_done, (4 if n == 4 else 0) + p + 1)
                for b in (2 * p, 2 * p + 1):
                    ins = dve.scalar_tensor_tensor(x_T[:, b, :], m_T[:, b, :], par[:, col + b:col + b + 1], x_T[:, b, :],
                                                   ALU.mult, ALU.add)
                ins.then_inc(x_done, 1)
                dve.wait_ge(x_done, count + p + 1)

            def post_and_gained(col, n, count, next_col, prep):
                for p in range(4):
                    post_pair(p, col, n, count)
                    if p:
                        gained(par, next_col, prep, range(2 * p - 2, 2 * p))
                gained(par, next_col, prep, range(6, 8))

            dve.wait_ge(gain_turned, 1)
            dve.tensor_copy(first_gain[:, :], bank[SUM][:, 0:KD]).then_inc(gain_done, 1)
            for b in range(4):
                dve.wait_ge(x_turned, b + 1)
                dve.tensor_copy(x_T[:, 2 * b:2 * b + 2, :], pair[ACC + b]).then_inc(x_done, 1)
            dve.wait_ge(x_done, 4)
            lo(0)
            gained(first_gain, 0, 0)
            lo(1)
            dve.wait_ge(wf_hi_done, 1)
            dve.wait_ge(zeroed, 10)
            dve.tensor_tensor(wf_lo[:, :, 0:8], wf[:, :, :], wf_hi[:, :, 0:8].bitcast(F32), ALU.subtract
                              ).then_inc(wf_lo_done, 1)
            lo(2)
            factor(0, rs)

            def query(c):
                src, b = result(c), 2 * (c - Q)
                dve.scalar_tensor_tensor(q_pad[0:64, 0, b:b + 2, :], src[0:64, :, :], 0.125, over(rs, p=slice(0, 64)),
                                         ALU.mult, ALU.mult)
                dve.scalar_tensor_tensor(q_pad[64:P, 1, b:b + 2, :], src[64:P, :, :], 0.125, over(rs, p=slice(64, P)),
                                         ALU.mult, ALU.mult).then_inc(up_free, 1)

            query(Q)
            lo(3)
            query(Q + 1)
            dve.wait_ge(par_turned, 1)
            dve.tensor_copy(par[:, :], bank[SUM][:, 0:P]).then_inc(par_ready, 1)
            dve.wait_ge(par_ready, 1)
            dve.tensor_tensor(lam_p[0:64, 0:1], par[0:64, LAMQ:LAMQ + 1], par[0:64, LAMK:LAMK + 1], ALU.mult)
            dve.tensor_tensor(lam_p[64:P, 1:2], par[64:P, LAMQ:LAMQ + 1], par[64:P, LAMK:LAMK + 1], ALU.mult
                              ).then_inc(par_ready, 1)
            lo(4)
            scaled(K, k_T[:, 0:2, :], rs)
            lo(5)
            dve.wait_ge(lamx_done, 1)
            then(dve.tensor_tensor(lam, lam_e[:, 1:2], lam_e[:, 0:1], ALU.subtract))
            then(dve.tensor_scalar(lam, lam, -LAM_INIT, None, ALU.add))
            then(dve.tensor_scalar(par[:, DIFN:DIFN + 1], par[:, DIFN:DIFN + 1], 1.0 - LAM_INIT, None, ALU.mult))
            keep_tok(A_TOKX, tok)
            scaled(K + 1, k_T[:, 2:4, :], rs)
            lo(6)
            dve.wait_ge(aux_done, A_F + 1)
            dve.tensor_tensor(fz[0:8, :], bank[AUX][0:8, 0:T], rs[0:8, :], ALU.mult).then_inc(aux_free, 1)
            dve.wait_ge(aux_free, A_F + 1)
            then(dve.tensor_scalar(fz[0:8, :], fz[0:8, :], par[0:8, BF:BF + 1], None, ALU.add))
            dve.scalar_tensor_tensor(fe[0:8, :], fz[0:8, :], -1.0, fz[0:8, :], ALU.mult, ALU.min).then_inc(fz_done, 1)
            lo(7)
            lo(8)
            dve.wait_ge(fln_done, 1)
            dve.scalar_tensor_tensor(logf[0:8, :], fz[0:8, :], 0.0, fe[0:8, :], ALU.min, ALU.subtract).then_inc(logf_done, 1)
            scaled(GB, gb_T[:, 0:2, :], rs)
            lo(9)
            scaled(GB + 1, gb_T[:, 2:4, :], rs)
            lo(10)
            dve.wait_ge(aux_done, A_LOGF + 1)
            dve.tensor_copy(logf_tok[:, :, :], pair[AUX].rearrange("p a t -> p (a t)")[:, 0:2 * P].rearrange(
                "p (t q) -> p t q", t=2)[:, :, 0:8]).then_inc(aux_free, 1)
            scaled(GC, z_T[:, 0:2, 2:T + 2], rs)
            lo(11)
            dve.wait_ge(aux_done, A_CUM + 1)
            dve.tensor_copy(c_tok[:, :, :].rearrange("p a b -> p (a b)"), bank[AUX][:, 0:16])
            dve.tensor_scalar(negc[0:8, :], bank[AUX][0:8, T:2 * T], -1.0, None, ALU.mult).then_inc(aux_free, 1)
            dve.wait_ge(aux_free, A_CUM + 1)
            scaled(GC + 1, z_T[:, 2:4, 2:T + 2], rs)
            lo(12)
            scaled(HC, hc_T[:, 0, :, :], rs)
            lo(13)
            for g in range(4):
                read_scores(g, 0)
            softmax_max(0, L0, P)
            scaled(HC + 1, hc_T[:, 1, :, :], rs)
            lo(14)
            for g in range(4, 8):
                read_scores(g, 0)
            softmax_max(1, L1, T)
            scaled(GATE_C, gate[:, 0:2, :], rs)
            lo(15)

            def normal(tile, L, nk):
                o = inverse_sums(tile)
                dve.tensor_tensor(L[:, :, 0:nk], L[:, :, 0:nk], prec[:, o:o + 8, None].to_broadcast([P, 8, nk]), ALU.mult
                                  ).then_inc(p_done, 1)

            def conv(b):
                dve.wait_ge(z_done, b // 2 + 1)
                if b >= 2:
                    dve.wait_ge(mixhi_done, b - 1)
                y = y_T[:, b % 2, :]
                for j in range(3):
                    w = par[:, CONV + 4 * j + b:CONV + 4 * j + b + 1]
                    if j == 0:
                        then(dve.tensor_scalar(y, z_T[:, b, 0:T], w, None, ALU.mult))
                    else:
                        then(dve.scalar_tensor_tensor(y, z_T[:, b, j:j + T], w, y, ALU.mult, ALU.add))
                dve.tensor_tensor(y, y, gb_T[:, b, :], ALU.mult).then_inc(y_done, 1)

            def conv_lo(b):
                dve.wait_ge(mixhi_done, b + 1)
                dve.tensor_tensor(mix_lo[:, b, :], y_T[:, b % 2, :], mix_hi[:, b, :].bitcast(F32), ALU.subtract
                                  ).then_inc(mixlo_done, 1)

            scaled(GATE_C + 1, gate[:, 2:4, :], rs)
            normal(0, L0, P)
            conv(0)
            lo(16)
            scaled(GATE_C + 2, gate[:, 4:6, :], rs)
            normal(1, L1, T)
            conv_lo(0)
            conv(1)
            lo(17)
            scaled(GATE_C + 3, gate[:, 6:8, :], rs)
            conv_lo(1)
            conv(2)
            lo(18)
            scaled(GATE_A, gate[:, 8:10, :], rs)
            conv_lo(2)
            conv(3)
            lo(19)
            scaled(GATE_A + 1, gate[:, 10:12, :], rs)
            conv_lo(3)
            lo(20)
            scaled(GATE_A + 2, gate[:, 12:14, :], rs)
            for b in range(4):
                dve.wait_ge(mixhi_done, 4 + b + 1)
                for p, i in ((slice(0, 64), 0), (slice(64, P), 1)):
                    ins = dve.tensor_tensor(mix_lo[p, 4 + b, :], pair[ACC + b][p, i, :], mix_hi[p, 4 + b, :].bitcast(F32),
                                            ALU.subtract)
                ins.then_inc(mixlo_done, 1)
            lo(21)
            scaled(GATE_A + 3, gate[:, 14:16, :], rs)
            lo(22)
            for j in range(2):
                dve.wait_ge(used, BR0 + j + 1)
                dve.wait_ge(gates_done, 2 * j + 2)
                for i in range(2):
                    g = gate_c[:, 4 * j + 2 * i:4 * j + 2 * i + 2, :]
                    ins = dve.tensor_tensor(g, pair[ACC + 2 * j + i], g, ALU.mult)
                ins.then_inc(br_free, 1)
                lo(23 + j)
            for j in range(2):
                dve.wait_ge(used, BR1 + j + 1)
                dve.wait_ge(gates_done, 4 + 2 * j + 2)
                for i in range(2):
                    g = gate_a[:, 4 * j + 2 * i:4 * j + 2 * i + 2, :]
                    ins = dve.tensor_tensor(g, pair[ACC + 2 * j + i], g, ALU.mult)
                ins.then_inc(br_free, 1)
                dve.wait_ge(br_free, 3 + j)
                for i in range(2):
                    s = slice(4 * j + 2 * i, 4 * j + 2 * i + 2)
                    dve.tensor_tensor(gate_c[:, s, :], gate_c[:, s, :], gate_a[:, s, :], ALU.add).then_inc(merged, 1)
                for i in range(2):
                    s = slice(4 * j + 2 * i, 4 * j + 2 * i + 2)
                    dve.wait_ge(act_hi_done, 8 + 4 * j + 2 * i + 2)
                    dve.tensor_tensor(act_lo[:, s, :], gate_c[:, s, :], act_hi[:, s, :].bitcast(F32), ALU.subtract
                                      ).then_inc(act_lo_done, 2)
            lo(25)
            lo(26)

            for b in range(4):
                dve.wait_ge(memt_turned, b + 1)
                dve.tensor_copy(mem_T[:, 2 * b:2 * b + 2, :], pair[ACC + b]).then_inc(memt_done, 1)
            lo(27)
            dve.wait_ge(memt_done, 4)
            for b in range(KD):
                dve.wait_ge(mem_hi_done, b + 1)
                dve.scalar_tensor_tensor(mix_lo[:, b, :], mem_T[:, b, :], par[:, G_MEMKV + b:G_MEMKV + b + 1],
                                         mix_hi[:, b, :].bitcast(F32), ALU.mult, ALU.subtract).then_inc(mem_lo_done, 1)
            lo(28)
            dve.wait_ge(std_done, 2)
            dve.scalar_tensor_tensor(k_eps, tok_std, EPS, tok_std, ALU.mult, ALU.mult).then_inc(keps_done, 1)
            dve.reciprocal(tok_mem[:, :], tok_std).then_inc(rs_done, 1)
            lo(29)
            lo(30)
            factor(2, rs_post)
            lo(31)
            lo(32)
            post_and_gained(G_MIX_POST, 2, 4, G_FFN_PRE, 2)
            lo(33)
            dve.wait_ge(kdev_done, 1)
            dve.reciprocal(k_f, k_f).then_inc(kf_done, 1)
            lo(34)
            factor(3, rs)
            lo(35)
            feed_forward(0)

            lo(66)
            lo(67)
            factor(4, rs_post)
            lo(68)
            post_and_gained(G_FFN_POST, 4, 8, G_FFN1, 3)
            lo(69)
            lo(70)
            factor(5, rs)
            lo(71)
            feed_forward(1)

            def half_residual(f, count):
                for p in range(4):
                    src = down_ready(f, p)
                    xs = x_T[:, 2 * p:2 * p + 2, :]
                    dve.scalar_tensor_tensor(xs, src, 0.5, xs, ALU.mult, ALU.add).then_inc(x_done, 1)
                    dve.wait_ge(x_done, count + p + 1)

            lo(102)
            half_residual(1, 12)
            gained(par, G_MIX2, 4)
            lo(103)
            lo(104)
            lo(105)
            factor(6, rs)

            def diff_raw(j):
                scaled(DQ + j, raw[:, 2 * j:2 * j + 2, :], rs)

            def diff_qk(j):
                def apply(r):
                    s = slice(2 * (j % 2), 2 * (j % 2) + 2)
                    src = raw[:, 2 * j:2 * j + 2, :]
                    if j >= 2:
                        return dve.scalar_tensor_tensor(k_T[:, s, :], src, par[:, DKN:DKN + 1], r, ALU.mult, ALU.mult)
                    for p, i in ((slice(0, 64), 0), (slice(64, P), 1)):
                        ins = dve.scalar_tensor_tensor(q_pad[p, i, s, :], src[p], par[p, DQN:DQN + 1], r[p],
                                                       ALU.mult, ALU.mult)
                    return ins
                head_norm(A_DIFF[j], H_DIFF + j, False, apply)

            diff_raw(0)
            diff_raw(1)
            lo(106)
            dve.wait_ge(zeroed, 11)
            lo(107)
            diff_qk(0)
            keep_tok(A_TOK2, tok)
            diff_raw(2)
            diff_raw(3)
            lo(108)
            diff_qk(1)
            lo(109)
            diff_qk(2)
            lo(110)
            diff_qk(3)
            scaled(RQ, rq_T[:, 0:2, :], rs)
            lo(111)
            dve.wait_ge(table_landed, 32)
            for g in range(4):
                read_scores(g, 8)
            softmax_max(2, L0, P)
            scaled(RQ + 1, rq_T[:, 2:4, :], rs)
            lo(112)
            for g in range(4, 8):
                read_scores(g, 8)
            softmax_max(3, L1, T)
            scaled(RK, rk_T[:, 0:2, :], rs)
            lo(113)

            def difference(tile, L, nk):
                o = inverse_sums(tile)
                odd = prec[:, o + 1:o + 8:2]
                then(dve.tensor_scalar(odd, odd, lam, None, ALU.mult))
                then(dve.tensor_tensor(L[:, :, 0:nk], L[:, :, 0:nk], prec[:, o:o + 8, None].to_broadcast([P, 8, nk]), ALU.mult))
                dve.tensor_tensor(L[:, 0:8:2, 0:nk], L[:, 0:8:2, 0:nk], L[:, 1:8:2, 0:nk], ALU.add).then_inc(p_done, 1)

            difference(2, L0, P)
            scaled(RK + 1, rk_T[:, 2:4, :], rs)
            lo(114)
            difference(3, L1, T)
            lo(115)
            lo(116)
            dve.wait_ge(sc_done, 1)
            for b in range(2):
                dve.tensor_tensor(a_T0[:, 2 * b:2 * b + 2, :], pair[ACC + b], decay[:, 2 * b:2 * b + 2, :], ALU.mult)
            dve.tensor_tensor(a_T1, quad[ACC + 2], decay[:, :, 0:P], ALU.mult).then_inc(at_done, 1)
            scaled(RG, rg_s[:, 0:2, :], rs)
            lo(117)
            dve.wait_ge(ro_done, 1)
            for b in range(2):
                dve.tensor_copy(ret_o[:, 2 * b:2 * b + 2, :], pair[ACC + b]).then_inc(ro_sum, 1)
            dve.wait_ge(pv_done, 5)
            for b in range(2):
                dve.tensor_copy(diff_o[:, 2 * b:2 * b + 2, :], pair[ACC + 2 + b]).then_inc(diff_done, 1)
            scaled(RG + 1, rg_s[:, 2:4, :], rs)
            dve.wait_ge(ro_sum, 2)
            for b in range(2):
                o = ret_o[:, 2 * b:2 * b + 2, :]
                dve.wait_ge(aux_done, A_MEAN[b] + 1)
                dve.scalar_tensor_tensor(o, pair[AUX], -1.0 / P, o, ALU.mult, ALU.add).then_inc(aux_free, 1)
                dve.wait_ge(aux_free, A_MEAN[b] + 1)
            for b in range(2):
                o = ret_o[:, 2 * b:2 * b + 2, :]
                head_norm(A_VAR[b], H_VAR + b, False, lambda r: dve.scalar_tensor_tensor(
                    o, o, par[:, RETN:RETN + 1], r, ALU.mult, ALU.mult))
                dve.wait_ge(hn_done, H_VAR + b + 1)
                dve.wait_ge(rg_done, b + 1)
                dve.tensor_tensor(o, o, rg_s[:, 2 * b:2 * b + 2, :], ALU.mult).then_inc(y_done, 1)
            dve.wait_ge(diff_done, 2)
            for b in range(2):
                o = diff_o[:, 2 * b:2 * b + 2, :]
                head_norm(A_DOUT[b], H_DOUT + b, False, lambda r: dve.scalar_tensor_tensor(
                    o, o, par[:, DIFN:DIFN + 1], r, ALU.mult, ALU.mult))
                dve.wait_ge(hn_done, H_DOUT + b + 1)
                dve.engine_nop().then_inc(y_done, 1)
            dve.wait_ge(y_done, 8)
            for b in range(4):
                i = 2 * (b % 2)
                src = (ret_o if b < 2 else diff_o)[:, i:i + 2, :]
                dve.wait_ge(mixhi_done, 8 + 2 * b + 2)
                dve.tensor_tensor(mix_lo[:, 2 * b:2 * b + 2, :], src, mix_hi[:, 2 * b:2 * b + 2, :].bitcast(F32), ALU.subtract
                                  ).then_inc(mixlo_done, 2)

            def residual(c, p, count):
                xs = x_T[:, 2 * p:2 * p + 2, :]
                dve.tensor_tensor(xs, result(c), xs, ALU.add).then_inc(x_done, 1)
                dve.wait_ge(x_done, count + p + 1)
                dve.sem_inc(up_free, 1)

            for j in range(4):
                lo(118 + j)
                residual(OUT2 + j, j, 16)
            gained(par, G_MEMQ, 5)

            def query_factor(b):
                dve.wait_ge(aux_free, A_QMEM[b] + 1)
                dve.reciprocal(q_f[:, 4 * b:4 * b + 4], q_f[:, 4 * b:4 * b + 4]).then_inc(qf_done, 1)

            def mem_max(h):
                dve.wait_ge(lg_done, 16 + h + 1)
                s = slice(2 * h, 2 * h + 2)
                then(dve.tensor_reduce(nmax[:, s], pair[SCORES[h]], AX, ALU.max, negate=True))
                dve.wait_ge(qf_done, h // 2 + 1)
                dve.tensor_tensor(nmax[:, s], nmax[:, s], q_f[:, s], ALU.mult).then_inc(max_done, 1)

            def mem_normal(h):
                dve.wait_ge(exp_done, 4 + h + 1)
                s = slice(2 * h, 2 * h + 2)
                then(dve.reciprocal(prec[:, s], psum_[:, s]))
                dve.tensor_tensor(p_mem[:, s, :], p_mem[:, s, :], prec[:, s, None].to_broadcast([P, 2, T]), ALU.mult
                                  ).then_inc(p_done, 1)

            def mem_lo(h):
                s = slice(2 * h, 2 * h + 2)
                dve.wait_ge(mixhi_done, 16 + 2 * h + 2)
                dve.tensor_tensor(mix_lo[:, s, :], pair[VALUES[h]], mix_hi[:, s, :].bitcast(F32), ALU.subtract
                                  ).then_inc(mixlo_done, 2)

            lo(122)
            lo(123)
            dve.wait_ge(sum_done, 8)
            dve.tensor_scalar(q_eps, bank[SUM][:, 0:2], T * EPS / D, T * EPS * EPS, ALU.mult, ALU.add).then_inc(std_done, 1)
            lo(124)
            query_factor(0)
            mem_max(0)
            mem_max(1)
            mem_normal(0)
            lo(125)
            mem_normal(1)
            query_factor(1)
            mem_lo(0)
            mem_max(2)
            mem_lo(1)
            mem_max(3)
            mem_normal(2)
            mem_normal(3)
            lo(126)
            lo(127)
            mem_lo(2)
            mem_lo(3)
            lo(128)
            for p in range(4):
                if p < 3:
                    dve.wait_ge(outm_done, p + 1)
                else:
                    dve.wait_ge(used, OUTM + 4)
                xs = x_T[:, 2 * p:2 * p + 2, :]
                dve.tensor_tensor(xs, pair[ACC + p], xs, ALU.add).then_inc(x_done, 1)
            dve.wait_ge(x_done, 24)
            gained(par, G_FFN2, 6)
            lo(129)
            lo(130)
            factor(8, rs)
            lo(131)
            feed_forward(2)
            half_residual(2, 24)
            for i, squares in enumerate((h_std, h_sq)):
                dve.wait_ge(sq_done, 10 + i)
                dve.wait_ge(qsq_done, 5 + i)
                dve.tensor_tensor(sq_acc[:, :, :], sq_acc[:, :, :], squares[:, :, :], ALU.add).then_inc(sq_done, 1)
            dve.wait_ge(std_done, 10)
            dve.reciprocal(tok[:, :], tok_std).then_inc(rs_done, 1)
            dve.wait_ge(rs_done, made(9))
            for j in range(2):
                dve.wait_ge(res_turned, j + 1)
                dve.tensor_scalar(natural[:, 1, 512 * j:512 * j + 512], back[2 * j + 1][:, :], tok[:, 1:2], None, ALU.mult
                                  ).then_inc(nat_done[1], 1)

        @block.gpsimd
        def _(pool):
            steps = [0]

            def then(ins):
                steps[0] += 1
                ins.then_inc(pool_step, 1)
                pool.wait_ge(pool_step, steps[0])

            def squares(n, src, ready, base, pairs=4):
                for p in range(pairs):
                    pool.wait_ge(ready, base + p + 1)
                    if p == 0 and n:
                        pool.wait_ge(sum_done, n)
                    s = src[:, 2 * p:2 * p + 2, :]
                    if p == 0:
                        then(pool.tensor_tensor(sq_acc[:, :, :], s, s, ALU.mult))
                        continue
                    then(pool.tensor_tensor(sq_tmp[:, :, :], s, s, ALU.mult))
                    ins = pool.tensor_tensor(sq_acc[:, :, :], sq_acc[:, :, :], sq_tmp[:, :, :], ALU.add)
                    if p < pairs - 1:
                        then(ins)
                    else:
                        ins.then_inc(sq_done, 1)

            def head_squares(src, before):
                if before is not None:
                    pool.wait_ge(aux_done, before + 1)
                pool.tensor_tensor(h_sq[:, :, :], src, src, ALU.mult).then_inc(hsq_done, 1)

            pool.memset(par_rows[:, :], 0.0).then_inc(zeroed, 1)
            pool.memset(small[:, :], 0.0).then_inc(zeroed, 1)
            pool.memset(wf_hi.bitcast(F32), 0.0).then_inc(zeroed, 1)
            pool.memset(wf_lo.bitcast(F32), 0.0).then_inc(zeroed, 1)
            pool.memset(q_pad[:, :, :, :], 0.0).then_inc(zeroed, 1)
            pool.memset(logf[:, :], 0.0).then_inc(zeroed, 1)
            pool.memset(negc[:, :], 0.0).then_inc(zeroed, 1)
            pool.memset(z_T[:, :, 0:2], 0.0).then_inc(zeroed, 1)
            pool.memset(eps_t[:, :], EPS).then_inc(zeroed, 1)
            pool.memset(fe[:, :], 0.0).then_inc(zeroed, 1)
            squares(0, x_T, x_done, 0)
            for j in range(2):
                wait_read(pool, HC + j)
                zs = z_T[:, 2 * j:2 * j + 2, 2:T + 2]
                pool.tensor_tensor(zs, zs, hc_T[:, j, :, :], ALU.mult).then_inc(z_done, 1)
            squares(1, mem_T, memt_done, 0)

            def normalised(n, ready, base):
                k = 2 if n == 4 else 0
                for p in range(4):
                    if p % 2:
                        pool.wait_ge(msq_done, k + p // 2 + 1)
                        src = h_sq if p == 1 else h_std
                        ins = pool.tensor_tensor(sq_acc[:, :, :], sq_acc[:, :, :], src[:, :, :], ALU.add)
                        if p == 3:
                            ins.then_inc(sq_done, 1)
                        else:
                            then(ins)
                        continue
                    pool.wait_ge(ready, base + p + 1)
                    if p == 0:
                        pool.wait_ge(sum_done, n)
                    s = m_T[:, 2 * p:2 * p + 2, :]
                    then(pool.tensor_tensor((sq_tmp if p else sq_acc)[:, :, :], s, s, ALU.mult))
                    if p:
                        then(pool.tensor_tensor(sq_acc[:, :, :], sq_acc[:, :, :], sq_tmp[:, :, :], ALU.add))
                pool.wait_ge(rs_done, n + 1)
                for p in range(4):
                    s = m_T[:, 2 * p:2 * p + 2, :]
                    pool.wait_ge(ready, base + p + 1)
                    pool.tensor_tensor(s, s, rs_post[:, None, :].to_broadcast([P, 2, T]), ALU.mult).then_inc(post_done, 1)

            normalised(2, up_free_act, FREED[OUT1] - 1)
            squares(3, x_T, x_done, 4)
            pool.wait_ge(kf_done, 1)
            for h in range(4):
                wait_read(pool, MEMK + h)
                for t in range(2):
                    k = raw_k[:, t, 256 * h:256 * h + 256]
                    ins = pool.tensor_scalar(k, k, k_f[:, 2 * h + t:2 * h + t + 1], None, ALU.mult)
                ins.then_inc(kscaled_done, 1)
            normalised(4, m_done, 0)
            squares(5, x_T, x_done, 8)
            pool.wait_ge(mem_lo_done, 8)
            pool.memset(q_pad[:, :, :, :], 0.0).then_inc(zeroed, 1)
            squares(6, x_T, x_done, 12)
            for j in range(4):
                wait_read(pool, DQ + j)
                head_squares(raw[:, 2 * j:2 * j + 2, :], A_DIFF[j - 1] if j else None)
            for b in range(2):
                pool.wait_ge(aux_free, A_MEAN[b] + 1)
                head_squares(ret_o[:, 2 * b:2 * b + 2, :], A_VAR[0] if b else A_DIFF[3])
            for b in range(2):
                pool.wait_ge(diff_done, b + 1)
                head_squares(diff_o[:, 2 * b:2 * b + 2, :], A_DOUT[0] if b else A_VAR[1])
            squares(7, x_T, x_done, 16)
            squares(8, x_T, x_done, 20)
            squares(9, x_T, x_done, 24, 2)


def constants():
    import numpy as np

    i = np.arange(P)
    q, k = np.arange(P)[:, None], np.arange(T)[None, :]
    tri = np.concatenate([i[:, None] <= i[None, :], np.ones((P, P))], 1)
    causal = np.where(P + q >= k, 0.0, -1e30)
    sel = (i[:, None, None] == np.arange(8)[None, :, None]) * np.ones((1, 1, P))
    dist = P + q - k
    slopes = 2.0 ** (-8.0 * np.arange(1, 5) / 4)
    alibi = np.where(dist[:, None, :] >= 0, -slopes[None, :, None] * dist[:, None, :], -1e30)
    rel = np.arange(T)[None, :] - i[:, None]
    gamma = 1.0 - 2.0 ** (-5.0 - np.arange(4))
    decay = np.where(rel[:, None, :] >= 0, gamma[None, :, None] ** np.maximum(rel, 0)[:, None, :], 0.0) * P ** -0.5
    parts = [np.eye(P), np.ones((P, P)), i[:, None] // 64 == i[None, :] // 64, tri, causal, sel, alibi, decay]
    return np.concatenate([np.asarray(x, np.float32).reshape(P, -1) for x in parts], 1)


def kernel(**inputs):
    import numpy as np
    import concourse.bacc as bacc
    from concourse.bass_utils import run_bass_kernel_spmd

    nc = bacc.Bacc("TRN2", target_bir_lowering=False, num_devices=1)
    arrays, args = {}, {}
    for name, value in {**inputs, "consts": constants()}.items():
        v = np.ascontiguousarray(value)
        arrays[f"in_{name}"] = v
        args[name] = nc.dram_tensor(f"in_{name}", v.shape, mybir.dt.from_np(v.dtype), kind="ExternalInput").ap()
    out = nc.dram_tensor("out_dram", (1, T, D), F32, kind="ExternalOutput").ap()
    build(nc, args, out)
    r = run_bass_kernel_spmd(nc, [arrays], core_ids=[0])
    return r.results[0]["out_dram"]
```

```python
from contextlib import ExitStack

import concourse.bass as bass
from concourse import mybir

F32 = mybir.dt.float32
F32R = mybir.dt.float32r
ALU = mybir.AluOpType
ACT = mybir.ActivationFunctionType
AX = mybir.AxisListType.X

P = 128
T = 256
D = 1024
KD = D // P
HID = 2816
PAIRS = HID // (2 * P)
CH = 2048
RING = 3
EPS = 1e-6
LAM_INIT = 0.2

Q, K, V, GB, GC, HC, GATE_C, GATE_A = 0, 2, 4, 6, 8, 10, 12, 16
BR0, BR1, OUT1, MEMK = 20, 22, 24, 28
FFN = [32, 68, 128]
MEMV = [65, 66, 67, 101]
DQ, DK, DV, RQ, RK, RV, RG = 102, 104, 106, 108, 110, 112, 114
OUT2, MEMQ, OUTM = 116, 120, 124
CHUNKS = 161
FFN_CHUNKS = 3 * PAIRS


def ffn_ups(base):
    inner = [base + 2 + 3 * t + i for t in range(PAIRS - 2) for i in (0, 2)]
    return [base, base + 1, *inner, base + FFN_CHUNKS - 4, base + FFN_CHUNKS - 3]


BANK, BEFORE, FREED = {}, {}, {}
BY_ACT = {V, V + 1, *range(OUT1, OUT1 + 4), *range(MEMK, MEMK + 4), *MEMV, DQ, DQ + 1, RV, RV + 1, DV, DV + 1,
          *range(MEMQ, MEMQ + 4)}


def through_banks(chunks, first=0):
    for i, c in enumerate(chunks):
        b = (first + i) % 2
        BEFORE[c] = next((x for x in reversed(BANK) if BANK[x] == b), None)
        BANK[c] = b
        FREED[c] = sum((x in BY_ACT) == (c in BY_ACT) for x in BANK)


through_banks(range(Q, BR0))
through_banks(range(OUT1, OUT1 + 8))
through_banks(ffn_ups(FFN[0]))
through_banks(MEMV[:3], 1)
through_banks(ffn_ups(FFN[1]))
through_banks(MEMV[3:], 1)
through_banks(range(DQ, RG + 2))
through_banks(range(MEMQ, MEMQ + 4))
through_banks(ffn_ups(FFN[2]))
UP_FFN = [FREED[b] - 1 for b in FFN]


def made(n):
    return n + 1 if n < 7 else n


A_TOKX, A_F, A_LOGF, A_CUM = 0, 1, 2, 3
A_TOK2, A_DQ = 4, 5
A_DK = [6, 7]
A_QMEM = [8, 9]
A_BEFORE_FFN = [4, 4, 10]

G_MIX_PRE, G_MIX_POST, G_FFN_PRE, G_FFN_POST = 0, 8, 16, 24
G_FFN1, G_MIX2, G_MEMQ, G_MEMKV, G_FFN2 = 32, 40, 48, 56, 64
CONV, RETN, DIFN, MQN, MKN, DQN, DKN, LAMQ, LAMK, BF = 80, 92, 93, 94, 96, 98, 99, 100, 101, 102
C_ID, C_ONE, C_HALVES, C_TRI, C_CAUSAL, C_END = 0, 128, 256, 384, 640, 896


def build(nc, a, out):
    with ExitStack() as ctx:
        def sb(name, shape, dt=F32):
            return ctx.enter_context(nc.sbuf_tensor(name, shape, dt))

        def sem(name):
            return ctx.enter_context(nc.semaphore(name))

        stage = sb("stage", [P, RING, CH])
        w_hi = sb("w_hi", [P, RING, CH], F32R)
        w_lo = sb("w_lo", [P, RING, CH], F32R)
        x_T = sb("x_T", [P, KD, T])
        act_hi = sb("act_hi", [P, KD, T], F32R)
        act_lo = sb("act_lo", [P, KD, T], F32R)
        mix_hi = sb("mix_hi", [P, KD, T], F32R)
        mix_lo = sb("mix_lo", [P, KD, T], F32R)
        ffn_hi = sb("ffn_hi", [P, 2, T], F32R)
        ffn_lo = sb("ffn_lo", [P, 2, T], F32R)
        k_mem = sb("k_mem", [P, KD, T])
        v_mem = sb("v_mem", [P, 2, D])
        rs = sb("rs", [P, T])
        rs_post = sb("rs_post", [P, T])
        std = sb("std", [P, T])
        tok = sb("tok", [P, 2])
        tok_mem = sb("tok_mem", [P, 2])
        sq_acc = sb("sq_acc", [P, 2, T])
        sq_tmp = sb("sq_tmp", [P, 2, T])
        h_sq = sb("h_sq", [P, 2, T])
        h_std = sb("h_std", [P, 2, T])
        q_pad = sb("q_pad", [P, 2, 4, T])
        k_T = sb("k_T", [P, 4, T])
        v_tok = sb("v_tok", [P, 2, 512])
        L0 = sb("L0", [P, 8, P])
        L1 = sb("L1", [P, 8, T])
        gate = sb("gate", [P, 16, T])
        const = sb("const", [P, C_END])
        table = sb("table", [P, 8, T])
        par_rows = sb("par_rows", [P, P])
        par = sb("par", [P, P])
        first_rows = sb("first_rows", [KD, P])
        first_gain = sb("first_gain", [P, KD])
        wf = sb("wf", [P, KD, 8])
        forget = sb("forget", [P, 4, T])
        fz, fe, logf = (forget[:, i, :] for i in range(3))
        logf_tok = sb("logf_tok", [P, 2, 8])
        c_tok = sb("c_tok", [P, 2, 8])
        small = sb("small", [P, 160])
        eps_t = sb("eps_t", [P, 1])
        idle = sb("idle", [P, P])

        natural = gate[:, 0:8, :].rearrange("p a b -> p (a b)").rearrange("p (t d) -> p t d", t=2)
        mem_nat = L1[:, :, :].rearrange("p a b -> p (a b)").rearrange("p (t d) -> p t d", t=2)
        mem_T = q_pad[:, :, :, :].rearrange("p a b t -> p (a b) t")
        p_T0 = mem_T
        p_T1 = k_T[:, :, :].rearrange("p a b -> p (a b)").rearrange("p (m q) -> p m q", m=8)
        wf_hi = mix_hi[:, 0:4, :].rearrange("p a b -> p (a b)").rearrange("p (k n) -> p k n", k=KD)
        wf_lo = mix_lo[:, 0:4, :].rearrange("p a b -> p (a b)").rearrange("p (k n) -> p k n", k=KD)
        v_flat = v_mem[:, :, :].rearrange("p a b -> p (a b)")
        gb_T = v_flat[:, 0:1024].rearrange("p (a t) -> p a t", a=4)
        hc_T = v_flat[:, 1024:2048].rearrange("p (j a t) -> p j a t", j=2, a=2)
        k_flat = k_mem[:, :, :].rearrange("p a b -> p (a b)")
        z_T = k_flat[:, 0:4 * (T + 2)].rearrange("p (a t) -> p a t", a=4)
        y_T = k_flat[:, 1040:1040 + 2 * T].rearrange("p (a t) -> p a t", a=2)
        gate_c, gate_a = gate[:, 0:8, :], gate[:, 8:16, :]
        m_T = gate[:, 8:16, :]
        g_s, silu, u_s, h_T = (gate[:, 2 * i:2 * i + 2, :] for i in range(4))
        sel = table[:, 0:4, :].rearrange("p a b -> p (a b)").rearrange("p (h m) -> p h m", h=8)
        gain_rows = table[:, 0:4, :].rearrange("p a b -> p (a b)")
        sel_r = mix_hi[0:8, 4:8, :].rearrange("p a b -> p (a b)").rearrange("p (h m) -> p h m", h=8)
        negc_hi, negc_lo = mix_lo[0:8, 4, :], mix_lo[0:8, 5, :]
        alibi, decay = table[:, 0:4, :], table[:, 4:8, :]
        k_sq = [gate[:, 4 + 2 * j:6 + 2 * j, :] for j in range(2)]
        k_n = [gate[:, 2 * j:2 * j + 2, :] for j in range(2)]
        rq_T, rk_T = gate[:, 8:12, :], gate[:, 12:16, :]
        rv_tok = [forget[:, 2 * t:2 * t + 2, :].rearrange("p a b -> p (a b)") for t in range(2)]
        a_T0 = gate[:, 0:4, :]
        a_T1 = gate[:, 4:6, :].rearrange("p a b -> p (a b)").rearrange("p (h q) -> p h q", h=4)
        rg_s = L1[:, 0:4, :]
        ret_n = L1[:, 4:8, :].rearrange("p a b -> p (a b)").rearrange("p (t n) -> p t n", t=2)
        diff_n = L0[:, :, :].rearrange("p a b -> p (a b)").rearrange("p (t n) -> p t n", t=2)
        unused = [gate[:, 8:12, :], gate[:, 12:16, :]]
        p_mem = L1
        p_memT = L0[:, :, :].rearrange("p a b -> p (a b)").rearrange("p (h k q) -> p h k q", h=2, k=2)
        ident = const[:, C_ID:C_ID + P]
        ones = const[:, C_ONE:C_ONE + P]
        halves = const[:, C_HALVES:C_HALVES + P]
        tri = const[:, C_TRI:C_TRI + T]
        causal = const[:, C_CAUSAL:C_CAUSAL + T]
        eps = eps_t[:, :]
        raw_k = L1[:, :, :].rearrange("p a b -> p (a b)").rearrange("p (t n) -> p t n", t=2)
        tok_std = small[:, 56:58]
        q_eps, q_f = small[:, 58:60], small[:, 60:68]
        k_eps, k_f = small[:, 68:70], small[:, 72:80]
        diff_eps, diffk_eps = small[:, 80:82], small[:, 82:84]
        diff_f, diffk_f = small[:, 84:100], small[:, 100:116]
        do_f = small[:, 116:124]
        ro_mean, ro_f = small[:, 124:132], small[:, 132:140]
        act_squares = {1: h_sq, 2: sq_tmp, 3: h_std}
        q_sq = [h_sq, h_std]
        out_sq = small[:, 140:148]
        nmax, psum_, prec = small[:, 8:24], small[:, 24:40], small[:, 40:56]
        lam, lam_e, lam_p = small[:, 1:2], small[:, 2:4], small[:, 4:6]

        bank = [ctx.enter_context(nc.psum_tensor(f"bank{i}", [P, 512], F32)) for i in range(8)]
        pair = [b[:, :].rearrange("p (a t) -> p a t", a=2) for b in bank]
        quad = [b[:, :].rearrange("p (a t) -> p a t", a=4) for b in bank]
        UP, SUM, AUX, ACC = 0, 2, 3, 4
        SCORES, TURN, VALUES = (ACC, ACC + 1, UP, UP + 1), (ACC + 2, SUM, SUM, UP), (ACC + 3, AUX, AUX, UP + 1)
        DIFF_OUT, RET_OUT = (ACC + 3, SUM), (SUM, AUX)
        back = [pair[i] for i in (UP, UP + 1, AUX, ACC)]

        x_landed, const_landed, par_landed = sem("x_landed"), sem("const_landed"), sem("par_landed")
        ident_landed = sem("ident_landed")
        gain_landed, gain_turned, gain_done = sem("gain_landed"), sem("gain_turned"), sem("gain_done")
        wf_landed, mem_landed, table_landed = sem("wf_landed"), sem("mem_landed"), sem("table_landed")
        landed = [sem(f"landed{i}") for i in range(RING)]
        half_landed, half_hi_done, half_lo_done = sem("half_landed"), sem("half_hi_done"), sem("half_lo_done")
        idle_ready = sem("idle_ready")
        hi_done, lo_done, used = sem("hi_done"), sem("lo_done"), sem("used")
        up_free, up_free_act = sem("up_free"), sem("up_free_act")
        msq_done, post_done = sem("msq_done"), sem("post_done")
        keps_done, kdev_done, kf_done = sem("keps_done"), sem("kdev_done"), sem("kf_done")
        kscaled_done, k_turned, k_done = sem("kscaled_done"), sem("k_turned"), sem("k_done")
        zeroed, par_turned, par_ready = sem("zeroed"), sem("par_turned"), sem("par_ready")
        x_turned, x_done = sem("x_turned"), sem("x_done")
        act_hi_done, act_lo_done = sem("act_hi_done"), sem("act_lo_done")
        sq_done, sum_done, std_done, rs_done = sem("sq_done"), sem("sum_done"), sem("std_done"), sem("rs_done")
        aux_done, aux_free = sem("aux_done"), sem("aux_free")
        teps_done, dqsq_done, diff_f_done = sem("teps_done"), sem("dqsq_done"), sem("diff_f_done")
        ksq_done, ksum_done, kd_done = sem("ksq_done"), sem("ksum_done"), sem("kd_done")
        dsum_done, dd_done, dn_done = sem("dsum_done"), sem("dd_done"), sem("dn_done")
        dt_done, dhi_done, dlo_done = sem("dt_done"), sem("dhi_done"), sem("dlo_done")
        rsum_done, rmean_done, rsq_done, rd_done = sem("rsum_done"), sem("rmean_done"), sem("rsq_done"), sem("rd_done")
        rn_done, rt_done, rhi_done, rlo_done = sem("rn_done"), sem("rt_done"), sem("rhi_done"), sem("rlo_done")
        out2_done = sem("out2_done")
        wf_hi_done, wf_lo_done = sem("wf_hi_done"), sem("wf_lo_done")
        fz_done, fexp_done, fln_done = sem("fz_done"), sem("fexp_done"), sem("fln_done")
        logf_done, negc_done = sem("logf_done"), sem("negc_done")
        lg_done, lg_free, max_done, exp_done = sem("lg_done"), sem("lg_free"), sem("max_done"), sem("exp_done")
        p_done, tp_done, tp_free, pv_done = sem("p_done"), sem("tp_done"), sem("tp_free"), sem("pv_done")
        mixhi_done, mixlo_done = sem("mixhi_done"), sem("mixlo_done")
        z_done, y_done = sem("z_done"), sem("y_done")
        gates_done, br_half, br_free, merged = sem("gates_done"), sem("br_half"), sem("br_free"), sem("merged")
        memt_turned, memt_done = sem("memt_turned"), sem("memt_done")
        mem_hi_done, mem_lo_done = sem("mem_hi_done"), sem("mem_lo_done")
        m_done, down_done = sem("m_done"), sem("down_done")
        silu_done, h_done = sem("silu_done"), sem("h_done")
        ffn_hi_done, ffn_lo_done = sem("ffn_hi_done"), sem("ffn_lo_done")
        lam_done, lamx_done = sem("lam_done"), sem("lamx_done")
        sc_done, at_done, ro_done, rg_done = sem("sc_done"), sem("at_done"), sem("ro_done"), sem("rg_done")
        qsq_done, qf_done, outm_done = sem("qsq_done"), sem("qf_done"), sem("outm_done")
        dve_step, pool_step = sem("dve_step"), sem("pool_step")
        rows_landed, res_turned, res_sq_done = sem("rows_landed"), sem("res_turned"), sem("res_sq_done")
        res_sum_done, res_gained, stored = sem("res_sum_done"), sem("res_gained"), sem("stored")
        nat_done = [sem(f"nat_done{i}") for i in range(2)]

        block = ctx.enter_context(nc.Block())
        w_in, w_in2 = a["w_in"][0], a["w_in_2"][0]

        def wait_read(engine, c):
            engine.wait_ge(up_free_act if c in BY_ACT else up_free, FREED[c])

        def parameters(engine):
            engine.wait_ge(zeroed, 1)

            def rows(r, n, src, cols=P, at=0):
                engine.dma_start(par_rows[r:r + n, at:at + cols], src).then_inc(par_landed, 16)

            for r, name in ((G_MIX_PRE, "norm_mix_pre"), (G_MIX_POST, "norm_mix_post"), (G_FFN_PRE, "norm_ffn_pre"),
                            (G_FFN_POST, "norm_ffn_post"), (G_FFN1, "norm_ffn1_2"), (G_MIX2, "norm_mix_2"),
                            (G_MEMQ, "norm_mem_q_2"), (G_MEMKV, "norm_mem_kv_2"), (G_FFN2, "norm_ffn2_2")):
                rows(r, KD, a[name][0].rearrange("(k p) -> k p", p=P))
            rows(CONV, 12, a["conv_w"][0].rearrange("j (b p) -> (j b) p", p=P))
            rows(RETN, 1, a["ret_norm_2"])
            rows(DIFN, 1, a["diff_norm_2"])
            rows(MQN, 2, a["mem_q_norm_2"][0].rearrange("(k p) -> k p", p=P))
            rows(MKN, 2, a["mem_k_norm_2"][0].rearrange("(k p) -> k p", p=P))
            for r, name in ((DQN, "diff_q_norm_2"), (DKN, "diff_k_norm_2")):
                rows(r, 1, a[name], 64, 0)
                rows(r, 1, a[name], 64, 64)
            for r, at, name in ((LAMQ, 0, "lambda_q1_2"), (LAMQ, 64, "lambda_q2_2"),
                                (LAMK, 0, "lambda_k1_2"), (LAMK, 64, "lambda_k2_2")):
                rows(r, 1, a[name], 64, at)
            rows(BF, 1, a["b_f"], 8, 0)

        def store(engine, t, j):
            cols = slice(512 * j, 512 * j + 512)
            engine.dma_start(out[0, P * t:P * t + P, cols], natural[:, t, cols]).then_inc(stored, 16)

        @block.sync
        def _(sp):
            def slot(c):
                return c % RING

            def free(c):
                if isinstance(c, int) and c < RING:
                    return
                sp.wait_ge(lo_done, c - RING + 1)

            def whole(c, w, col, place):
                free(c)
                sp.dma_start(stage[:, place, :].rearrange("p (k n) -> p k n", k=KD),
                             w.rearrange("(k p) n -> p k n", p=P)[:, :, bass.ds(col, 2 * P)]
                             ).then_inc(landed[place], 16)

            def rows(c, w, r, n, col, width, place):
                free(c)
                sp.dma_start(stage[:, place, :].rearrange("p (k n) -> p k n", k=n),
                             w[bass.ds(r, n * P), col:col + width].rearrange("(k p) n -> p k n", p=P)
                             ).then_inc(landed[place], 16)

            def wholes(c, w, col, n):
                for i in range(n):
                    whole(c + i, w, col + 256 * i, slot(c + i))

            def feed_forward(base, w_g, g_col, w_u, u_col, w_d):
                whole(base, w_g, g_col, slot(base))
                whole(base + 1, w_u, u_col, slot(base + 1))
                with sp.Fori(0, PAIRS - 2) as t:
                    c = base + 2 + t * 3
                    whole(c, w_g, t * 256 + (g_col + 256), slot(base + 2))
                    rows(c + 1, w_d, t * 256, 2, 0, D, slot(base + 3))
                    whole(c + 2, w_u, t * 256 + (u_col + 256), slot(base + 4))
                last = base + FFN_CHUNKS - 1
                whole(last - 3, w_g, (PAIRS - 1) * 256 + g_col, slot(last - 3))
                whole(last - 2, w_u, (PAIRS - 1) * 256 + u_col, slot(last - 2))
                for i in range(2):
                    rows(last - 1 + i, w_d, (PAIRS - 2 + i) * 256, 2, 0, D, slot(last - 1 + i))

            for t in range(2):
                sp.dma_start(natural[:, t, :], a["x"][0, t * P:t * P + P, :]).then_inc(x_landed, 16)
            for half, done in enumerate((half_landed, landed[0])):
                sp.dma_start(stage[:, 0, half * CH // 2:(half + 1) * CH // 2].rearrange("p (k n) -> p k n", k=KD // 2),
                             w_in.rearrange("(k p) n -> p k n", p=P)[:, half * KD // 2:(half + 1) * KD // 2, 0:2 * P]
                             ).then_inc(done, 16)
            wholes(Q + 1, w_in, 256, 2)
            parameters(sp)
            wholes(K + 1, w_in, 256 * 3, 3)
            wholes(GB, w_in, 1544, 14)
            for i in range(4):
                rows(BR0 + i, a["w_branch"][0, i // 2], 0, 4, 512 * (i % 2), 512, slot(BR0 + i))
            wholes(OUT1, a["w_out"][0], 0, 4)
            wholes(MEMK, a["mem_w_kv_2"][0], 0, 4)
            feed_forward(FFN[0], a["w_gate_up"][0], 0, a["w_gate_up"][0], HID, a["w_down"][0])
            wholes(MEMV[0], a["mem_w_kv_2"][0], D, 3)
            feed_forward(FFN[1], a["ffn1_w1_2"][0], 0, a["ffn1_w3_2"][0], 0, a["ffn1_w2_2"][0])
            wholes(MEMV[3], a["mem_w_kv_2"][0], D + 3 * 256, 1)
            for c, col in ((DQ, 2048), (DK, 2560), (DV, 3072), (RQ, 0), (RK, 512), (RV, 1024), (RG, 1536)):
                wholes(c, w_in2, col, 2)
            for j in range(4):
                rows(OUT2 + j, a["w_out_2"][0], 512 if j < 2 else 0, 4, 512 * (j % 2), 512, slot(OUT2 + j))
            wholes(MEMQ, a["mem_w_q_2"][0], 0, 4)
            for j in range(4):
                rows(OUTM + j, a["mem_w_o_2"][0], 256 * j, 2, 0, D, slot(OUTM + j))
            sp.wait_ge(at_done, 1)
            sp.dma_start(gain_rows, a["norm_out_2"][0:1, :].to_broadcast([P, D])).then_inc(rows_landed, 16)
            feed_forward(FFN[2], a["ffn2_w1_2"][0], 0, a["ffn2_w3_2"][0], 0, a["ffn2_w2_2"][0])
            for t, j in ((1, 0), (0, 0), (1, 1)):
                sp.wait_ge(nat_done[t], j + 1)
                store(sp, t, j)
            sp.wait_ge(stored, 64)

        @block.tensor
        def _(pe):
            def three(dst, w, lo_w, x, lo_x, first, last, group=True):
                pe.matmul(dst, w, x, start=first, stop=False, skip_group_check=not group)
                pe.matmul(dst, w, lo_x, start=False, stop=False, skip_group_check=not group)
                return pe.matmul(dst, lo_w, x, start=False, stop=last, skip_group_check=not group)

            def up_bank(c):
                pe.wait_ge(lo_done, c + 1)
                if BEFORE[c] is not None:
                    wait_read(pe, BEFORE[c])

            def up_product(dst, place, hi, lo, ready=None, base=0, halves=False):
                wh = w_hi[:, place, :].rearrange("p (k n) -> p k n", k=KD)
                wl = w_lo[:, place, :].rearrange("p (k n) -> p k n", k=KD)
                if ready is None:
                    for m in range(2):
                        for k in range(KD):
                            mm = three(dst[:, m, :], wh[:, k, m * P:m * P + P], wl[:, k, m * P:m * P + P],
                                       hi[:, k, :], lo[:, k, :], k == 0, k == KD - 1)
                else:
                    for k in range(KD):
                        pe.wait_ge(ready, base + k + 1)
                        if halves and k == KD // 2:
                            pe.wait_ge(lo_done, 1)
                        for m in range(2):
                            mm = three(dst[:, m, :], wh[:, k, m * P:m * P + P], wl[:, k, m * P:m * P + P],
                                       hi[:, k, :], lo[:, k, :], k == 0 and m == 0, k == KD - 1, group=False)
                mm.then_inc(used, 1)

            def up(c, hi, lo, ready=None, base=0):
                up_bank(c)
                up_product(pair[UP + BANK[c]], c % RING, hi, lo, ready, base)

            def up_tok(c, hi, lo, ready=None):
                up_bank(c)
                wh = w_hi[:, c % RING, :].rearrange("p (k n) -> p k n", k=KD)
                wl = w_lo[:, c % RING, :].rearrange("p (k n) -> p k n", k=KD)
                for t in range(2):
                    for k in range(KD):
                        if ready is not None and t == 0:
                            pe.wait_ge(ready, k + 1)
                        xs = slice(t * P, t * P + P)
                        mm = three(pair[UP + BANK[c]][:, t, :], hi[:, k, xs], lo[:, k, xs],
                                   wh[:, k, :], wl[:, k, :], k == 0, k == KD - 1)
                mm.then_inc(used, 1)

            def sums(n):
                pe.wait_ge(sq_done, n + 1)
                if n:
                    pe.wait_ge(std_done, n)
                pe.matmul(bank[SUM][:, 0:T], ones, sq_acc[:, 0, :], start=True, stop=True).then_inc(sum_done, 1)

            def sums_by_token(n):
                pe.wait_ge(sq_done, n + 1)
                pe.wait_ge(std_done, n)
                for t in range(2):
                    mm = pe.matmul(bank[SUM][:, t:t + 1], sq_acc[:, 0, t * P:t * P + P], ones[:, 0:1],
                                   start=True, stop=True)
                mm.then_inc(sum_done, 1)

            def aux(n):
                if n:
                    pe.wait_ge(aux_free, n)

            def turn_rs(n, which, norm):
                pe.wait_ge(rs_done, made(norm))
                aux(n)
                pe.transpose(bank[AUX][:, 0:P], which[:, 0:P], ident)
                pe.transpose(bank[AUX][:, P:2 * P], which[:, P:T], ident).then_inc(aux_done, 1)

            def logits(g, first, bias):
                qt, b = g // 4, g % 4
                nk = P * (qt + 1)
                if qt:
                    pe.wait_ge(lg_free, first + g - 3)
                for par_ in range(2):
                    dst = pair[ACC + b][:, par_, 0:nk]
                    mm = pe.matmul(dst, q_pad[:, par_, b, qt * P:qt * P + P], k_T[:, b, 0:nk],
                                   start=True, stop=not bias)
                    if bias:
                        pe.matmul(dst, sel_r[:, 2 * b + par_, :], negc_hi[:, 0:nk], start=False, stop=False)
                        mm = pe.matmul(dst, sel_r[:, 2 * b + par_, :], negc_lo[:, 0:nk], start=False, stop=True)
                mm.then_inc(lg_done, 1)

            def down(c, place, hid_hi, hid_lo, first, done=None, cleared=None):
                pe.wait_ge(lo_done, c + 1)
                wh = w_hi[:, place, :].rearrange("p (k n) -> p k n", k=2)
                wl = w_lo[:, place, :].rearrange("p (k n) -> p k n", k=2)
                for m in range(KD):
                    if cleared is not None and m % 2 == 0:
                        pe.wait_ge(cleared, m // 2 + 1)
                    for k in range(2):
                        ms = slice(m * P, m * P + P)
                        mm = three(pair[ACC + m // 2][:, m % 2, :], wh[:, k, ms], wl[:, k, ms], hid_hi[:, k, :],
                                   hid_lo[:, k, :], first and k == 0 and m % 2 == 0, done is not None and k == 1,
                                   group=False)
                    if done is not None and m % 2 and m < KD - 1:
                        mm.then_inc(done, 1)
                mm.then_inc(used, 1)

            def ffn_chunk(c, f, i, first, place):
                pe.wait_ge(ffn_lo_done, i + (f * PAIRS + 1))
                hid_hi, hid_lo = (act_hi, act_lo) if first == "last" else (ffn_hi, ffn_lo)
                down(c, place, hid_hi, hid_lo, first == "first", down_done if first == "last" else None,
                     k_done if f == 0 and first == "first" else None)

            def feed_forward(f, prep, norm, extra=None):
                base, free = FFN[f], UP_FFN[f]
                up(base, act_hi, act_lo, act_lo_done, 8 * prep)
                sums(norm)
                up(base + 1, act_hi, act_lo)
                s = [(base + 2 + j) % RING for j in range(3)]

                def body(t, first):
                    c = base + 2 + t * 3
                    pe.wait_ge(lo_done, c + 1)
                    if first:
                        aux(A_BEFORE_FFN[f])
                    else:
                        pe.wait_ge(up_free, t * 2 + (free + 1))
                    up_product(pair[AUX if first else UP], s[0], act_hi, act_lo)
                    if first and extra is not None:
                        extra()
                    ffn_chunk(c + 1, f, t, first, s[1])
                    pe.wait_ge(lo_done, c + 3)
                    pe.wait_ge(up_free, t * 2 + (free + 2))
                    up_product(pair[UP + 1], s[2], act_hi, act_lo)

                body(0, "first")
                with pe.Fori(1, PAIRS - 2) as t:
                    body(t, "")
                last = base + FFN_CHUNKS - 1
                up(last - 3, act_hi, act_lo)
                up(last - 2, act_hi, act_lo)
                ffn_chunk(last - 1, f, PAIRS - 2, "", (last - 1) % RING)
                ffn_chunk(last, f, PAIRS - 1, "last", last % RING)

            pe.wait_ge(idle_ready, 1)
            for _ in range(10):
                pe.matmul(bank[AUX][:, 0:P], idle[:, :], idle[:, :], start=True, stop=True)
            pe.wait_ge(ident_landed, 16)
            pe.wait_ge(gain_landed, 16)
            pe.transpose(bank[SUM][:, 0:KD], first_rows[:, :], ident[0:KD, 0:KD]).then_inc(gain_turned, 1)
            pe.wait_ge(x_landed, 32)
            for b in range(4):
                for m in range(2):
                    for t in range(2):
                        d0 = (2 * b + m) * P
                        mm = pe.transpose(pair[ACC + b][:, m, t * P:t * P + P], natural[:, t, d0:d0 + P], ident)
                mm.then_inc(x_turned, 1)

            for _ in range(12):
                pe.matmul(bank[AUX][:, 0:P], idle[:, :], idle[:, :], start=True, stop=True)
            pe.wait_ge(half_lo_done, 1)
            up_product(pair[UP], 0, act_hi, act_lo, act_lo_done, 0, halves=True)
            pe.wait_ge(const_landed, 16)
            pe.wait_ge(gain_done, 1)
            sums(0)
            up(Q + 1, act_hi, act_lo)
            pe.wait_ge(par_landed, 16 * 23)
            pe.wait_ge(std_done, 1)
            pe.transpose(bank[SUM][:, 0:P], par_rows[:, :], ident).then_inc(par_turned, 1)
            up(K, act_hi, act_lo)
            turn_rs(A_TOKX, rs, 0)
            pe.wait_ge(par_ready, 2)
            pe.matmul(bank[SUM][:, 0:2], ones, lam_p, start=True, stop=True).then_inc(lam_done, 1)
            up(K + 1, act_hi, act_lo)
            pe.wait_ge(wf_lo_done, 1)
            aux(A_F)
            for k in range(KD):
                mm = three(bank[AUX][:, 0:T], wf_hi[:, k, :], wf_lo[:, k, :], act_hi[:, k, :], act_lo[:, k, :],
                           k == 0, k == KD - 1)
            mm.then_inc(aux_done, 1)
            up_tok(V, act_hi, act_lo)
            up_tok(V + 1, act_hi, act_lo)
            up(GB, act_hi, act_lo)
            up(GB + 1, act_hi, act_lo)
            pe.wait_ge(logf_done, 1)
            aux(A_LOGF)
            for t in range(2):
                mm = pe.transpose(bank[AUX][:, t * P:t * P + P], logf[:, t * P:t * P + P], ident)
            mm.then_inc(aux_done, 1)
            up(GC, act_hi, act_lo)
            aux(A_CUM)
            pe.matmul(bank[AUX][:, 0:8], tri[:, 0:P], logf_tok[:, 0, :], start=True, stop=True)
            pe.matmul(bank[AUX][:, 8:16], tri[:, P:T], logf_tok[:, 0, :], start=True, stop=False)
            pe.matmul(bank[AUX][:, 8:16], tri[:, 0:P], logf_tok[:, 1, :], start=False, stop=True)
            pe.matmul(bank[AUX][0:8, T:2 * T], logf_tok[:, 0, :], tri, start=True, stop=False)
            pe.matmul(bank[AUX][0:8, T + P:2 * T], logf_tok[:, 1, :], tri[:, 0:P],
                      start=False, stop=True).then_inc(aux_done, 1)
            up(GC + 1, act_hi, act_lo)
            up(HC, act_hi, act_lo)
            pe.wait_ge(aux_free, A_CUM + 1)
            pe.wait_ge(x_done, 4)
            for g in range(4):
                logits(g, 0, True)
            up(HC + 1, act_hi, act_lo)
            for g in range(4, 8):
                logits(g, 0, True)
            up(GATE_C, act_hi, act_lo)
            up(GATE_C + 1, act_hi, act_lo)
            up(GATE_C + 2, act_hi, act_lo)

            def turn_probs(e, tile, src, maps, e0):
                pe.wait_ge(p_done, tile + 1)
                if e >= 4 + e0:
                    pe.wait_ge(tp_free, e - 3)
                for i in range(4):
                    mm = pe.transpose(quad[ACC + (e - e0) % 4][:, i, :], src(maps + i), ident)
                mm.then_inc(tp_done, 1)

            pe.wait_ge(lg_free, 8)
            for e in range(2):
                turn_probs(e, 0, lambda m: L0[:, m, :], 4 * e, 0)
            up(GATE_C + 3, act_hi, act_lo)
            for e in range(2, 6):
                k0 = P * ((e - 2) // 2)
                turn_probs(e, 1, lambda m: L1[:, m, k0:k0 + P], 4 * (e % 2), 0)
            up(GATE_A, act_hi, act_lo)
            up(GATE_A + 1, act_hi, act_lo)
            pe.wait_ge(tp_free, 6)
            for b in range(4):
                for par_ in range(2):
                    m = 2 * b + par_
                    pe.matmul(pair[ACC + b][:, par_, :], v_tok[:, 0, b * P:b * P + P], p_T0[:, m, :],
                              start=True, stop=False)
                    mm = pe.matmul(pair[ACC + b][:, par_, P:T], v_tok[:, 1, b * P:b * P + P], p_T1[:, m, :],
                                   start=False, stop=True)
                mm.then_inc(pv_done, 1)
            up(GATE_A + 2, act_hi, act_lo)
            up(GATE_A + 3, act_hi, act_lo)
            for j in range(4):
                c = BR0 + j
                pe.wait_ge(lo_done, c + 1)
                pe.wait_ge(mixlo_done, 6 if j == 0 else 8)
                if j >= 2:
                    pe.wait_ge(br_free, j - 1)
                wh = w_hi[:, c % RING, :].rearrange("p (k n) -> p k n", k=4)
                wl = w_lo[:, c % RING, :].rearrange("p (k n) -> p k n", k=4)
                for m in range(4):
                    for k in range(4):
                        ms, kk = slice(m * P, m * P + P), 4 * (j // 2) + k
                        mm = three(pair[ACC + 2 * (j % 2) + m // 2][:, m % 2, :], wh[:, k, ms], wl[:, k, ms],
                                   mix_hi[:, kk, :], mix_lo[:, kk, :], k == 0, k == 3)
                    if j >= 2 and m == 1:
                        mm.then_inc(br_half, 1)
                mm.then_inc(used, 1)
            up(OUT1, act_hi, act_lo, act_lo_done, 8)
            pe.wait_ge(mem_landed, 16)
            pe.wait_ge(br_free, 6)
            for b in range(4):
                for m in range(2):
                    for t in range(2):
                        d0 = (2 * b + m) * P
                        mm = pe.transpose(pair[ACC + b][:, m, t * P:t * P + P], mem_nat[:, t, d0:d0 + P], ident)
                mm.then_inc(memt_turned, 1)
            up(OUT1 + 1, act_hi, act_lo)
            up(OUT1 + 2, act_hi, act_lo)
            sums_by_token(1)
            up(OUT1 + 3, act_hi, act_lo)
            up_tok(MEMK, mix_hi, mix_lo, mem_lo_done)
            sums(2)
            for j in range(1, 4):
                up_tok(MEMK + j, mix_hi, mix_lo)

            def turn_keys():
                pe.wait_ge(memt_done, 4)
                for h in range(4):
                    pe.wait_ge(kscaled_done, h + 1)
                    for i in range(2):
                        for t in range(2):
                            n0 = (2 * h + i) * P
                            mm = pe.transpose(pair[ACC + h][:, i, t * P:t * P + P], raw_k[:, t, n0:n0 + P], ident)
                    mm.then_inc(k_turned, 1)

            feed_forward(0, 2, 3, turn_keys)
            up_tok(MEMV[0], mix_hi, mix_lo)
            sums(4)
            for j in range(1, 3):
                up_tok(MEMV[j], mix_hi, mix_lo)
            feed_forward(1, 3, 5)
            up_tok(MEMV[3], mix_hi, mix_lo)
            up(DQ, act_hi, act_lo, act_lo_done, 32)
            sums(6)
            up(DQ + 1, act_hi, act_lo)
            turn_rs(A_TOK2, rs, 6)
            up_tok(DK, act_hi, act_lo)
            pe.wait_ge(dqsq_done, 2)
            aux(A_DQ)
            for b in range(4):
                for t in range(2):
                    o = 8 * t + 2 * b
                    mm = pe.matmul(bank[AUX][:, o:o + 2], q_sq[b // 2][:, b % 2, t * P:t * P + P], halves[:, 0:P:64],
                                   start=True, stop=True)
            mm.then_inc(aux_done, 1)
            up_tok(DK + 1, act_hi, act_lo)

            def turn_diff_keys(j):
                wait_read(pe, DK + j)
                aux(A_DK[j])
                for i in range(2):
                    for t in range(2):
                        mm = pe.transpose(pair[AUX][:, i, t * P:t * P + P], k_n[j][:, t, i * P:i * P + P], ident)
                mm.then_inc(aux_done, 1)

            turn_diff_keys(0)
            up_tok(DV, act_hi, act_lo)
            turn_diff_keys(1)
            up_tok(DV + 1, act_hi, act_lo)
            wait_read(pe, DQ + 1)
            for g in range(4):
                if g % 2 == 0:
                    pe.wait_ge(aux_free, A_DK[g // 2] + 1)
                logits(g, 8, False)
            up(RQ, act_hi, act_lo)
            for g in range(4, 8):
                logits(g, 8, False)
            up(RQ + 1, act_hi, act_lo)
            up(RK, act_hi, act_lo)
            pe.wait_ge(lg_free, 16)
            turn_probs(6, 2, lambda m: L0[:, 2 * m, :], 0, 6)
            for e in (7, 8):
                k0 = P * (e - 7)
                turn_probs(e, 3, lambda m: L1[:, 2 * m, k0:k0 + P], 0, 6)
            up(RK + 1, act_hi, act_lo)
            wait_read(pe, DV + 1)
            pe.wait_ge(tp_free, 9)
            for t in range(2):
                for h in range(4):
                    hs = slice(h * P, h * P + P)
                    mm = pe.matmul(quad[DIFF_OUT[t]][:, h, :], p_T0[:, h, t * P:t * P + P], v_tok[:, 0, hs],
                                   start=True, stop=t == 0)
                    if t:
                        mm = pe.matmul(quad[DIFF_OUT[t]][:, h, :], p_T1[:, h, :], v_tok[:, 1, hs], start=False, stop=True)
                mm.then_inc(pv_done, 1)
            up_tok(RV, act_hi, act_lo)
            wait_read(pe, RK + 1)
            for h in range(4):
                pe.matmul(pair[ACC + h // 2][:, h % 2, :], rk_T[:, h, 0:P], rq_T[:, h, :], start=True, stop=True)
            for h in range(4):
                mm = pe.matmul(quad[ACC + 2][:, h, :], rk_T[:, h, P:T], rq_T[:, h, P:T], start=True, stop=True)
            mm.then_inc(sc_done, 1)
            for t in range(2):
                pe.wait_ge(dn_done, t + 1)
                if t:
                    pe.wait_ge(dlo_done, t)
                else:
                    pe.wait_ge(aux_free, A_DK[1] + 1)
                for h in range(4):
                    mm = pe.transpose(quad[AUX][:, h, :], diff_n[:, t, h * P:h * P + P], ident)
                mm.then_inc(dt_done, 1)
                if t == 0:
                    up_tok(RV + 1, act_hi, act_lo)
            up(RG, act_hi, act_lo)
            pe.wait_ge(at_done, 1)
            wait_read(pe, RV + 1)
            pe.wait_ge(dlo_done, 2)
            for t in range(2):
                for h in range(4):
                    hs = slice(h * P, h * P + P)
                    mm = pe.matmul(quad[RET_OUT[t]][:, h, :], a_T0[:, h, t * P:t * P + P], rv_tok[0][:, hs],
                                   start=True, stop=t == 0)
                    if t:
                        mm = pe.matmul(quad[RET_OUT[t]][:, h, :], a_T1[:, h, :], rv_tok[1][:, hs], start=False, stop=True)
                mm.then_inc(ro_done, 1)
            up(RG + 1, act_hi, act_lo)

            def out2(j):
                c = OUT2 + j
                pe.wait_ge(lo_done, c + 1)
                wh = w_hi[:, c % RING, :].rearrange("p (k n) -> p k n", k=4)
                wl = w_lo[:, c % RING, :].rearrange("p (k n) -> p k n", k=4)
                for m in range(4):
                    for k in range(4):
                        ms, kk = slice(m * P, m * P + P), (4 if j < 2 else 0) + k
                        mm = three(pair[ACC + 2 * (j % 2) + m // 2][:, m % 2, :], wh[:, k, ms], wl[:, k, ms],
                                   mix_hi[:, kk, :], mix_lo[:, kk, :], j < 2 and k == 0 and m % 2 == 0,
                                   j >= 2 and k == 3, group=False)
                    if j >= 2 and m == 1:
                        mm.then_inc(out2_done, 1)
                mm.then_inc(used, 1)

            out2(0)
            wait_read(pe, RG + 1)
            for t in range(2):
                pe.wait_ge(rn_done, t + 1)
                for h in range(4):
                    mm = pe.transpose(quad[UP + t][:, h, :], ret_n[:, t, h * P:h * P + P], ident)
                mm.then_inc(rt_done, 1)
            out2(1)
            pe.wait_ge(rlo_done, 2)
            out2(2)
            out2(3)
            def query(j):
                up(MEMQ + j, act_hi, act_lo, None if j else act_lo_done, 40)

            def query_squares(h):
                pe.wait_ge(qsq_done, h + 1)
                if h % 2 == 0:
                    aux(A_QMEM[h // 2])
                for t in range(2):
                    for i in range(2):
                        mm = pe.matmul(bank[AUX][:, 2 * h + t:2 * h + t + 1], q_sq[h % 2][:, i, t * P:t * P + P],
                                       ones[:, 0:1], start=i == 0, stop=i == 1)
                if h % 2:
                    mm.then_inc(aux_done, 1)

            def mem_scores(h):
                wait_read(pe, MEMQ + h)
                for t in range(2):
                    for i in range(2):
                        b = 2 * h + i
                        mm = pe.matmul(pair[SCORES[h]][:, t, :], mem_T[:, b, t * P:t * P + P], k_mem[:, b, :],
                                       start=i == 0, stop=i == 1)
                mm.then_inc(lg_done, 1)

            def mem_turn(h):
                pe.wait_ge(p_done, 4 + h + 1)
                for k in range(2):
                    for t in range(2):
                        mm = pe.transpose(pair[TURN[h]][:, k, t * P:t * P + P],
                                          p_mem[:, 2 * h + t, k * P:k * P + P], ident)
                mm.then_inc(tp_done, 1)

            def mem_values(h):
                pe.wait_ge(tp_free, 9 + h + 1)
                if h:
                    aux(A_QMEM[1] + 1)
                if h == 2:
                    pe.wait_ge(mixlo_done, 12)
                for e in range(2):
                    for k in range(2):
                        d0 = (2 * h + e) * P
                        mm = pe.matmul(pair[VALUES[h]][:, e, :], v_mem[:, k, d0:d0 + P], p_memT[:, h % 2, k, :],
                                       start=k == 0, stop=k == 1)
                mm.then_inc(pv_done, 1)

            def mem_output(h):
                pe.wait_ge(mixlo_done, 8 + 2 * h + 2)
                s = slice(2 * h, 2 * h + 2)
                down(OUTM + h, (OUTM + h) % RING, mix_hi[:, s, :], mix_lo[:, s, :], h == 0, outm_done if h == 3 else None)

            query(0)
            query(1)
            sums_by_token(7)
            query_squares(0)
            mem_scores(0)
            query(2)
            query_squares(1)
            mem_scores(1)
            query(3)
            mem_turn(0)
            query_squares(2)
            mem_scores(2)
            mem_turn(1)
            mem_values(0)
            query_squares(3)
            mem_scores(3)
            mem_values(1)
            mem_output(0)
            mem_turn(2)
            mem_turn(3)
            mem_output(1)
            mem_values(2)
            mem_values(3)
            mem_output(2)
            mem_output(3)
            feed_forward(2, 6, 8)
            wait_read(pe, CHUNKS - 3)
            for p in range(4):
                pe.wait_ge(x_done, 24 + p + 1)
                for m in range(2):
                    for t in range(2):
                        mm = pe.transpose(back[p][:, t, m * P:m * P + P], x_T[:, 2 * p + m, t * P:t * P + P], ident)
                mm.then_inc(res_turned, 1)

        @block.scalar
        def _(act):
            copy, table_exp = ACT.Copy, ACT.Exp

            def hi(c):
                place = c % RING
                act.wait_ge(landed[place], 16 * (c // RING + 1))
                if c >= RING:
                    act.wait_ge(used, c - RING + 1)
                act.activation(w_hi[:, place, :], stage[:, place, :], copy).then_inc(hi_done, 1)

            def hi_in_loop(t, first):
                place = first % RING
                act.wait_ge(landed[place], t * 16 + 16 * (first // RING + 1))
                act.wait_ge(used, t * 3 + (first - RING + 1))
                act.activation(w_hi[:, place, :], stage[:, place, :], copy).then_inc(hi_done, 1)

            def gained(gains, col, pairs_done, after, blocks=range(KD)):
                for b in blocks:
                    act.wait_ge(x_done, pairs_done + b // 2 + 1)
                    if b == 0 and after:
                        act.wait_ge(used, after)
                    act.activation(act_hi[:, b, :], x_T[:, b, :], copy,
                                   scale=gains[:, col + b:col + b + 1]).then_inc(act_hi_done, 1)

            def warm(function):
                act.activation(small[:, 6:7], eps, function)

            def square(p, src):
                act.activation(act_squares[p][:, :, :], src, ACT.Square).then_inc(msq_done, 1)

            def gained_and_squares(col, pairs_done, after):
                for p in range(4):
                    act.wait_ge(x_done, pairs_done + p + 1)
                    xs = x_T[:, 2 * p:2 * p + 2, :]
                    if p == 3:
                        square(p, xs)
                    gained(par, col, pairs_done, after, range(2 * p, 2 * p + 2))
                    if p in (1, 2):
                        square(p, xs)

            def deviation(n):
                act.wait_ge(sum_done, n + 1)
                if n:
                    act.wait_ge(rs_done, made(n - 1))
                act.activation(std[:, :], bank[SUM][:, 0:T], ACT.Sqrt, bias=eps, scale=1.0 / D).then_inc(std_done, 1)

            def result(c):
                act.wait_ge(used, c + 1)
                return pair[UP + BANK[c]]

            def scaled_tok(c, to, r):
                src = result(c)
                for t in range(2):
                    e = act.activation(to[t], src[:, t, :], copy, scale=r[:, t:t + 1])
                e.then_inc(up_free_act, 1)

            def keep_m(p, src):
                if p % 2:
                    square(p, src)
                return act.activation(m_T[:, 2 * p:2 * p + 2, :], src, copy)

            def down_ready(f, p):
                if p < 3:
                    act.wait_ge(down_done, 3 * f + p + 1)
                else:
                    act.wait_ge(used, FFN[f] + FFN_CHUNKS)
                return pair[ACC + p]

            def exps(tile, L, nk):
                act.wait_ge(max_done, tile + 1)
                o = 8 * (tile % 2)
                for m in range(8):
                    e = act.activation(L[:, m, 0:nk], L[:, m, 0:nk], table_exp, bias=nmax[:, o + m:o + m + 1],
                                       accum_out=psum_[:, o + m:o + m + 1])
                e.then_inc(exp_done, 1)

            def feed_forward(f):
                base, u0 = FFN[f], UP_FFN[f]

                def hidden(t, i):
                    act.wait_ge(up_free, t * 2 + (u0 + 2 * i + 1))
                    act.activation(silu, g_s, ACT.Silu).then_inc(silu_done, 1)

                def hidden_hi(t, i, after, to):
                    act.wait_ge(h_done, t + (f * PAIRS + i + 1))
                    if after is not None:
                        act.wait_ge(used, after)
                    act.activation(to, h_T, copy).then_inc(ffn_hi_done, 1)

                hidden(0, 0)
                hidden_hi(0, 0, None if f == 0 else FFN[f - 1] + FFN_CHUNKS, ffn_hi[:, :, :])
                with act.Fori(0, PAIRS - 2) as t:
                    hi_in_loop(t, base + 4)
                    hidden(t, 1)
                    hi_in_loop(t, base + 5)
                    hi_in_loop(t, base + 6)
                    hidden_hi(t, 1, t * 3 + (base + 4), ffn_hi[:, :, :])
                last = base + FFN_CHUNKS - 1
                hi(last - 1)
                hidden(PAIRS - 2, 1)
                hi(last)
                hidden_hi(PAIRS - 2, 1, last - 1, act_hi[:, 0:2, :])
                if last + 1 < CHUNKS:
                    hi(last + 1)

            act.dma_start(ident, a["consts"][:, C_ID:C_ID + P]).then_inc(ident_landed, 16)
            act.dma_start(first_rows[:, :], a["norm_mix_pre"][0].rearrange("(k p) -> k p", p=P)).then_inc(gain_landed, 16)
            act.dma_start(const[:, P:C_END], a["consts"][:, P:C_END]).then_inc(const_landed, 16)
            act.dma_start(wf[:, :, :], a["w_in"][0].rearrange("(k p) n -> p k n", p=P)[:, :, 1536:1544]
                          ).then_inc(wf_landed, 16)
            act.dma_start(sel, a["consts"][:, C_END:C_END + 1024].rearrange("p (h m) -> p h m", h=8)
                          ).then_inc(table_landed, 16)
            act.wait_ge(idle_ready, 1)
            act.activation(std[:, 0:1], idle[:, 0:1], copy)
            first, second = slice(0, CH // 2), slice(CH // 2, CH)
            act.wait_ge(gain_done, 1)
            gained(first_gain, 0, 0, 0, range(0, 2))
            act.wait_ge(half_landed, 16)
            act.activation(w_hi[:, 0, first], stage[:, 0, first], copy).then_inc(half_hi_done, 1)
            gained(first_gain, 0, 0, 0, range(2, 4))
            act.wait_ge(landed[0], 16)
            act.activation(w_hi[:, 0, second], stage[:, 0, second], copy).then_inc(hi_done, 1)
            gained(first_gain, 0, 0, 0, range(4, KD))
            square(3, x_T[:, 6:8, :])
            hi(1)
            act.wait_ge(wf_landed, 16)
            act.wait_ge(zeroed, 9)
            act.activation(wf_hi[:, :, 0:8], wf[:, :, :], copy).then_inc(wf_hi_done, 1)
            warm(ACT.Sqrt)
            deviation(0)
            hi(2)
            hi(3)
            hi(4)
            act.wait_ge(lam_done, 1)
            act.activation(lam_e, bank[SUM][:, 0:2], table_exp).then_inc(lamx_done, 1)
            hi(5)
            hi(6)
            hi(7)
            act.wait_ge(aux_free, A_TOKX + 1)
            scaled_tok(V, [v_tok[:, t, 0:256] for t in range(2)], tok)
            act.wait_ge(fz_done, 1)
            act.activation(fe[0:8, :], fe[0:8, :], table_exp).then_inc(fexp_done, 1)
            act.wait_ge(fexp_done, 1)
            act.activation(fe[0:8, :], fe[0:8, :], ACT.Ln, bias=1.0).then_inc(fln_done, 1)
            hi(8)
            scaled_tok(V + 1, [v_tok[:, t, 256:512] for t in range(2)], tok)
            act.wait_ge(table_landed, 16)
            act.activation(sel_r, sel[0:8, :, :], copy)
            hi(9)
            hi(10)
            hi(11)
            act.wait_ge(aux_done, A_CUM + 1)
            act.activation(negc_hi, bank[AUX][0:8, T:2 * T], copy, scale=-1.0).then_inc(negc_done, 1)
            hi(12)
            hi(13)
            hi(14)
            exps(0, L0, P)
            hi(15)
            exps(1, L1, T)

            def conv_hi(b):
                act.wait_ge(y_done, b + 1)
                if b == 0:
                    act.wait_ge(aux_done, A_F + 1)
                act.activation(mix_hi[:, b, :], y_T[:, b % 2, :], copy).then_inc(mixhi_done, 1)

            def keep_probs(e, to):
                act.wait_ge(tp_done, e + 1)
                act.activation(to, quad[ACC + (e if e < 6 else e - 6) % 4], copy).then_inc(tp_free, 1)

            hi(16)
            conv_hi(0)
            for e in range(2):
                keep_probs(e, p_T0[:, 4 * e:4 * e + 4, 0:P])
            hi(17)
            for e in range(2, 4):
                keep_probs(e, p_T0[:, 4 * e - 8:4 * e - 4, P:T])
            for e in range(4, 6):
                keep_probs(e, p_T1[:, 4 * e - 16:4 * e - 12, :])
            conv_hi(1)
            hi(18)
            conv_hi(2)
            conv_hi(3)
            act.wait_ge(tp_done, 6)
            act.dma_start(mem_nat, a["mem_2"][0].rearrange("(t p) d -> p t d", p=P)).then_inc(mem_landed, 16)
            act.wait_ge(lg_done, 8)
            act.dma_start(table[:, :, :], a["consts"][:, C_END + 1024:C_END + 3072].rearrange("p (h m) -> p h m", h=8)
                          ).then_inc(table_landed, 16)
            hi(19)
            hi(20)
            for b in range(4):
                act.wait_ge(pv_done, b + 1)
                act.activation(mix_hi[0:64, 4 + b, :], pair[ACC + b][0:64, 0, :], copy)
                act.activation(mix_hi[64:P, 4 + b, :], pair[ACC + b][64:P, 1, :], copy).then_inc(mixhi_done, 1)
            hi(21)
            for i in range(8):
                if i == 4:
                    hi(22)
                wait_read(act, GATE_C + i)
                act.activation(gate[:, 2 * i:2 * i + 2, :], gate[:, 2 * i:2 * i + 2, :], ACT.Sigmoid).then_inc(gates_done, 1)
            hi(23)
            hi(24)
            act.wait_ge(used, GATE_A + 4)
            for i in range(4):
                if i == 2:
                    hi(25)
                act.wait_ge(merged, i + 1)
                act.activation(act_hi[:, 2 * i:2 * i + 2, :], gate_c[:, 2 * i:2 * i + 2, :], copy).then_inc(act_hi_done, 2)
            hi(26)

            def out1(p):
                keep_m(p, result(OUT1 + p)).then_inc(up_free_act, 1)

            def key_read(h):
                src, s = result(MEMK + h), slice(256 * h, 256 * h + 256)
                if h >= 2:
                    wait_read(act, MEMK + h - 2)
                for t in range(2):
                    act.activation(forget[:, 2 * (h % 2) + t, :], src[:, t, :], ACT.Square, accum_out=k_f[:, 2 * h + t:2 * h + t + 1])
                act.activation(raw_k[:, :, s], src, copy).then_inc(up_free_act, 1)

            out1(0)
            hi(27)
            for b in range(KD):
                act.wait_ge(memt_done, b // 2 + 1)
                if b == 0:
                    act.wait_ge(used, BR1 + 2)
                act.activation(mix_hi[:, b, :], mem_T[:, b, :], copy,
                               scale=par[:, G_MEMKV + b:G_MEMKV + b + 1]).then_inc(mem_hi_done, 1)
            square(3, mem_T[:, 6:8, :])
            out1(1)
            hi(28)
            act.wait_ge(sum_done, 2)
            act.wait_ge(rs_done, 1)
            act.activation(tok_std, bank[SUM][:, 0:2], ACT.Sqrt, bias=eps, scale=1.0 / D).then_inc(std_done, 1)
            out1(2)
            hi(29)
            out1(3)
            hi(30)
            key_read(0)
            deviation(2)
            hi(31)
            key_read(1)
            hi(32)
            gained(par, G_FFN_PRE, 4, OUT1 + 4, range(0, 4))
            key_read(2)
            gained(par, G_FFN_PRE, 4, OUT1 + 4, range(4, 8))
            square(3, x_T[:, 6:8, :])
            hi(33)
            key_read(3)
            act.wait_ge(keps_done, 1)
            wait_read(act, MEMK + 3)
            for t in range(2):
                e = act.activation(k_f[:, t::2], k_f[:, t::2], ACT.Sqrt, bias=k_eps[:, t:t + 1], scale=1.0 / T)
            e.then_inc(kdev_done, 1)
            hi(34)
            deviation(3)
            warm(ACT.Silu)
            hi(35)
            feed_forward(0)
            warm(ACT.Sqrt)
            for p in range(4):
                keep_m(p, down_ready(0, p)).then_inc(m_done, 1)
            hi(66)
            hi(67)

            def memory_values(j):
                scaled_tok(MEMV[j], [v_mem[:, t, 256 * j:256 * j + 256] for t in range(2)], tok_mem)

            deviation(4)
            hi(68)
            memory_values(0)
            memory_values(1)
            hi(69)
            gained_and_squares(G_FFN1, 8, FFN[0] + FFN_CHUNKS)
            memory_values(2)
            hi(70)
            deviation(5)
            warm(ACT.Silu)
            hi(71)
            feed_forward(1)
            hi(102)
            warm(ACT.Sqrt)
            gained(par, G_MIX2, 12, FFN[1] + FFN_CHUNKS)
            memory_values(3)
            hi(103)
            hi(104)

            def diff_query(j):
                src = result(DQ + j)
                act.activation(q_sq[j][:, :, :], src, ACT.Square).then_inc(dqsq_done, 1)
                if j == 0:
                    act.wait_ge(zeroed, 10)
                for p, i in ((slice(0, 64), 0), (slice(64, P), 1)):
                    e = act.activation(q_pad[p, i, 2 * j:2 * j + 2, :], src[p], copy, scale=par[p, DQN:DQN + 1])
                e.then_inc(up_free_act, 1)

            def diff_key_squares(j):
                act.activation(k_sq[j], result(DK + j), ACT.Square).then_inc(ksq_done, 1)

            def diff_key_deviation(j):
                act.wait_ge(teps_done, 1)
                act.wait_ge(ksum_done, j + 1)
                for t in range(2):
                    s = diffk_f[:, 8 * j + 4 * t:8 * j + 4 * t + 4]
                    e = act.activation(s, s, ACT.Sqrt, bias=diffk_eps[:, t:t + 1], scale=1.0 / 64)
                e.then_inc(kd_done, 1)

            def diff_keys(j):
                act.wait_ge(aux_done, A_DK[j] + 1)
                act.activation(k_T[:, 2 * j:2 * j + 2, :], pair[AUX], copy, scale=par[:, DKN:DKN + 1]).then_inc(aux_free, 1)

            diff_query(0)
            deviation(6)
            hi(105)
            diff_query(1)
            hi(106)
            diff_key_squares(0)
            hi(107)
            diff_key_deviation(0)
            act.wait_ge(aux_done, A_DQ + 1)
            for t in range(2):
                s = slice(8 * t, 8 * t + 8)
                e = act.activation(diff_f[:, s], bank[AUX][:, s], ACT.Sqrt, bias=diff_eps[:, t:t + 1])
            e.then_inc(aux_free, 1)
            diff_key_squares(1)
            hi(108)
            diff_keys(0)
            diff_key_deviation(1)
            act.wait_ge(aux_free, A_TOK2 + 1)
            scaled_tok(DV, [v_tok[:, t, 0:256] for t in range(2)], tok)
            hi(109)
            diff_keys(1)
            scaled_tok(DV + 1, [v_tok[:, t, 256:512] for t in range(2)], tok)
            hi(110)
            exps(2, L0, P)
            hi(111)
            exps(3, L1, T)
            hi(112)
            keep_probs(6, p_T0[:, 0:4, 0:P])
            keep_probs(7, p_T0[:, 0:4, P:T])
            keep_probs(8, p_T1[:, 0:4, :])
            hi(113)
            warm(ACT.Sqrt)

            def head_sums(bank_, t, to, place, done, function, shift=None):
                for h in range(4):
                    i = slice(4 * t + h, 4 * t + h + 1)
                    bias = 0.0 if shift is None else shift[:, i]
                    e = act.activation(place[:, h, :], quad[bank_][:, h, :], function, bias=bias, accum_out=to[:, i])
                e.then_inc(done, 1)

            def head_deviations(t, to, summed, done):
                act.wait_ge(summed, t + 1)
                s = to[:, 4 * t:4 * t + 4]
                act.activation(s, s, ACT.Sqrt, bias=eps, scale=1.0 / P).then_inc(done, 1)

            squares_of_diff = [q[:, :, :].rearrange("p a b -> p (a b)").rearrange("p (h e) -> p h e", h=4) for q in q_sq]
            for t in range(2):
                act.wait_ge(pv_done, 4 + t + 1)
                head_sums(DIFF_OUT[t], t, do_f, squares_of_diff[t], dsum_done, ACT.Square)
            for t in range(2):
                head_deviations(t, do_f, dsum_done, dd_done)
            scaled_tok(RV, [r[:, 0:256] for r in rv_tok], tok)
            hi(114)

            def diff_hi(t):
                act.wait_ge(dt_done, t + 1)
                if t == 0:
                    act.wait_ge(used, MEMV[3] + 1)
                act.activation(mix_hi[:, 4:8, t * P:t * P + P], quad[AUX], copy, scale=par[:, DIFN:DIFN + 1]).then_inc(dhi_done, 1)

            diff_hi(0)
            scaled_tok(RV + 1, [r[:, 256:512] for r in rv_tok], tok)
            hi(115)
            diff_hi(1)
            hi(116)
            hi(117)

            def silu_gate(i):
                wait_read(act, RG + i)
                act.activation(rg_s[:, 2 * i:2 * i + 2, :], rg_s[:, 2 * i:2 * i + 2, :], ACT.Silu).then_inc(rg_done, 1)

            silu_gate(0)
            warm(ACT.Sqrt)
            sums_place, squares_place = ([u[:, 2 * t:2 * t + 2, :].rearrange("p a b -> p (a b)").rearrange(
                "p (h e) -> p h e", h=4) for t in range(2)] for u in unused)
            for t in range(2):
                act.wait_ge(ro_done, t + 1)
                head_sums(RET_OUT[t], t, ro_mean, sums_place[t], rsum_done, copy)
            for t in range(2):
                act.wait_ge(rmean_done, t + 1)
                head_sums(RET_OUT[t], t, ro_f, squares_place[t], rsq_done, ACT.Square, ro_mean)
                head_deviations(t, ro_f, rsq_done, rd_done)
            hi(118)
            silu_gate(1)
            for t in range(2):
                act.wait_ge(y_done, 4 + t + 1)
                act.activation(mix_hi[:, 0:4, t * P:t * P + P], rg_s[:, :, t * P:t * P + P], copy).then_inc(rhi_done, 1)
            hi(119)
            hi(120)
            gained(par, G_MEMQ, 16, RG + 2, range(0, 4))
            hi(121)
            gained(par, G_MEMQ, 16, RG + 2, range(4, KD))

            def query(h):
                src = result(MEMQ + h)
                if h == 2:
                    act.wait_ge(aux_done, A_QMEM[0] + 1)
                act.activation(q_sq[h % 2][:, :, :], src, ACT.Square).then_inc(qsq_done, 1)
                for i in range(2):
                    e = act.activation(mem_T[:, 2 * h + i, :], src[:, i, :], copy, scale=par[:, MQN + i:MQN + i + 1])
                e.then_inc(up_free_act, 1)

            def query_deviation(b):
                act.wait_ge(std_done, 8)
                act.wait_ge(aux_done, A_QMEM[b] + 1)
                for t in range(2):
                    s = slice(4 * b + t, 4 * b + 4, 2)
                    e = act.activation(q_f[:, s], bank[AUX][:, s], ACT.Sqrt, bias=q_eps[:, t:t + 1])
                e.then_inc(aux_free, 1)

            def mem_exps(h):
                act.wait_ge(max_done, 4 + h + 1)
                for t in range(2):
                    i = 2 * h + t
                    e = act.activation(p_mem[:, i, :], pair[SCORES[h]][:, t, :], table_exp, bias=nmax[:, i:i + 1],
                                       scale=q_f[:, i:i + 1], accum_out=psum_[:, i:i + 1])
                e.then_inc(exp_done, 1)

            def mem_out(h):
                act.wait_ge(tp_done, 9 + h + 1)
                act.activation(p_memT[:, h % 2, :, :], pair[TURN[h]], copy).then_inc(tp_free, 1)

            def mem_hi(h):
                act.wait_ge(pv_done, 6 + h + 1)
                if h == 0:
                    act.wait_ge(used, OUT2 + 4)
                act.activation(mix_hi[:, 2 * h:2 * h + 2, :], pair[VALUES[h]], copy).then_inc(mixhi_done, 2)

            warm(ACT.Sqrt)
            hi(122)
            query(0)
            hi(123)
            query(1)
            hi(124)
            query_deviation(0)
            mem_exps(0)
            query(2)
            mem_exps(1)
            hi(125)
            mem_out(0)
            query(3)
            mem_out(1)
            query_deviation(1)
            mem_hi(0)
            mem_hi(1)
            mem_exps(2)
            mem_exps(3)
            hi(126)
            mem_out(2)
            mem_out(3)
            hi(127)
            mem_hi(2)
            mem_hi(3)
            hi(128)
            hi(129)
            gained_and_squares(G_FFN2, 20, MEMQ + 4)
            hi(130)
            deviation(8)
            warm(ACT.Silu)
            hi(131)
            feed_forward(2)
            warm(ACT.Sqrt)
            for p in range(4):
                act.wait_ge(res_turned, p + 1)
                for t in range(2):
                    i = 2 * p + t
                    e = act.activation(m_T[:, i, :], back[p][:, t, :], ACT.Square, accum_out=out_sq[:, i:i + 1])
                e.then_inc(res_sq_done, 1)
            act.wait_ge(res_sum_done, 1)
            act.activation(tok_std, tok_std, ACT.Sqrt, bias=eps, scale=1.0 / D).then_inc(std_done, 1)
            act.wait_ge(rs_done, made(9))
            act.wait_ge(res_gained, 4)
            for j in range(2):
                s = natural[:, 0, 512 * j:512 * j + 512]
                act.activation(s, s, copy, scale=tok[:, 0:1]).then_inc(nat_done[0], 1)
            act.wait_ge(nat_done[0], 2)
            store(act, 0, 1)

        @block.vector
        def _(dve):
            steps = [0]

            def then(ins):
                steps[0] += 1
                ins.then_inc(dve_step, 1)
                dve.wait_ge(dve_step, steps[0])

            def over(r, n=2, p=slice(0, P)):
                return r[p, None, :].to_broadcast([p.stop - p.start, n, T])

            def lo(c):
                place = c % RING
                dve.wait_ge(hi_done, c + 1)
                dve.tensor_tensor(w_lo[:, place, :], stage[:, place, :], w_hi[:, place, :].bitcast(F32),
                                  ALU.subtract).then_inc(lo_done, 1)

            def lo_in_loop(t, first):
                place = first % RING
                dve.wait_ge(hi_done, t * 3 + (first + 1))
                dve.tensor_tensor(w_lo[:, place, :], stage[:, place, :], w_hi[:, place, :].bitcast(F32),
                                  ALU.subtract).then_inc(lo_done, 1)

            def gained(gains, col, prep, blocks=range(KD)):
                for b in blocks:
                    dve.wait_ge(act_hi_done, 8 * prep + b + 1)
                    dve.scalar_tensor_tensor(act_lo[:, b, :], x_T[:, b, :], gains[:, col + b:col + b + 1],
                                             act_hi[:, b, :].bitcast(F32), ALU.mult, ALU.subtract
                                             ).then_inc(act_lo_done, 1)

            def factor(n, to):
                dve.wait_ge(std_done, n + 1)
                dve.reciprocal(to[:, :], std[:, :]).then_inc(rs_done, 1)
                dve.wait_ge(rs_done, made(n))

            def result(c):
                dve.wait_ge(used, c + 1)
                return pair[UP + BANK[c]]

            def scaled(c, to, r):
                dve.tensor_tensor(to, result(c), over(r), ALU.mult).then_inc(up_free, 1)

            def keep_tok(n, to):
                dve.wait_ge(aux_done, n + 1)
                dve.tensor_copy(to[:, :], bank[AUX][:, 0:2 * P:P]).then_inc(aux_free, 1)
                dve.wait_ge(aux_free, n + 1)

            def softmax_max(tile, L, nk):
                o = 8 * (tile % 2)
                dve.wait_ge(dve_step, steps[0])
                dve.tensor_reduce(nmax[:, o:o + 8], L[:, :, 0:nk], AX, ALU.max, negate=True).then_inc(max_done, 1)

            def inverse_sums(tile):
                o = 8 * (tile % 2)
                dve.wait_ge(exp_done, tile + 1)
                then(dve.reciprocal(prec[:, o:o + 8], psum_[:, o:o + 8]))
                return o

            def read_scores(g, first):
                qt, b = g // 4, g % 4
                nk = P * (qt + 1)
                L = L1 if qt else L0
                dve.wait_ge(lg_done, first + g + 1)
                for i in range(2):
                    m = 2 * b + i
                    src = pair[ACC + b][:, i, 0:nk]
                    if first == 0:
                        ins = dve.scalar_tensor_tensor(L[:, m, :], src, c_tok[:, qt, m:m + 1],
                                                       causal[:, T - nk:T], ALU.add, ALU.add)
                    else:
                        ins = dve.scalar_tensor_tensor(L[:, m, :], src, diff_f[:, 8 * qt + m:8 * qt + m + 1],
                                                       alibi[:, b, T - nk:T], ALU.mult, ALU.add)
                ins.then_inc(lg_free, 1)
                dve.wait_ge(lg_free, first + g + 1)

            def feed_forward(f, extra=None):
                base, u0 = FFN[f], UP_FFN[f]

                def gate_part(t, i, src=pair[UP]):
                    dve.wait_ge(used, t * 3 + (base + (2 + 3 * (i - 1) if i else 0) + 1))
                    dve.tensor_tensor(g_s, src, over(rs), ALU.mult).then_inc(up_free, 1)

                def up_part(t, i, chunk, to=ffn_lo[:, :, :], of=ffn_hi[:, :, :]):
                    n = f * PAIRS + i + 1
                    dve.wait_ge(used, t * 3 + (chunk + 1))
                    dve.tensor_tensor(u_s, pair[UP + 1], over(rs), ALU.mult).then_inc(up_free, 1)
                    dve.wait_ge(up_free, t * 2 + (u0 + 2 * i + 2))
                    dve.wait_ge(silu_done, t + n)
                    dve.tensor_tensor(h_T, u_s, silu, ALU.mult).then_inc(h_done, 1)
                    dve.wait_ge(ffn_hi_done, t + n)
                    dve.tensor_tensor(to, h_T, of.bitcast(F32), ALU.subtract).then_inc(ffn_lo_done, 1)

                gate_part(0, 0)
                up_part(0, 0, base + 1)
                if extra is not None:
                    extra()

                def body(t, src):
                    lo_in_loop(t, base + 4)
                    gate_part(t, 1, src)
                    lo_in_loop(t, base + 5)
                    lo_in_loop(t, base + 6)
                    up_part(t, 1, base + 4)

                body(0, pair[AUX])
                with dve.Fori(1, PAIRS - 2) as t:
                    body(t, pair[UP])
                last = base + FFN_CHUNKS - 1
                lo(last - 1)
                gate_part(PAIRS - 2, 1)
                lo(last)
                up_part(PAIRS - 2, 1, base + 3, act_lo[:, 0:2, :], act_hi[:, 0:2, :])
                if last + 1 < CHUNKS:
                    lo(last + 1)

            def down_ready(f, p):
                if p < 3:
                    dve.wait_ge(down_done, 3 * f + p + 1)
                else:
                    dve.wait_ge(used, FFN[f] + FFN_CHUNKS)
                return pair[ACC + p]

            def post_pair(p, col, n, count):
                dve.wait_ge(post_done, (4 if n == 4 else 0) + p + 1)
                for b in (2 * p, 2 * p + 1):
                    ins = dve.scalar_tensor_tensor(x_T[:, b, :], m_T[:, b, :], par[:, col + b:col + b + 1], x_T[:, b, :],
                                                   ALU.mult, ALU.add)
                ins.then_inc(x_done, 1)
                dve.wait_ge(x_done, count + p + 1)

            def post_and_gained(col, n, count, next_col, prep):
                for p in range(4):
                    post_pair(p, col, n, count)
                    if p:
                        gained(par, next_col, prep, range(2 * p - 2, 2 * p))
                gained(par, next_col, prep, range(6, 8))

            dve.memset(idle[:, :], 0.0).then_inc(idle_ready, 1)
            dve.wait_ge(gain_turned, 1)
            dve.tensor_copy(first_gain[:, :], bank[SUM][:, 0:KD]).then_inc(gain_done, 1)
            for b in range(4):
                dve.wait_ge(x_turned, b + 1)
                dve.tensor_copy(x_T[:, 2 * b:2 * b + 2, :], pair[ACC + b]).then_inc(x_done, 1)
            dve.wait_ge(x_done, 4)

            def half_lo(half, ready, done):
                dve.wait_ge(ready, 1)
                dve.tensor_tensor(w_lo[:, 0, half], stage[:, 0, half], w_hi[:, 0, half].bitcast(F32), ALU.subtract
                                  ).then_inc(done, 1)

            half_lo(slice(0, CH // 2), half_hi_done, half_lo_done)
            gained(first_gain, 0, 0, range(0, 4))
            half_lo(slice(CH // 2, CH), hi_done, lo_done)
            gained(first_gain, 0, 0, range(4, KD))
            lo(1)
            dve.wait_ge(wf_hi_done, 1)
            dve.wait_ge(zeroed, 9)
            dve.tensor_tensor(wf_lo[:, :, 0:8], wf[:, :, :], wf_hi[:, :, 0:8].bitcast(F32), ALU.subtract
                              ).then_inc(wf_lo_done, 1)
            factor(0, rs)

            def query(c):
                src, b = result(c), 2 * (c - Q)
                dve.scalar_tensor_tensor(q_pad[0:64, 0, b:b + 2, :], src[0:64, :, :], 0.125, over(rs, p=slice(0, 64)),
                                         ALU.mult, ALU.mult)
                dve.scalar_tensor_tensor(q_pad[64:P, 1, b:b + 2, :], src[64:P, :, :], 0.125, over(rs, p=slice(64, P)),
                                         ALU.mult, ALU.mult).then_inc(up_free, 1)

            query(Q)
            lo(2)
            lo(3)
            query(Q + 1)
            dve.wait_ge(par_turned, 1)
            dve.tensor_copy(par[:, :], bank[SUM][:, 0:P]).then_inc(par_ready, 1)
            dve.wait_ge(par_ready, 1)
            dve.tensor_tensor(lam_p[0:64, 0:1], par[0:64, LAMQ:LAMQ + 1], par[0:64, LAMK:LAMK + 1], ALU.mult)
            dve.tensor_tensor(lam_p[64:P, 1:2], par[64:P, LAMQ:LAMQ + 1], par[64:P, LAMK:LAMK + 1], ALU.mult
                              ).then_inc(par_ready, 1)
            lo(4)
            scaled(K, k_T[:, 0:2, :], rs)
            lo(5)
            dve.wait_ge(lamx_done, 1)
            then(dve.tensor_tensor(lam, lam_e[:, 1:2], lam_e[:, 0:1], ALU.subtract))
            then(dve.tensor_scalar(lam, lam, -LAM_INIT, None, ALU.add))
            then(dve.tensor_scalar(par[:, DIFN:DIFN + 1], par[:, DIFN:DIFN + 1], 1.0 - LAM_INIT, None, ALU.mult))
            keep_tok(A_TOKX, tok)
            scaled(K + 1, k_T[:, 2:4, :], rs)
            lo(6)
            dve.wait_ge(aux_done, A_F + 1)
            dve.tensor_tensor(fz[0:8, :], bank[AUX][0:8, 0:T], rs[0:8, :], ALU.mult).then_inc(aux_free, 1)
            dve.wait_ge(aux_free, A_F + 1)
            then(dve.tensor_scalar(fz[0:8, :], fz[0:8, :], par[0:8, BF:BF + 1], None, ALU.add))
            dve.scalar_tensor_tensor(fe[0:8, :], fz[0:8, :], -1.0, fz[0:8, :], ALU.mult, ALU.min).then_inc(fz_done, 1)
            lo(7)
            lo(8)
            dve.wait_ge(fln_done, 1)
            dve.scalar_tensor_tensor(logf[0:8, :], fz[0:8, :], 0.0, fe[0:8, :], ALU.min, ALU.subtract).then_inc(logf_done, 1)
            scaled(GB, gb_T[:, 0:2, :], rs)
            lo(9)
            scaled(GB + 1, gb_T[:, 2:4, :], rs)
            lo(10)
            dve.wait_ge(aux_done, A_LOGF + 1)
            dve.tensor_copy(logf_tok[:, :, :], pair[AUX].rearrange("p a t -> p (a t)")[:, 0:2 * P].rearrange(
                "p (t q) -> p t q", t=2)[:, :, 0:8]).then_inc(aux_free, 1)
            scaled(GC, z_T[:, 0:2, 2:T + 2], rs)
            lo(11)
            dve.wait_ge(aux_done, A_CUM + 1)
            dve.wait_ge(negc_done, 1)
            dve.tensor_copy(c_tok[:, :, :].rearrange("p a b -> p (a b)"), bank[AUX][:, 0:16])
            dve.scalar_tensor_tensor(negc_lo, bank[AUX][0:8, T:2 * T], -1.0, negc_hi.bitcast(F32), ALU.mult, ALU.subtract
                                     ).then_inc(aux_free, 1)
            dve.wait_ge(aux_free, A_CUM + 1)
            scaled(GC + 1, z_T[:, 2:4, 2:T + 2], rs)
            lo(12)
            scaled(HC, hc_T[:, 0, :, :], rs)
            lo(13)
            for g in range(4):
                read_scores(g, 0)
            softmax_max(0, L0, P)
            scaled(HC + 1, hc_T[:, 1, :, :], rs)
            lo(14)
            for g in range(4, 8):
                read_scores(g, 0)
            softmax_max(1, L1, T)
            scaled(GATE_C, gate[:, 0:2, :], rs)
            lo(15)

            def normal(tile, L, nk):
                o = inverse_sums(tile)
                dve.tensor_tensor(L[:, :, 0:nk], L[:, :, 0:nk], prec[:, o:o + 8, None].to_broadcast([P, 8, nk]), ALU.mult
                                  ).then_inc(p_done, 1)

            def conv(b):
                dve.wait_ge(z_done, b // 2 + 1)
                if b >= 2:
                    dve.wait_ge(mixhi_done, b - 1)
                y = y_T[:, b % 2, :]
                for j in range(3):
                    w = par[:, CONV + 4 * j + b:CONV + 4 * j + b + 1]
                    if j == 0:
                        then(dve.tensor_scalar(y, z_T[:, b, 0:T], w, None, ALU.mult))
                    else:
                        then(dve.scalar_tensor_tensor(y, z_T[:, b, j:j + T], w, y, ALU.mult, ALU.add))
                dve.tensor_tensor(y, y, gb_T[:, b, :], ALU.mult).then_inc(y_done, 1)

            def conv_lo(b):
                dve.wait_ge(mixhi_done, b + 1)
                dve.tensor_tensor(mix_lo[:, b, :], y_T[:, b % 2, :], mix_hi[:, b, :].bitcast(F32), ALU.subtract
                                  ).then_inc(mixlo_done, 1)

            scaled(GATE_C + 1, gate[:, 2:4, :], rs)
            normal(0, L0, P)
            conv(0)
            lo(16)
            scaled(GATE_C + 2, gate[:, 4:6, :], rs)
            normal(1, L1, T)
            conv_lo(0)
            conv(1)
            lo(17)
            scaled(GATE_C + 3, gate[:, 6:8, :], rs)
            conv_lo(1)
            conv(2)
            lo(18)
            scaled(GATE_A, gate[:, 8:10, :], rs)
            conv_lo(2)
            conv(3)
            lo(19)
            scaled(GATE_A + 1, gate[:, 10:12, :], rs)
            conv_lo(3)
            lo(20)
            scaled(GATE_A + 2, gate[:, 12:14, :], rs)
            for b in range(4):
                dve.wait_ge(mixhi_done, 4 + b + 1)
                for p, i in ((slice(0, 64), 0), (slice(64, P), 1)):
                    ins = dve.tensor_tensor(mix_lo[p, 4 + b, :], pair[ACC + b][p, i, :], mix_hi[p, 4 + b, :].bitcast(F32),
                                            ALU.subtract)
                ins.then_inc(mixlo_done, 1)
            lo(21)
            scaled(GATE_A + 3, gate[:, 14:16, :], rs)
            lo(22)
            for j in range(2):
                dve.wait_ge(used, BR0 + j + 1)
                dve.wait_ge(gates_done, 2 * j + 2)
                for i in range(2):
                    g = gate_c[:, 4 * j + 2 * i:4 * j + 2 * i + 2, :]
                    ins = dve.tensor_tensor(g, pair[ACC + 2 * j + i], g, ALU.mult)
                ins.then_inc(br_free, 1)
                lo(23 + j)
            for j in range(2):
                dve.wait_ge(gates_done, 4 + 2 * j + 2)
                for i in range(2):
                    if i == 0:
                        dve.wait_ge(br_half, j + 1)
                    else:
                        dve.wait_ge(used, BR1 + j + 1)
                    s = slice(4 * j + 2 * i, 4 * j + 2 * i + 2)
                    g = gate_a[:, s, :]
                    dve.tensor_tensor(g, pair[ACC + 2 * j + i], g, ALU.mult).then_inc(br_free, 1)
                    dve.wait_ge(br_free, 3 + 2 * j + i)
                    dve.tensor_tensor(gate_c[:, s, :], gate_c[:, s, :], g, ALU.add).then_inc(merged, 1)
                for i in range(2):
                    s = slice(4 * j + 2 * i, 4 * j + 2 * i + 2)
                    dve.wait_ge(act_hi_done, 8 + 4 * j + 2 * i + 2)
                    dve.tensor_tensor(act_lo[:, s, :], gate_c[:, s, :], act_hi[:, s, :].bitcast(F32), ALU.subtract
                                      ).then_inc(act_lo_done, 2)
            lo(25)
            lo(26)

            for b in range(4):
                dve.wait_ge(memt_turned, b + 1)
                dve.tensor_copy(mem_T[:, 2 * b:2 * b + 2, :], pair[ACC + b]).then_inc(memt_done, 1)
            lo(27)
            dve.wait_ge(memt_done, 4)
            for b in range(KD):
                dve.wait_ge(mem_hi_done, b + 1)
                dve.scalar_tensor_tensor(mix_lo[:, b, :], mem_T[:, b, :], par[:, G_MEMKV + b:G_MEMKV + b + 1],
                                         mix_hi[:, b, :].bitcast(F32), ALU.mult, ALU.subtract).then_inc(mem_lo_done, 1)
            lo(28)
            dve.wait_ge(std_done, 2)
            dve.scalar_tensor_tensor(k_eps, tok_std, EPS, tok_std, ALU.mult, ALU.mult).then_inc(keps_done, 1)
            dve.reciprocal(tok_mem[:, :], tok_std).then_inc(rs_done, 1)
            lo(29)
            lo(30)
            factor(2, rs_post)
            lo(31)
            lo(32)
            post_and_gained(G_MIX_POST, 2, 4, G_FFN_PRE, 2)
            lo(33)
            dve.wait_ge(kdev_done, 1)
            dve.reciprocal(k_f, k_f).then_inc(kf_done, 1)
            lo(34)
            factor(3, rs)
            lo(35)

            def memory_keys():
                for h in range(4):
                    dve.wait_ge(k_turned, h + 1)
                    for i in range(2):
                        ins = dve.tensor_scalar(k_mem[:, 2 * h + i, :], pair[ACC + h][:, i, :], par[:, MKN + i:MKN + i + 1],
                                                None, ALU.mult)
                    ins.then_inc(k_done, 1)

            feed_forward(0, memory_keys)

            lo(66)
            lo(67)
            factor(4, rs_post)
            lo(68)
            post_and_gained(G_FFN_POST, 4, 8, G_FFN1, 3)
            lo(69)
            lo(70)
            factor(5, rs)
            lo(71)
            feed_forward(1)

            def half_residual(f, count):
                for p in range(4):
                    src = down_ready(f, p)
                    xs = x_T[:, 2 * p:2 * p + 2, :]
                    dve.scalar_tensor_tensor(xs, src, 0.5, xs, ALU.mult, ALU.add).then_inc(x_done, 1)
                    dve.wait_ge(x_done, count + p + 1)

            lo(102)
            half_residual(1, 12)
            gained(par, G_MIX2, 4)
            lo(103)
            lo(104)
            factor(6, rs)
            lo(105)
            keep_tok(A_TOK2, tok)
            then(dve.reciprocal(tok_mem[:, :], tok[:, :]))
            dve.scalar_tensor_tensor(diffk_eps, tok_mem[:, :], EPS, tok_mem[:, :], ALU.mult, ALU.mult)
            dve.scalar_tensor_tensor(diff_eps, tok_mem[:, :], 64 * EPS, tok_mem[:, :], ALU.mult, ALU.mult).then_inc(teps_done, 1)
            lo(106)

            def groups(x):
                return x.rearrange("p t n -> p (t n)").rearrange("p (g d) -> p g d", g=8)

            def diff_key_sums(j):
                dve.wait_ge(ksq_done, j + 1)
                dve.tensor_reduce(diffk_f[:, 8 * j:8 * j + 8], groups(k_sq[j]), AX, ALU.add).then_inc(ksum_done, 1)

            def diff_key_normal(j):
                dve.wait_ge(kd_done, j + 1)
                f = diffk_f[:, 8 * j:8 * j + 8]
                then(dve.reciprocal(f, f))
                dve.tensor_tensor(groups(k_n[j]), groups(result(DK + j)), f[:, :, None].to_broadcast([P, 8, 64]), ALU.mult
                                  ).then_inc(up_free, 1)

            diff_key_sums(0)
            lo(107)
            diff_key_normal(0)
            dve.wait_ge(aux_free, A_DQ + 1)
            dve.reciprocal(diff_f, diff_f).then_inc(diff_f_done, 1)
            diff_key_sums(1)
            lo(108)
            diff_key_normal(1)
            lo(109)
            dve.wait_ge(table_landed, 32)
            dve.wait_ge(diff_f_done, 1)
            for g in range(4):
                read_scores(g, 8)
            softmax_max(2, L0, P)
            lo(110)
            scaled(RQ, rq_T[:, 0:2, :], rs)
            for g in range(4, 8):
                read_scores(g, 8)
            softmax_max(3, L1, T)
            lo(111)

            def difference(tile, L, nk):
                o = inverse_sums(tile)
                odd = prec[:, o + 1:o + 8:2]
                dve.tensor_scalar(odd, odd, lam, None, ALU.mult)
                first = L[:, 0:8:2, 0:nk]
                then(dve.tensor_tensor(first, first, prec[:, o:o + 8:2, None].to_broadcast([P, 4, nk]), ALU.mult))
                for h in range(4):
                    ins = dve.scalar_tensor_tensor(L[:, 2 * h, 0:nk], L[:, 2 * h + 1, 0:nk], prec[:, o + 2 * h + 1:o + 2 * h + 2],
                                                   L[:, 2 * h, 0:nk], ALU.mult, ALU.add)
                ins.then_inc(p_done, 1)

            difference(2, L0, P)
            difference(3, L1, T)
            scaled(RQ + 1, rq_T[:, 2:4, :], rs)
            lo(112)
            scaled(RK, rk_T[:, 0:2, :], rs)
            lo(113)
            scaled(RK + 1, rk_T[:, 2:4, :], rs)
            for t in range(2):
                dve.wait_ge(dd_done, t + 1)
                f = do_f[:, 4 * t:4 * t + 4]
                then(dve.reciprocal(f, f))
                dve.tensor_tensor(diff_n[:, t, :].rearrange("p (h e) -> p h e", h=4), quad[DIFF_OUT[t]],
                                  f[:, :, None].to_broadcast([P, 4, P]), ALU.mult).then_inc(dn_done, 1)
            lo(114)

            def diff_lo(t):
                dve.wait_ge(dhi_done, t + 1)
                s = slice(t * P, t * P + P)
                dve.scalar_tensor_tensor(mix_lo[:, 4:8, s], quad[AUX], par[:, DIFN:DIFN + 1], mix_hi[:, 4:8, s].bitcast(F32),
                                         ALU.mult, ALU.subtract).then_inc(dlo_done, 1)

            diff_lo(0)
            dve.wait_ge(sc_done, 1)
            for b in range(2):
                dve.tensor_tensor(a_T0[:, 2 * b:2 * b + 2, :], pair[ACC + b], decay[:, 2 * b:2 * b + 2, :], ALU.mult)
            dve.tensor_tensor(a_T1, quad[ACC + 2], decay[:, :, 0:P], ALU.mult).then_inc(at_done, 1)
            lo(115)
            diff_lo(1)
            lo(116)
            scaled(RG, rg_s[:, 0:2, :], rs)
            lo(117)
            for t in range(2):
                dve.wait_ge(rsum_done, t + 1)
                m = ro_mean[:, 4 * t:4 * t + 4]
                dve.tensor_scalar(m, m, -1.0 / P, None, ALU.mult).then_inc(rmean_done, 1)
            for t in range(2):
                dve.wait_ge(rd_done, t + 1)
                f = ro_f[:, 4 * t:4 * t + 4]
                then(dve.reciprocal(f, f))
                for h in range(4):
                    i = 4 * t + h
                    ins = dve.tensor_scalar(ret_n[:, t, h * P:h * P + P], quad[RET_OUT[t]][:, h, :], ro_mean[:, i:i + 1],
                                            ro_f[:, i:i + 1], ALU.add, ALU.mult)
                ins.then_inc(rn_done, 1)
            scaled(RG + 1, rg_s[:, 2:4, :], rs)
            lo(118)
            dve.wait_ge(rg_done, 2)
            for t in range(2):
                dve.wait_ge(rt_done, t + 1)
                g = rg_s[:, :, t * P:t * P + P]
                dve.scalar_tensor_tensor(g, quad[UP + t], par[:, RETN:RETN + 1], g, ALU.mult, ALU.mult).then_inc(y_done, 1)
            for t in range(2):
                dve.wait_ge(rhi_done, t + 1)
                s = slice(t * P, t * P + P)
                dve.tensor_tensor(mix_lo[:, 0:4, s], rg_s[:, :, s], mix_hi[:, 0:4, s].bitcast(F32), ALU.subtract).then_inc(rlo_done, 1)
            lo(119)
            lo(120)
            for p in range(4):
                if p == 2:
                    gained(par, G_MEMQ, 5, range(2, 4))
                    lo(121)
                if p % 2 == 0:
                    dve.wait_ge(out2_done, p // 2 + 1)
                else:
                    dve.wait_ge(used, OUT2 + 2 + p // 2 + 1)
                xs = x_T[:, 2 * p:2 * p + 2, :]
                dve.tensor_tensor(xs, pair[ACC + p], xs, ALU.add).then_inc(x_done, 1)
                dve.wait_ge(x_done, 16 + p + 1)
                if p % 2:
                    gained(par, G_MEMQ, 5, range(2 * p - 2, 2 * p))
            gained(par, G_MEMQ, 5, range(6, KD))

            def query_factor(b):
                dve.wait_ge(aux_free, A_QMEM[b] + 1)
                dve.reciprocal(q_f[:, 4 * b:4 * b + 4], q_f[:, 4 * b:4 * b + 4]).then_inc(qf_done, 1)

            def mem_max(h):
                dve.wait_ge(lg_done, 16 + h + 1)
                s = slice(2 * h, 2 * h + 2)
                then(dve.tensor_reduce(nmax[:, s], pair[SCORES[h]], AX, ALU.max, negate=True))
                dve.wait_ge(qf_done, h // 2 + 1)
                dve.tensor_tensor(nmax[:, s], nmax[:, s], q_f[:, s], ALU.mult).then_inc(max_done, 1)

            def mem_normal(h):
                dve.wait_ge(exp_done, 4 + h + 1)
                s = slice(2 * h, 2 * h + 2)
                then(dve.reciprocal(prec[:, s], psum_[:, s]))
                dve.tensor_tensor(p_mem[:, s, :], p_mem[:, s, :], prec[:, s, None].to_broadcast([P, 2, T]), ALU.mult
                                  ).then_inc(p_done, 1)

            def mem_lo(h):
                s = slice(2 * h, 2 * h + 2)
                dve.wait_ge(mixhi_done, 8 + 2 * h + 2)
                dve.tensor_tensor(mix_lo[:, s, :], pair[VALUES[h]], mix_hi[:, s, :].bitcast(F32), ALU.subtract
                                  ).then_inc(mixlo_done, 2)

            lo(122)
            lo(123)
            dve.wait_ge(sum_done, 8)
            dve.tensor_scalar(q_eps, bank[SUM][:, 0:2], T * EPS / D, T * EPS * EPS, ALU.mult, ALU.add).then_inc(std_done, 1)
            lo(124)
            query_factor(0)
            mem_max(0)
            mem_max(1)
            mem_normal(0)
            lo(125)
            mem_normal(1)
            query_factor(1)
            mem_lo(0)
            mem_max(2)
            mem_lo(1)
            mem_max(3)
            mem_normal(2)
            mem_normal(3)
            lo(126)
            lo(127)
            mem_lo(2)
            mem_lo(3)
            lo(128)
            for p in range(4):
                if p < 3:
                    dve.wait_ge(outm_done, p + 1)
                else:
                    dve.wait_ge(used, OUTM + 4)
                xs = x_T[:, 2 * p:2 * p + 2, :]
                dve.tensor_tensor(xs, pair[ACC + p], xs, ALU.add).then_inc(x_done, 1)
                dve.wait_ge(x_done, 20 + p + 1)
                if p:
                    gained(par, G_FFN2, 6, range(2 * p - 2, 2 * p))
            gained(par, G_FFN2, 6, range(6, KD))
            lo(129)
            lo(130)
            factor(8, rs)
            lo(131)
            feed_forward(2)
            half_residual(2, 24)
            dve.wait_ge(rows_landed, 16)

            def result_gained(p):
                dve.wait_ge(res_sq_done, p + 1)
                s = slice(2 * p * P, 2 * p * P + 2 * P)
                dve.tensor_tensor(natural[:, :, s], back[p], gain_rows[:, None, s].to_broadcast([P, 2, 2 * P]), ALU.mult
                                  ).then_inc(res_gained, 1)

            for p in range(3):
                result_gained(p)
            dve.wait_ge(res_sq_done, 4)
            dve.tensor_reduce(tok_std, out_sq.rearrange("p (q t) -> p t q", t=2), AX, ALU.add).then_inc(res_sum_done, 1)
            result_gained(3)
            dve.wait_ge(std_done, 10)
            dve.reciprocal(tok[:, :], tok_std).then_inc(rs_done, 1)
            dve.wait_ge(rs_done, made(9))
            dve.wait_ge(res_gained, 4)
            for j in range(2):
                s = natural[:, 1, 512 * j:512 * j + 512]
                dve.tensor_scalar(s, s, tok[:, 1:2], None, ALU.mult).then_inc(nat_done[1], 1)

        @block.gpsimd
        def _(pool):
            steps = [0]

            def then(ins):
                steps[0] += 1
                ins.then_inc(pool_step, 1)
                pool.wait_ge(pool_step, steps[0])

            def squares(n, src, ready, base, by_act=(), before=0):
                for p in range(4):
                    if p in by_act:
                        pool.wait_ge(msq_done, before + by_act.index(p) + 1)
                    else:
                        pool.wait_ge(ready, base + p + 1)
                        if p == 0 and n:
                            pool.wait_ge(sum_done, n)
                        s = src[:, 2 * p:2 * p + 2, :]
                        then(pool.tensor_tensor((sq_tmp if p else sq_acc)[:, :, :], s, s, ALU.mult))
                    if p:
                        sq = act_squares[p] if p in by_act else sq_tmp
                        then(pool.tensor_tensor(sq_acc[:, :, :], sq_acc[:, :, :], sq[:, :, :], ALU.add))
                pool.tensor_tensor(sq_acc[:, 0, :], sq_acc[:, 0, :], sq_acc[:, 1, :], ALU.add).then_inc(sq_done, 1)

            pool.memset(par_rows[:, :], 0.0).then_inc(zeroed, 1)
            pool.memset(small[:, :], 0.0).then_inc(zeroed, 1)
            pool.memset(wf_hi.bitcast(F32), 0.0).then_inc(zeroed, 1)
            pool.memset(wf_lo.bitcast(F32), 0.0).then_inc(zeroed, 1)
            pool.memset(q_pad[:, :, :, :], 0.0).then_inc(zeroed, 1)
            pool.memset(logf[:, :], 0.0).then_inc(zeroed, 1)
            pool.memset(z_T[:, :, 0:2], 0.0).then_inc(zeroed, 1)
            pool.memset(eps_t[:, :], EPS).then_inc(zeroed, 1)
            pool.memset(fe[:, :], 0.0).then_inc(zeroed, 1)
            squares(0, x_T, x_done, 0, (3,), 0)
            for j in range(2):
                wait_read(pool, HC + j)
                zs = z_T[:, 2 * j:2 * j + 2, 2:T + 2]
                pool.tensor_tensor(zs, zs, hc_T[:, j, :, :], ALU.mult).then_inc(z_done, 1)
            squares(1, mem_T, memt_done, 0, (3,), 1)

            def normalised(n, ready, base, before):
                squares(n, m_T, ready, base, (1, 3), before)
                pool.wait_ge(rs_done, n + 1)
                for p in range(4):
                    s = m_T[:, 2 * p:2 * p + 2, :]
                    pool.wait_ge(ready, base + p + 1)
                    pool.tensor_tensor(s, s, rs_post[:, None, :].to_broadcast([P, 2, T]), ALU.mult).then_inc(post_done, 1)

            normalised(2, up_free_act, FREED[OUT1] - 1, 2)
            squares(3, x_T, x_done, 4, (3,), 4)
            pool.wait_ge(kf_done, 1)
            for h in range(4):
                wait_read(pool, MEMK + h)
                for t in range(2):
                    k = raw_k[:, t, 256 * h:256 * h + 256]
                    ins = pool.tensor_scalar(k, k, k_f[:, 2 * h + t:2 * h + t + 1], None, ALU.mult)
                ins.then_inc(kscaled_done, 1)
            normalised(4, m_done, 0, 5)
            squares(5, x_T, x_done, 8, (1, 2, 3), 7)
            pool.wait_ge(mem_lo_done, 8)
            pool.memset(q_pad[:, :, :, :], 0.0).then_inc(zeroed, 1)
            squares(6, x_T, x_done, 12)
            squares(7, x_T, x_done, 16)
            squares(8, x_T, x_done, 20, (1, 2, 3), 10)


def constants():
    import numpy as np

    i = np.arange(P)
    q, k = np.arange(P)[:, None], np.arange(T)[None, :]
    tri = np.concatenate([i[:, None] <= i[None, :], np.ones((P, P))], 1)
    causal = np.where(P + q >= k, 0.0, -1e30)
    sel = (i[:, None, None] == np.arange(8)[None, :, None]) * np.ones((1, 1, P))
    dist = P + q - k
    slopes = 2.0 ** (-8.0 * np.arange(1, 5) / 4)
    alibi = np.where(dist[:, None, :] >= 0, -slopes[None, :, None] * dist[:, None, :], -1e30)
    rel = np.arange(T)[None, :] - i[:, None]
    gamma = 1.0 - 2.0 ** (-5.0 - np.arange(4))
    decay = np.where(rel[:, None, :] >= 0, gamma[None, :, None] ** np.maximum(rel, 0)[:, None, :], 0.0) * P ** -0.5
    parts = [np.eye(P), np.ones((P, P)), i[:, None] // 64 == i[None, :] // 64, tri, causal, sel, alibi, decay]
    return np.concatenate([np.asarray(x, np.float32).reshape(P, -1) for x in parts], 1)


def kernel(**inputs):
    import numpy as np
    import concourse.bacc as bacc
    from concourse.bass_utils import run_bass_kernel_spmd

    nc = bacc.Bacc("TRN2", target_bir_lowering=False, num_devices=1)
    arrays, args = {}, {}
    for name, value in {**inputs, "consts": constants()}.items():
        v = np.ascontiguousarray(value)
        arrays[f"in_{name}"] = v
        args[name] = nc.dram_tensor(f"in_{name}", v.shape, mybir.dt.from_np(v.dtype), kind="ExternalInput").ap()
    out = nc.dram_tensor("out_dram", (1, T, D), F32, kind="ExternalOutput").ap()
    build(nc, args, out)
    r = run_bass_kernel_spmd(nc, [arrays], core_ids=[0])
    return r.results[0]["out_dram"]
```
